# Optimizing a Trainium2 kernel written in Bass

```python
import math
import jax, jax.numpy as jnp
from jax import lax
import numpy as np

D_MODEL = 1024
BATCH = 1
SEQ = 256
DEPTH = 2

N_MIXERS = 2
N_Q_HEADS = 8
N_KV_HEADS = 2
HEAD_DIM = D_MODEL // N_Q_HEADS
Q_PER_KV = N_Q_HEADS // N_KV_HEADS
ROT_DIM = HEAD_DIM // 4
ROPE_THETA = 500000.0
WINDOW = 128
BLOCK = 128
D_RNN = 3 * D_MODEL // 2
N_RNN_BLOCKS = 16
RNN_BLOCK_W = D_RNN // N_RNN_BLOCKS
CONV_W = 4
CONV_LEFT = 2
LRU_C = 8.0
D_FF = 4 * D_MODEL
DN_ALPHA = (2.0 * DEPTH) ** 0.25
DN_BETA = (8.0 * DEPTH) ** -0.25
LN_EPS = 1e-5
ADA_INIT = 0.5

N_ATTN_LAYERS = (DEPTH + N_MIXERS - 1) // N_MIXERS
N_RNN_LAYERS = DEPTH // N_MIXERS


def layer_norm(x, g, b):
    xf = x.astype(jnp.float32)
    mu = jnp.mean(xf, axis=-1, keepdims=True)
    var = jnp.mean(jnp.square(xf - mu), axis=-1, keepdims=True)
    y = (xf - mu) * lax.rsqrt(var + LN_EPS)
    return (y * g.astype(jnp.float32) + b.astype(jnp.float32)).astype(x.dtype)

def ada_modulation(c, w, b):
    mod = jax.nn.silu(c) @ w + b
    shift, scale, gate = jnp.split(mod, 3, axis=-1)
    return shift[:, None, :], scale[:, None, :], gate[:, None, :]

def partial_rope(t, cos, sin):
    half = ROT_DIM // 2
    tr = t[..., :ROT_DIM].astype(jnp.float32)
    t1, t2 = tr[..., :half], tr[..., half:]
    cs, sn = cos[None, :, None, :], sin[None, :, None, :]
    rot = jnp.concatenate([t1 * cs - t2 * sn, t2 * cs + t1 * sn], axis=-1).astype(t.dtype)
    return jnp.concatenate([rot, t[..., ROT_DIM:]], axis=-1)

def windowed_gqa(h, w_in, w_out, sinks):
    B, S, _ = h.shape
    nblk = S // BLOCK
    qkv = h @ w_in
    q, k, v = jnp.split(qkv, [N_Q_HEADS * HEAD_DIM, (N_Q_HEADS + N_KV_HEADS) * HEAD_DIM], axis=-1)
    q = q.reshape(B, S, N_Q_HEADS, HEAD_DIM)
    k = k.reshape(B, S, N_KV_HEADS, HEAD_DIM)
    v = v.reshape(B, S, N_KV_HEADS, HEAD_DIM)
    pos = jnp.arange(S, dtype=jnp.float32)
    inv_freq = ROPE_THETA ** (-jnp.arange(0, ROT_DIM, 2, dtype=jnp.float32) / ROT_DIM)
    ang = pos[:, None] * inv_freq[None, :]
    cos, sin = jnp.cos(ang), jnp.sin(ang)
    q = partial_rope(q, cos, sin)
    k = partial_rope(k, cos, sin)
    qb = q.reshape(B, nblk, BLOCK, N_KV_HEADS, Q_PER_KV, HEAD_DIM)

    def band(t):
        tp = jnp.pad(t, ((0, 0), (BLOCK, BLOCK), (0, 0), (0, 0)))
        tb = tp.reshape(B, nblk + 2, BLOCK, N_KV_HEADS, HEAD_DIM)
        return jnp.concatenate([tb[:, :-2], tb[:, 1:-1], tb[:, 2:]], axis=2)

    kb, vb = band(k), band(v)
    scores = jnp.einsum("bnqhgd,bnjhd->bnhgqj", qb, kb,
                        preferred_element_type=jnp.float32) * (HEAD_DIM ** -0.5)
    blk = jnp.arange(nblk)[:, None, None] * BLOCK
    qpos = blk + jnp.arange(BLOCK)[None, :, None]
    kpos = blk - BLOCK + jnp.arange(3 * BLOCK)[None, None, :]
    valid = (jnp.abs(qpos - kpos) <= WINDOW) & (kpos >= 0) & (kpos < S)
    scores = jnp.where(valid[None, :, None, None], scores, -jnp.inf)
    sink = sinks.astype(jnp.float32).reshape(N_KV_HEADS, Q_PER_KV)[None, None, :, :, None, None]
    m = jnp.maximum(jnp.max(scores, axis=-1, keepdims=True), sink)
    p = jnp.exp(scores - m)
    denom = jnp.sum(p, axis=-1, keepdims=True) + jnp.exp(sink - m)
    probs = (p / denom).astype(v.dtype)
    o = jnp.einsum("bnhgqj,bnjhd->bnqhgd", probs, vb)
    o = o.reshape(B, S, N_Q_HEADS * HEAD_DIM)
    return o @ w_out

def centred_depthwise_conv(x, w, b):
    S = x.shape[1]
    xp = jnp.pad(x, ((0, 0), (CONV_LEFT, CONV_W - 1 - CONV_LEFT), (0, 0)))
    out = xp[:, 0:S] * w[0] + b
    for j in range(1, CONV_W):
        out = out + xp[:, j:j + S] * w[j]
    return out

def rg_lru(x, w_a, b_a, w_x, b_x, lam, reverse):
    B, S, _ = x.shape
    xb = x.reshape(B, S, N_RNN_BLOCKS, RNN_BLOCK_W)
    r = jax.nn.sigmoid((jnp.einsum("bsni,nij->bsnj", xb, w_a).reshape(B, S, D_RNN) + b_a).astype(jnp.float32))
    i = jax.nn.sigmoid((jnp.einsum("bsni,nij->bsnj", xb, w_x).reshape(B, S, D_RNN) + b_x).astype(jnp.float32))
    log_a = -LRU_C * r * jax.nn.softplus(-lam.astype(jnp.float32))
    a = jnp.exp(log_a)
    mult = jnp.sqrt(-jnp.expm1(2.0 * log_a))
    u = mult * (i * x.astype(jnp.float32))

    def combine(left, right):
        a_l, b_l = left
        a_r, b_r = right
        return a_l * a_r, a_r * b_l + b_r

    _, hs = lax.associative_scan(combine, (a, u), axis=1, reverse=reverse)
    return hs

def recurrent_block(h, w_in, conv_w, conv_b, w_a, b_a, w_x, b_x, lam, w_out):
    z = h @ w_in
    xr, gate = jnp.split(z, 2, axis=-1)
    xr = centred_depthwise_conv(xr, conv_w, conv_b)
    y = (rg_lru(xr, w_a[0], b_a[0], w_x[0], b_x[0], lam[0], reverse=False)
         + rg_lru(xr, w_a[1], b_a[1], w_x[1], b_x[1], lam[1], reverse=True))
    y = y.astype(h.dtype) * jax.nn.gelu(gate)
    return y @ w_out

def sq_relu_mlp(h, w1, w2):
    return jnp.square(jax.nn.relu(h @ w1)) @ w2

def first_inputs(seed: int = 0) -> dict:
    key = jax.random.key(seed)
    ks = jax.random.split(key, 24)
    nrm = lambda k, shape, s: jax.random.normal(k, shape, jnp.float32) * s
    u = jax.random.uniform(ks[17], (N_RNN_LAYERS, 2, D_RNN), jnp.float32, 0.9, 0.999)
    s_lam = u ** (1.0 / LRU_C)
    lam = jnp.log(s_lam) - jnp.log1p(-s_lam)
    return {
        "x": nrm(ks[0], (BATCH, SEQ, D_MODEL), 1.0),
        "c": nrm(ks[1], (BATCH, D_MODEL), 1.0),
        "ada_w": nrm(ks[2], (DEPTH, 2, D_MODEL, 3 * D_MODEL), ADA_INIT * D_MODEL ** -0.5),
        "ada_b": nrm(ks[3], (DEPTH, 2, 3 * D_MODEL), 0.01),
        "ln_g": 1.0 + nrm(ks[4], (DEPTH, 2, D_MODEL), 0.02),
        "ln_b": nrm(ks[5], (DEPTH, 2, D_MODEL), 0.02),
        "attn_w_in": nrm(ks[6], (N_ATTN_LAYERS, D_MODEL, (N_Q_HEADS + 2 * N_KV_HEADS) * HEAD_DIM), D_MODEL ** -0.5),
        "attn_w_out": nrm(ks[7], (N_ATTN_LAYERS, N_Q_HEADS * HEAD_DIM, D_MODEL), DN_BETA * (N_Q_HEADS * HEAD_DIM) ** -0.5),
        "attn_sinks": nrm(ks[8], (N_ATTN_LAYERS, N_Q_HEADS), 1.0),
        "rnn_w_in": nrm(ks[9], (N_RNN_LAYERS, D_MODEL, 2 * D_RNN), D_MODEL ** -0.5),
        "rnn_conv_w": nrm(ks[10], (N_RNN_LAYERS, CONV_W, D_RNN), CONV_W ** -0.5),
        "rnn_conv_b": nrm(ks[11], (N_RNN_LAYERS, D_RNN), 0.01),
        "rnn_w_a": nrm(ks[12], (N_RNN_LAYERS, 2, N_RNN_BLOCKS, RNN_BLOCK_W, RNN_BLOCK_W), RNN_BLOCK_W ** -0.5),
        "rnn_b_a": nrm(ks[13], (N_RNN_LAYERS, 2, D_RNN), 0.01),
        "rnn_w_x": nrm(ks[14], (N_RNN_LAYERS, 2, N_RNN_BLOCKS, RNN_BLOCK_W, RNN_BLOCK_W), RNN_BLOCK_W ** -0.5),
        "rnn_b_x": nrm(ks[15], (N_RNN_LAYERS, 2, D_RNN), 0.01),
        "rnn_lam": lam,
        "rnn_w_out": nrm(ks[16], (N_RNN_LAYERS, D_RNN, D_MODEL), DN_BETA * D_RNN ** -0.5),
        "mlp_w1": nrm(ks[18], (DEPTH, D_MODEL, D_FF), D_MODEL ** -0.5),
        "mlp_w2": nrm(ks[19], (DEPTH, D_FF, D_MODEL), DN_BETA * D_FF ** -0.5),
    }

def first_block(x, c, ada_w, ada_b, ln_g, ln_b, attn_w_in, attn_w_out, attn_sinks,
              rnn_w_in, rnn_conv_w, rnn_conv_b, rnn_w_a, rnn_b_a, rnn_w_x, rnn_b_x, rnn_lam,
              rnn_w_out, mlp_w1, mlp_w2):
    for i in range(DEPTH):
        j = i // N_MIXERS
        shift, scale, gate = ada_modulation(c, ada_w[i, 0], ada_b[i, 0])
        h = x * (1.0 + scale) + shift
        if i % N_MIXERS == 0:
            y = windowed_gqa(h, attn_w_in[j], attn_w_out[j], attn_sinks[j])
        else:
            y = recurrent_block(h, rnn_w_in[j], rnn_conv_w[j], rnn_conv_b[j], rnn_w_a[j], rnn_b_a[j],
                                rnn_w_x[j], rnn_b_x[j], rnn_lam[j], rnn_w_out[j])
        x = layer_norm(DN_ALPHA * x + (1.0 + gate) * y, ln_g[i, 0], ln_b[i, 0])
        shift, scale, gate = ada_modulation(c, ada_w[i, 1], ada_b[i, 1])
        y = sq_relu_mlp(x * (1.0 + scale) + shift, mlp_w1[i], mlp_w2[i])
        x = layer_norm(DN_ALPHA * x + (1.0 + gate) * y, ln_g[i, 1], ln_b[i, 1])
    return x


DEPTH_2 = 1

GRID_W = 64
CTX_LEN = 256

D_HY = D_MODEL // 4
D_HG = D_MODEL // 2
D_FN = D_MODEL // 4
D_MIX = D_HY + D_HG + D_FN

HY_ORDER = 2
HY_SHORT_CONV = 3
HY_BANDS = 16
HY_EMB_DIM = 1 + 2 * HY_BANDS
HY_FILTER_HIDDEN = 64
HY_DECAY_TARGET = 1e-2
HY_FAST_DECAY_PCT = 0.3
HY_SLOW_DECAY_PCT = 1.5
D_HY_PROJ = (HY_ORDER + 1) * D_HY

HG_HEAD_DIM = 128
HG_HEADS = D_HG // HG_HEAD_DIM
HG_CHUNK = 64
HG_PROJ = 5 * D_HG

FN_GROUPS = 4
FN_GROUP_DIM = D_FN // FN_GROUPS

D_PROJ = D_HY_PROJ + HG_PROJ + D_FN

N_EXPERTS = 16
N_GROUPS = 4
EXPERTS_PER_GROUP = N_EXPERTS // N_GROUPS
TOP_K = 2
D_EXPERT = 512

N_MOD = 6
RMS_EPS = 1e-6
POS_BASE = 10000.0


def rmsnorm(x, g):
    xf = x.astype(jnp.float32)
    y = xf * lax.rsqrt(jnp.mean(xf * xf, axis=-1, keepdims=True) + RMS_EPS)
    return (y * g.astype(jnp.float32)).astype(x.dtype)

def modulate(h, shift, scale):
    return h * (1 + scale) + shift

def ada_modulation_2(cond, w, b):
    return jnp.split(jax.nn.silu(cond) @ w + b, N_MOD, axis=-1)

def grid_sincos(n_tok):
    rows = n_tok // GRID_W
    row = jnp.repeat(jnp.arange(rows, dtype=jnp.float32), GRID_W)
    col = jnp.tile(jnp.arange(GRID_W, dtype=jnp.float32), rows)
    quarter = D_MODEL // 4
    omega = 1.0 / (POS_BASE ** (jnp.arange(quarter, dtype=jnp.float32) / quarter))
    ar = row[:, None] * omega
    ac = col[:, None] * omega
    return jnp.concatenate([jnp.sin(ar), jnp.cos(ar), jnp.sin(ac), jnp.cos(ac)], axis=-1)

def short_conv3(u, w, b):
    up = jnp.pad(u, ((0, 0), (1, 1), (0, 0)))
    return up[:, :-2] * w[0] + up[:, 1:-1] * w[1] + up[:, 2:] * w[2] + b

def hyena_deltas():
    max_decay = math.log(HY_DECAY_TARGET) / HY_FAST_DECAY_PCT
    min_decay = math.log(HY_DECAY_TARGET) / HY_SLOW_DECAY_PCT
    return jnp.linspace(min_decay, max_decay, D_HY, dtype=jnp.float32)

def hyena_filters(L, w1, b1, w2, b2, w3, freq):
    f32 = jnp.float32
    t = jnp.linspace(0.0, 1.0, L, dtype=f32)[:, None]
    w = 2.0 * math.pi * jnp.arange(L, dtype=f32)[:, None] / L
    bands = jnp.linspace(1e-4, HY_BANDS - 1, HY_BANDS, dtype=f32)[None, :]
    z = jnp.concatenate([t, jnp.cos(bands * w), -jnp.sin(bands * w)], axis=-1)
    fr = freq.astype(f32)
    h = jnp.sin(fr * (z @ w1.astype(f32) + b1.astype(f32)))
    h = jnp.sin(fr * (h @ w2.astype(f32) + b2.astype(f32)))
    h = (h @ w3.astype(f32)).reshape(L, 2 * HY_ORDER, D_HY)
    decay = jnp.exp(-t[:, :, None] * jnp.abs(hyena_deltas()))
    return h * decay

def bidir_fftconv(u, h_fwd, h_bwd, skip):
    L, C = h_fwd.shape
    k = jnp.concatenate([h_fwd, jnp.zeros((1, C), jnp.float32), h_bwd[1:][::-1]], axis=0)
    uf = jnp.fft.rfft(u.astype(jnp.float32), n=2 * L, axis=1)
    kf = jnp.fft.rfft(k, n=2 * L, axis=0)
    y = jnp.fft.irfft(uf * kf[None], n=2 * L, axis=1)[:, :L]
    return (y + u.astype(jnp.float32) * skip.astype(jnp.float32)).astype(u.dtype)

def hyena_mixer(z, conv_w, conv_b, w1, b1, w2, b2, w3, freq, bias, norm_g):
    L = z.shape[1]
    u = short_conv3(z, conv_w, conv_b)
    v, x1, x2 = jnp.split(u, HY_ORDER + 1, axis=-1)
    h = hyena_filters(L, w1, b1, w2, b2, w3, freq)
    y = x1 * bidir_fftconv(v, h[:, 0], h[:, 1], bias[0])
    y = x2 * bidir_fftconv(y, h[:, 2], h[:, 3], bias[1])
    return rmsnorm(y, norm_g)

def fourier_mixer(z, w, b, norm_g):
    B, L, _ = z.shape
    zg = z.astype(jnp.float32).reshape(B, L, FN_GROUPS, FN_GROUP_DIM)
    y = jnp.fft.fftn(zg, axes=(1, 3), norm="ortho").real
    y = jnp.einsum("blgc,gcd->blgd", y, w.astype(jnp.float32)).reshape(B, L, D_FN) + b.astype(jnp.float32)
    return rmsnorm(y.astype(z.dtype), norm_g)

def hgrn_lower_bounds(raw):
    cs = jnp.cumsum(jax.nn.softmax(raw.astype(jnp.float32), axis=0), axis=0)
    return cs - cs[0:1]

def hgrn2_inputs(z, lb):
    B, L, _ = z.shape
    q, f_fwd, f_bwd, i, g = jnp.split(z.astype(jnp.float32), 5, axis=-1)
    heads = lambda t: t.reshape(B, L, HG_HEADS, HG_HEAD_DIM)
    q = heads(jax.nn.silu(q)) * (HG_HEAD_DIM ** -0.5)
    dirs = []
    for d, f_raw in enumerate((f_fwd, f_bwd)):
        lbd = lb[d]
        forget = lbd + (1.0 - lbd) * jax.nn.sigmoid(f_raw)
        dirs.append((heads(1.0 - forget), heads(jnp.log(forget))))
    return q, heads(i), g, dirs

def to_chunks(t):
    B, L, H, d = t.shape
    return t.reshape(B, L // HG_CHUNK, HG_CHUNK, H, d).transpose(1, 0, 3, 2, 4)

def from_chunks(t):
    n, B, H, C, d = t.shape
    return t.transpose(1, 0, 3, 2, 4).reshape(B, n * C, H, d)

def gla_chunk_scan(q, k, v, logf, s0):
    causal = jnp.tril(jnp.ones((HG_CHUNK, HG_CHUNK), dtype=bool))

    def step(s, inp):
        qc, kc, vc, gc = inp
        b = jnp.cumsum(gc, axis=2)
        o_inter = jnp.einsum("bhtd,bhdv->bhtv", qc * jnp.exp(b), s)
        diff = b[:, :, :, None, :] - b[:, :, None, :, :]
        decay = jnp.exp(jnp.where(causal[:, :, None], diff, -jnp.inf))
        scores = jnp.einsum("bhtd,bhsd,bhtsd->bhts", qc, kc, decay)
        o_intra = jnp.einsum("bhts,bhsv->bhtv", scores, vc)
        b_end = b[:, :, -1, :]
        s_new = jnp.exp(b_end)[..., None] * s + jnp.einsum(
            "bhsd,bhsv->bhdv", kc * jnp.exp(b_end[:, :, None, :] - b), vc)
        return s_new, o_inter + o_intra

    s_fin, o = lax.scan(step, s0, (to_chunks(q), to_chunks(k), to_chunks(v), to_chunks(logf)))
    return s_fin, from_chunks(o)

def hgrn2_bidir(q, v, dirs, s0_fwd, s0_bwd):
    (k_f, g_f), (k_b, g_b) = dirs
    s_f, o_f = gla_chunk_scan(q, k_f, v, g_f, s0_fwd)
    flip = lambda t: t[:, ::-1]
    s_b, o_b = gla_chunk_scan(flip(q), flip(k_b), flip(v), flip(g_b), s0_bwd)
    return s_f, s_b, o_f + flip(o_b)

def hgrn2_readout(o, g, norm_g):
    B, L, H, d = o.shape
    on = o * lax.rsqrt(jnp.mean(o * o, axis=-1, keepdims=True) + RMS_EPS)
    return on.reshape(B, L, D_HG) * norm_g.astype(jnp.float32) * jax.nn.silu(g)

def mixer_output(z, o_hg, g_hg, w_out, conv_w, conv_b, w1, b1, w2, b2, w3, freq,
                 hy_bias, hy_norm_g, hg_norm_g, fn_w, fn_b, fn_norm_g):
    y_hy = hyena_mixer(z[..., :D_HY_PROJ], conv_w, conv_b, w1, b1, w2, b2, w3, freq, hy_bias, hy_norm_g)
    y_hg = hgrn2_readout(o_hg, g_hg, hg_norm_g).astype(z.dtype)
    y_fn = fourier_mixer(z[..., D_HY_PROJ + HG_PROJ:], fn_w, fn_b, fn_norm_g)
    return jnp.concatenate([y_hy, y_hg, y_fn], axis=-1) @ w_out

def moe_ffn(h, router_w, router_b, w_gate, w_up, w_down):
    N = h.shape[0]
    probs = jax.nn.softmax(h.astype(jnp.float32) @ router_w.astype(jnp.float32), axis=-1)
    sel = probs + router_b.astype(jnp.float32)
    group_score = lax.top_k(sel.reshape(N, N_GROUPS, EXPERTS_PER_GROUP), TOP_K)[0].sum(-1)
    best_group = jnp.argmax(group_score, axis=-1)
    in_group = (jnp.arange(N_EXPERTS) // EXPERTS_PER_GROUP)[None, :] == best_group[:, None]
    _, idx = lax.top_k(jnp.where(in_group, sel, -jnp.inf), TOP_K)
    gp = jnp.take_along_axis(probs, idx, axis=-1)
    gp = gp / jnp.sum(gp, axis=-1, keepdims=True)
    combine = jnp.sum(jax.nn.one_hot(idx, N_EXPERTS, dtype=jnp.float32) * gp[..., None], axis=1)
    out = jnp.zeros(h.shape, jnp.float32)
    for e in range(N_EXPERTS):
        he = (jax.nn.silu(h @ w_gate[e]) * (h @ w_up[e])) @ w_down[e]
        out = out + combine[:, e:e + 1] * he.astype(jnp.float32)
    return out.astype(h.dtype)

def second_inputs(seed: int = 0) -> dict:
    key = jax.random.key(seed)
    ks = jax.random.split(key, 32)
    f32 = jnp.float32
    nrm = lambda k, shape, s: s * jax.random.normal(k, shape, f32)
    D = D_MODEL
    return {
        "x": nrm(ks[0], (BATCH, SEQ, D), 1.0),
        "c": nrm(ks[1], (BATCH, D), 1.0),
        "ctx": nrm(ks[2], (BATCH, CTX_LEN, D), 1.0),
        "c_ctx": nrm(ks[3], (D,), 1.0),
        "ada_w": nrm(ks[4], (DEPTH_2, D, N_MOD * D), 0.5 * D ** -0.5),
        "ada_b": nrm(ks[5], (DEPTH_2, N_MOD * D), 0.02),
        "norm1_g": 1.0 + nrm(ks[6], (DEPTH_2, D), 0.1),
        "norm2_g": 1.0 + nrm(ks[7], (DEPTH_2, D), 0.1),
        "w_in": nrm(ks[8], (DEPTH_2, D, D_PROJ), D ** -0.5),
        "w_out": nrm(ks[9], (DEPTH_2, D_MIX, D), D_MIX ** -0.5),
        "hy_conv_w": nrm(ks[10], (DEPTH_2, HY_SHORT_CONV, D_HY_PROJ), 0.5),
        "hy_conv_b": nrm(ks[11], (DEPTH_2, D_HY_PROJ), 0.02),
        "hy_filt_w1": nrm(ks[12], (DEPTH_2, HY_EMB_DIM, HY_FILTER_HIDDEN), HY_EMB_DIM ** -0.5),
        "hy_filt_b1": nrm(ks[13], (DEPTH_2, HY_FILTER_HIDDEN), 0.02),
        "hy_filt_w2": nrm(ks[14], (DEPTH_2, HY_FILTER_HIDDEN, HY_FILTER_HIDDEN), HY_FILTER_HIDDEN ** -0.5),
        "hy_filt_b2": nrm(ks[15], (DEPTH_2, HY_FILTER_HIDDEN), 0.02),
        "hy_filt_w3": nrm(ks[16], (DEPTH_2, HY_FILTER_HIDDEN, 2 * HY_ORDER * D_HY), HY_FILTER_HIDDEN ** -0.5),
        "hy_filt_freq": 1.0 + nrm(ks[17], (DEPTH_2, HY_FILTER_HIDDEN), 0.1),
        "hy_bias": nrm(ks[18], (DEPTH_2, HY_ORDER, D_HY), 0.5),
        "hy_norm_g": 1.0 + nrm(ks[19], (DEPTH_2, D_HY), 0.1),
        "hg_lower_bounds": nrm(ks[20], (DEPTH_2, 2, D_HG), 1.0),
        "hg_norm_g": 1.0 + nrm(ks[21], (DEPTH_2, D_HG), 0.1),
        "fn_w": nrm(ks[22], (DEPTH_2, FN_GROUPS, FN_GROUP_DIM, FN_GROUP_DIM), FN_GROUP_DIM ** -0.5),
        "fn_b": nrm(ks[23], (DEPTH_2, D_FN), 0.02),
        "fn_norm_g": 1.0 + nrm(ks[24], (DEPTH_2, D_FN), 0.1),
        "router_w": nrm(ks[25], (D, N_EXPERTS), D ** -0.5),
        "router_b": nrm(ks[26], (N_EXPERTS,), 0.01),
        "moe_w_gate": nrm(ks[27], (DEPTH_2, N_EXPERTS, D, D_EXPERT), D ** -0.5),
        "moe_w_up": nrm(ks[28], (DEPTH_2, N_EXPERTS, D, D_EXPERT), D ** -0.5),
        "moe_w_down": nrm(ks[29], (DEPTH_2, N_EXPERTS, D_EXPERT, D), D_EXPERT ** -0.5),
        "final_norm_g": 1.0 + nrm(ks[30], (D,), 0.1),
    }

def second_block(x, c, ctx, c_ctx, ada_w, ada_b, norm1_g, norm2_g, w_in, w_out, hy_conv_w, hy_conv_b,
              hy_filt_w1, hy_filt_b1, hy_filt_w2, hy_filt_b2, hy_filt_w3, hy_filt_freq, hy_bias, hy_norm_g,
              hg_lower_bounds, hg_norm_g, fn_w, fn_b, fn_norm_g, router_w, router_b,
              moe_w_gate, moe_w_up, moe_w_down, final_norm_g):
    B, L, D = x.shape
    n_ctx = ctx.shape[1]
    lower_bounds = hgrn_lower_bounds(hg_lower_bounds)
    x = x + grid_sincos(L).astype(x.dtype)[None]
    cond_x = c[:, None, :]
    cond_c = c_ctx[None, None, :]
    s_zero = jnp.zeros((B, HG_HEADS, HG_HEAD_DIM, HG_HEAD_DIM), jnp.float32)
    hg_lo, hg_hi = D_HY_PROJ, D_HY_PROJ + HG_PROJ
    for layer in range(DEPTH_2):
        last = layer == DEPTH_2 - 1
        mod_x = ada_modulation_2(cond_x, ada_w[layer], ada_b[layer])
        mod_c = ada_modulation_2(cond_c, ada_w[layer], ada_b[layer])
        mix_params = (w_out[layer], hy_conv_w[layer], hy_conv_b[layer], hy_filt_w1[layer], hy_filt_b1[layer],
                      hy_filt_w2[layer], hy_filt_b2[layer], hy_filt_w3[layer], hy_filt_freq[layer],
                      hy_bias[layer], hy_norm_g[layer], hg_norm_g[layer], fn_w[layer], fn_b[layer], fn_norm_g[layer])
        hx = modulate(rmsnorm(x, norm1_g[layer]), mod_x[0], mod_x[1])
        hc = modulate(rmsnorm(ctx, norm1_g[layer]), mod_c[0], mod_c[1])
        zx = hx @ w_in[layer]
        zc = hc @ w_in[layer]
        q_c, v_c, g_c, dirs_c = hgrn2_inputs(zc[..., hg_lo:hg_hi], lower_bounds[layer])
        s_f, s_b, o_c = hgrn2_bidir(q_c, v_c, dirs_c, s_zero, s_zero)
        q_x, v_x, g_x, dirs_x = hgrn2_inputs(zx[..., hg_lo:hg_hi], lower_bounds[layer])
        _, _, o_x = hgrn2_bidir(q_x, v_x, dirs_x, s_f, s_b)
        x = x + mod_x[2] * mixer_output(zx, o_x, g_x, *mix_params)
        hx2 = modulate(rmsnorm(x, norm2_g[layer]), mod_x[3], mod_x[4])
        if last:
            ff_x = moe_ffn(hx2.reshape(B * L, D), router_w, router_b,
                           moe_w_gate[layer], moe_w_up[layer], moe_w_down[layer])
        else:
            ctx = ctx + mod_c[2] * mixer_output(zc, o_c, g_c, *mix_params)
            hc2 = modulate(rmsnorm(ctx, norm2_g[layer]), mod_c[3], mod_c[4])
            ff = moe_ffn(jnp.concatenate([hc2.reshape(B * n_ctx, D), hx2.reshape(B * L, D)], axis=0),
                         router_w, router_b, moe_w_gate[layer], moe_w_up[layer], moe_w_down[layer])
            ctx = ctx + mod_c[5] * ff[:B * n_ctx].reshape(B, n_ctx, D)
            ff_x = ff[B * n_ctx:]
        x = x + mod_x[5] * ff_x.reshape(B, L, D)
    return rmsnorm(x, final_norm_g)


def setup_inputs(seed=0):
    out = dict(first_inputs(seed))
    for name, value in second_inputs(seed + 1).items():
        if name != "x":
            out[name + "_2"] = value
    return out


def reference(
    x, c, ada_w, ada_b, ln_g, ln_b, attn_w_in, attn_w_out, attn_sinks, rnn_w_in, rnn_conv_w,
    rnn_conv_b, rnn_w_a, rnn_b_a, rnn_w_x, rnn_b_x, rnn_lam, rnn_w_out, mlp_w1, mlp_w2, c_2,
    ctx_2, c_ctx_2, ada_w_2, ada_b_2, norm1_g_2, norm2_g_2, w_in_2, w_out_2, hy_conv_w_2,
    hy_conv_b_2, hy_filt_w1_2, hy_filt_b1_2, hy_filt_w2_2, hy_filt_b2_2, hy_filt_w3_2,
    hy_filt_freq_2, hy_bias_2, hy_norm_g_2, hg_lower_bounds_2, hg_norm_g_2, fn_w_2, fn_b_2,
    fn_norm_g_2, router_w_2, router_b_2, moe_w_gate_2, moe_w_up_2, moe_w_down_2, final_norm_g_2,
):
    x = first_block(
        x, c, ada_w, ada_b, ln_g, ln_b, attn_w_in, attn_w_out, attn_sinks, rnn_w_in, rnn_conv_w,
        rnn_conv_b, rnn_w_a, rnn_b_a, rnn_w_x, rnn_b_x, rnn_lam, rnn_w_out, mlp_w1, mlp_w2,
    )
    return second_block(
        x, c_2, ctx_2, c_ctx_2, ada_w_2, ada_b_2, norm1_g_2, norm2_g_2, w_in_2, w_out_2,
        hy_conv_w_2, hy_conv_b_2, hy_filt_w1_2, hy_filt_b1_2, hy_filt_w2_2, hy_filt_b2_2,
        hy_filt_w3_2, hy_filt_freq_2, hy_bias_2, hy_norm_g_2, hg_lower_bounds_2, hg_norm_g_2,
        fn_w_2, fn_b_2, fn_norm_g_2, router_w_2, router_b_2, moe_w_gate_2, moe_w_up_2,
        moe_w_down_2, final_norm_g_2,
    )


_drawn_inputs = setup_inputs


def setup_inputs(seed=0):
    import zlib

    import numpy as np

    out = dict(_drawn_inputs(seed))
    spreads = {}
    factors = {'attn_sinks': 8.0,
     'rnn_conv_b': 3.234,
     'rnn_b_a': 31.35,
     'rnn_b_x': 27.615,
     'ctx_2': 25.58,
     'c_ctx_2': 8.0,
     'hy_conv_b_2': 4.297,
     'hy_filt_b1_2': 2.976,
     'hy_filt_b2_2': 2.761,
     'hy_bias_2': 2.977,
     'hg_norm_g_2': 2.816,
     'fn_b_2': 8.0,
     'fn_norm_g_2': 2.697,
     'hy_filt_freq_2': 2.799,
     'hy_norm_g_2': 4.267}
    for name, (base, spread) in spreads.items():
        noise = np.random.default_rng([zlib.crc32(name.encode()), seed]).standard_normal(out[name].shape)
        drawn = base * np.exp(spread * noise) if base else spread * noise
        out[name] = __import__('jax').numpy.asarray(drawn.astype(out[name].dtype))
    for name, factor in factors.items():
        out[name] = (out[name] * factor).astype(out[name].dtype)
    return out
```

```python
import math

import numpy as np

import concourse.bass as bass
from concourse import mybir

F32 = mybir.dt.float32
U32 = mybir.dt.uint32
ALU = mybir.AluOpType
ACT = mybir.ActivationFunctionType
AX = mybir.AxisListType.X

D, S, P = 1024, 256, 128
KT = D // P
NH, NKV, WIN = 8, 2, 128
NB, BW = 16, 96
FF = 4096
HGH = 4
NE, DE = 16, 512
DEPTH = 2
ALPHA = (2.0 * DEPTH) ** 0.25
LN_EPS, RMS_EPS = 1e-5, 1e-6
CH = 2048
RING = 6

ADA = 12
N_CHUNKS = 284


def _cols(spec):
    at, out = 0, {}
    for name, n in spec:
        out[name] = (at, at + n)
        at += n
    return out, at


PCOL, PN = _cols([("ada_b", 96), ("ada_b2", 48), ("ln_g", 32), ("ln_b", 32), ("n1g", 8), ("n2g", 8),
                  ("fing", 8), ("hycw", 18), ("hycb", 6), ("hybias", 4), ("hyg", 2), ("lb", 8),
                  ("hgg", 4), ("fnb", 2), ("fng", 2), ("sinks", 8), ("rb", 16), ("rw", 128),
                  ("fnw", 256), ("eps5", 1), ("eps6", 1)])
RCOL, RN = _cols([("cw", 64), ("cb", 16), ("ba", 32), ("bx", 32), ("lam", 32)])
FCOL, FN = _cols([("w1", 64), ("w2", 64), ("w3", 1024), ("b1", 1), ("b2", 1), ("fr", 1)])
TCOL, TN = _cols([("ident", 128), ("ropec", 256), ("ropes", 256), ("roper", 32), ("amask", 512),
                  ("zf", 256), ("dc", 512), ("ds", 512), ("ic", 512), ("is", 512), ("flc", 512),
                  ("fls", 512), ("fcc", 128), ("fcs", 128), ("decf", 512), ("decb", 512),
                  ("lmask", 1024), ("iota", 16)])


class Tok:

    def __init__(self, sem, n, k, loop):
        self.sem, self.n, self.k, self.loop = sem, n, k, loop

    def before(self):
        return Tok(self.sem, self.n - self.k, self.k, self.loop)


class Loop:
    def __init__(self, reg, turns, per_turn):
        self.reg, self.turns, self.per_turn = reg, turns, per_turn


class Count:

    def __init__(self, nc):
        self.nc = nc
        self.loop = None
        self.eng = {}
        for name, e in (("pe", nc.tensor), ("dve", nc.vector), ("act", nc.scalar), ("pool", nc.gpsimd)):
            self.eng[name] = [e, nc.alloc_semaphore("done_" + name), 0, None]
        self.arrived = [nc.alloc_semaphore(f"arrived{j}") for j in range(RING)]
        self.freed = [nc.alloc_semaphore(f"freed{j}") for j in range(RING)]

    def wait(self, name, *toks):
        e = self.eng[name][0]
        for t in toks:
            if t is None:
                continue
            if t.loop is not None and t.loop is self.loop and t.k:
                e.wait_ge(t.sem, self.loop.reg * t.k + t.n)
            elif t.loop is not None and t.loop is not self.loop:
                e.wait_ge(t.sem, t.n + (t.loop.turns - 1) * t.k)
            else:
                e.wait_ge(t.sem, t.n)

    def done(self, name, ins, frees=None):
        rec = self.eng[name]
        if frees is not None:
            ins.then_inc(self.freed[frees % RING], 1)
            rec[3] = Tok(self.freed[frees % RING], frees // RING + 1, 1 if self.loop else 0, self.loop)
        else:
            ins.then_inc(rec[1], 1)
            rec[2] += 1
            rec[3] = Tok(rec[1], rec[2], self.loop.per_turn[name] if self.loop else 0, self.loop)
        return rec[3]

    def last(self, name):
        return self.eng[name][3]

    def wait_chunk(self, name, c):
        n = 16 * (c // RING + 1)
        self.wait(name, Tok(self.arrived[c % RING], n, 16 if self.loop else 0, self.loop))

    def run_loop(self, turns, per_turn, body):
        base = {k: v[2] for k, v in self.eng.items()}
        engines = [mybir.EngineType.PE, mybir.EngineType.DVE, mybir.EngineType.Activation, mybir.EngineType.Pool]
        with self.nc.Fori(0, turns, engines=engines) as i:
            self.loop = Loop(i, turns, per_turn)
            for k, v in self.eng.items():
                if v[2] and per_turn[k]:
                    v[3] = Tok(v[1], v[2], per_turn[k], self.loop)
            body(i)
            for k, v in self.eng.items():
                assert v[2] - base[k] == per_turn[k], (k, v[2] - base[k], per_turn[k])
                v[2] = base[k] + turns * per_turn[k]
            self.loop = None


def build(nc, stream, xT, ctxT, posT, cvec, par, rpar, fpar, tab, sel, outT):
    q = Count(nc)
    wait, done, last, wait_chunk = q.wait, q.done, q.last, q.wait_chunk
    SB = nc.alloc_sbuf_tensor("sb", [P, 51400], F32)
    PS = nc.alloc_psum_tensor("ps", [P, 8, 512], F32)
    at = [0]

    def place(n):
        a = at[0]
        at[0] += n
        return a

    def view(a, n, p=P):
        return SB[0:p, a:a + n]

    ring = view(place(RING * CH), RING * CH)
    X = view(place(2048), 2048).rearrange("p (k t) -> p k t", k=KT)
    aH = place(4096)
    H2 = view(aH, 4096).rearrange("p (k t) -> p k t", k=KT)
    HX = view(aH, 2048).rearrange("p (k t) -> p k t", k=KT)
    aT1 = place(2048)
    aT2 = place(2048)
    T1 = view(aT1, 2048).rearrange("p (k t) -> p k t", k=KT)
    T2 = view(aT2, 2048).rearrange("p (k t) -> p k t", k=KT)
    aC = place(3072)
    CB = view(aC, 3072).rearrange("p (a n) -> p a n", a=3)
    MOD = view(place(160), 160)
    PAR = view(place(PN), PN)
    RPAR = view(place(RN), RN, BW)
    TAB = view(place(TN), TN)
    aM = place(384)
    MISC = view(aM, 384)
    ONES = view(place(P), P)
    RS = view(place(512), 512)
    KF = view(place(2048), 2048)
    aA = at[0]
    FPAR = view(51400 - FN, FN, 64)

    def par_(name, j=0, n=1):
        return PAR[:, PCOL[name][0] + j:PCOL[name][0] + j + n]

    def tab_(name, p=P):
        return TAB[0:p, TCOL[name][0]:TCOL[name][1]]



    def V(f, *a, w=(), frees=None, **k):
        wait("dve", last("dve"), *w)
        return done("dve", f(*a, **k), frees)

    def A(out, in_, func, w=(), **k):
        wait("act", last("act"), *w)
        return done("act", nc.scalar.activation(out, in_, func, **k))

    def G(f, *a, w=(), **k):
        wait("pool", last("pool"), *w)
        return done("pool", f(*a, **k))

    vv = nc.vector

    def mm(out, lhsT, rhs, start, stop):
        return nc.tensor.matmul(out, lhsT, rhs, start=start, stop=stop, skip_group_check=True)

    def chunk(c):
        return ring[:, (c % RING) * CH:(c % RING + 1) * CH]

    def all_wait():
        toks = {n: last(n) for n in q.eng}
        for n in q.eng:
            wait(n, *[t for m, t in toks.items() if m != n])

    sp = nc.sync
    turns = N_CHUNKS // RING

    def fetch(c, j):
        src = stream[c] if isinstance(c, int) else stream[bass.ds(c, 1)].rearrange("a p n -> (a p) n")
        sp.dma_start(ring[:, j * CH:(j + 1) * CH], src).then_inc(q.arrived[j], 16)

    for j in range(RING):
        fetch(j, j)
    with sp.Fori(1, turns) as i:
        for j in range(RING):
            sp.wait_ge(q.freed[j], i)
            fetch(i * RING + j, j)
    for j in range(N_CHUNKS - turns * RING):
        sp.wait_ge(q.freed[j], turns)
        fetch(turns * RING + j, j)

    s_c, s_in, s_ctx = nc.alloc_semaphore("s_c"), nc.alloc_semaphore("s_in"), nc.alloc_semaphore("s_ctx")
    nc.scalar.dma_start(CB[:, 0, :], cvec[0:1, :].broadcast_to([P, D])).then_inc(s_c, 16)
    nc.scalar.dma_start(PAR, par).then_inc(s_in, 16)
    nc.scalar.dma_start(TAB, tab).then_inc(s_in, 16)
    nc.scalar.dma_start(FPAR, fpar).then_inc(s_in, 16)
    nc.scalar.dma_start(X, xT).then_inc(s_in, 16)
    nc.scalar.dma_start(RPAR, rpar).then_inc(s_in, 16)
    nc.scalar.dma_start(CB[:, 1, :], cvec[1:2, :].broadcast_to([P, D])).then_inc(s_in, 16)
    nc.scalar.dma_start(CB[:, 2, :], cvec[2:3, :].broadcast_to([P, D])).then_inc(s_in, 16)
    IN = Tok(s_in, 112, 0, None)
    A(CB[:, 0, :], CB[:, 0, :], ACT.Silu, w=[Tok(s_c, 16, 0, None)])
    silu_c = last("act")
    G(nc.gpsimd.memset, ONES, 1.0)
    wait("pool", IN)
    wait("pe", IN, last("pool"))
    wait("dve", IN, silu_c)
    wait("act", IN)
    silu_c2 = A(CB[:, 1:3, :], CB[:, 1:3, :], ACT.Silu)

    JUNK = view(aT2, 1024)

    def ada_chunk(c, col, conds=((0, 0),), junk=None):
        wait_chunk("dve", c)
        junk = JUNK if junk is None else junk
        for j in range(2):
            for n, (v, off) in enumerate(conds):
                src = chunk(c)[:, j * D:(j + 1) * D]
                acc = MOD[:, col + off + j:col + off + j + 1] if q.loop is None else MISC[:, 2 * n + j:2 * n + j + 1]
                V(vv.tensor_tensor_reduce, junk, src, CB[:, v, :], 1.0, 0.0, ALU.mult, ALU.add, acc,
                  frees=c if j == 1 and n == len(conds) - 1 else None)
        if q.loop is not None:
            for n, (v, off) in enumerate(conds):
                V(vv.tensor_copy, MOD[:, bass.ds(q.loop.reg * 4 + (col + off), 2)], MISC[:, 2 * n:2 * n + 2])

    def ada_bias(a, n, name, j):
        V(vv.tensor_tensor, MOD[:, a:a + n], MOD[:, a:a + n], par_(name, j, n), ALU.add)

    c_now = 0
    def sin_of(dst, ps, bcol, frcol, tmp, w):
        TP = 2 * math.pi
        HI = float(np.float32(6.28125))
        V(vv.tensor_scalar, dst, ps, bcol, frcol, ALU.add, ALU.mult, w=w)
        V(vv.tensor_scalar, tmp, dst, 1.0 / TP, 12582912.0, ALU.mult, ALU.add)
        V(vv.tensor_scalar, tmp, tmp, 12582912.0, None, ALU.subtract)
        V(vv.scalar_tensor_tensor, dst, tmp, -HI, dst, ALU.mult, ALU.add)
        V(vv.scalar_tensor_tensor, dst, tmp, -(TP - HI), dst, ALU.mult, ALU.add)
        V(vv.tensor_scalar, dst, dst, math.pi, -math.pi, ALU.min, ALU.max)
        return A(dst, dst, ACT.Sin, w=[last("dve")])

    fp = lambda n: FPAR[:, FCOL[n][0]:FCOL[n][1]]
    h1, tmp1, h2 = view(aA, 256, 64), view(aA + 256, 256, 64), view(aA + 512, 256, 64)
    HS = view(aA + 1024, 1024).rearrange("p (o b c) -> p o b c", o=2, b=2)
    HD = view(aA + 2048, 1024).rearrange("p (o b c) -> p o b c", o=2, b=2)
    ht = view(aA + 3072, 512)
    t = done("pe", mm(PS[0:64, 0, 0:256], fp("w1")[0:33, :], tab_("zf", 33), True, True))
    t = sin_of(h1, PS[0:64, 0, 0:256], fp("b1"), fp("fr"), tmp1, [t])
    wait("pe", t)
    t = done("pe", mm(PS[0:64, 1, 0:256], fp("w2"), h1, True, True))
    t = sin_of(h2, PS[0:64, 1, 0:256], fp("b2"), fp("fr"), tmp1, [t])
    wait("pe", t)
    for o in range(2):
        for b in range(2):
            pe = done("pe", mm(PS[:, 2 * o + b, :], h2[:, b * P:(b + 1) * P], fp("w3")[:, o * 512:(o + 1) * 512], True, True))
            V(vv.tensor_tensor, ht[:, 0:256], PS[:, 2 * o + b, 0:256], tab_("decf")[:, b * 256:(b + 1) * 256], ALU.mult, w=[pe])
            V(vv.tensor_tensor, ht[:, 256:512], PS[:, 2 * o + b, 256:512], tab_("decb")[:, b * 256:(b + 1) * 256], ALU.mult)
            V(vv.tensor_tensor, HS[:, o, b, :], ht[:, 0:256], ht[:, 256:512], ALU.add)
            V(vv.tensor_tensor, HD[:, o, b, :], ht[:, 0:256], ht[:, 256:512], ALU.subtract)
    wait("pe", last("dve"))
    KFv = KF.rearrange("p (o r f c) -> p o r f c", o=2, r=2, f=2)
    for o in range(2):
        for r, (tb_, src) in enumerate((("dc", HS), ("ds", HD))):
            for f in range(2):
                for b in range(2):
                    ins = mm(PS[:, 4 + 2 * o + r, f * 256:(f + 1) * 256],
                             tab_(tb_)[:, b * 256 + f * P:b * 256 + (f + 1) * P], src[:, o, b, :], b == 0, b == 1)
            pe = done("pe", ins)
            A(KFv[:, o, r, :, :], PS[:, 4 + 2 * o + r, :].rearrange("p (f c) -> p f c", f=2), ACT.Copy, w=[pe])

    for j in range(ADA):
        ada_chunk(c_now, 2 * j)
        c_now += 1
    ada_bias(0, 24, "ada_b", 0)

    XC, SQ = T1, T2
    MEAN, VAR = PS[:, 0, 0:256], PS[:, 1, 0:256]
    RSTD = RS[:, 0:256]
    combo = MISC[:, 16:80]

    def modulate_x(m, dst):
        sc = combo[:, 0:8]
        V(vv.tensor_scalar, sc, MOD[:, 24 * m + 8:24 * m + 16], 1.0, None, ALU.add)
        toks = []
        for k in range(KT):
            toks.append(V(vv.tensor_scalar, dst[:, k, 0:S], X[:, k, :], sc[:, k:k + 1], MOD[:, 24 * m + k:24 * m + k + 1],
                          ALU.mult, ALU.add))
        V(vv.tensor_scalar, X[:, :, :], X[:, :, :], ALPHA, None, ALU.mult)
        return toks

    def add_branch(n, y, g, tok):
        return V(vv.scalar_tensor_tensor, X[:, n, :], y, g, X[:, n, :], ALU.mult, ALU.add, w=[tok])

    def column_sums(bank, src, toks, half=None):
        for k in range(KT):
            wait("pe", toks[k])
            ins = mm(bank, ONES, src[:, k, :], k == 0, k == KT - 1)
        return done("pe", ins)

    def root(dst, src, scale, eps, w):
        A(dst, src, ACT.Sqrt, w=w, scale=scale, bias=eps)
        return V(vv.reciprocal, dst, dst, w=[last("act")])

    def layer_norm(ln, toks, scale_col, shift_col, nxt_alpha, dst):
        lg, lb_ = par_("ln_g", 8 * ln, 8), par_("ln_b", 8 * ln, 8)
        pe = column_sums(MEAN, X, toks)
        mean = RS[:, 256:512]
        V(vv.tensor_scalar, mean, MEAN, 1.0 / D, None, ALU.mult, w=[pe])
        sq = []
        for h in range(2):
            v = V(vv.tensor_tensor, XC[:, 4 * h:4 * h + 4, :], X[:, 4 * h:4 * h + 4, :],
                  mean.unsqueeze(1).broadcast_to([P, 4, S]), ALU.subtract)
            sq += [A(SQ[:, 4 * h:4 * h + 4, :], XC[:, 4 * h:4 * h + 4, :], ACT.Square, w=[v])] * 4
        ga, ba = combo[:, 8:16], combo[:, 16:24]
        V(vv.tensor_scalar, ga, lg, nxt_alpha, None, ALU.mult)
        V(vv.tensor_scalar, ba, lb_, nxt_alpha, None, ALU.mult)
        gm, bm = combo[:, 24:32], combo[:, 32:40]
        if dst is not None:
            V(vv.tensor_scalar, combo[:, 40:48], scale_col, 1.0, None, ALU.add)
            V(vv.tensor_tensor, gm, lg, combo[:, 40:48], ALU.mult)
            V(vv.tensor_tensor, bm, lb_, combo[:, 40:48], ALU.mult)
            V(vv.tensor_tensor, bm, bm, shift_col, ALU.add)
        pe = column_sums(VAR, SQ, sq)
        v = root(RSTD, VAR, 1.0 / D, par_("eps5"), [pe])
        out, xs = [], []
        for h in range(2):
            V(vv.tensor_tensor, XC[:, 4 * h:4 * h + 4, :], XC[:, 4 * h:4 * h + 4, :],
              RSTD.unsqueeze(1).broadcast_to([P, 4, S]), ALU.mult)
            if dst is not None:
                for k in range(4 * h, 4 * h + 4):
                    out.append(V(vv.tensor_scalar, dst[:, k, 0:S], XC[:, k, :], gm[:, k:k + 1], bm[:, k:k + 1], ALU.mult, ALU.add))
        for k in range(KT):
            xs.append(V(vv.tensor_scalar, X[:, k, :], XC[:, k, :], ga[:, k:k + 1], ba[:, k:k + 1], ALU.mult, ALU.add))
        return out, xs

    htok = modulate_x(0, HX)
    all_wait()
    QK = view(aA, 2560).rearrange("p (n t) -> p n t", n=10)
    VT = view(aA + 2560, 512).rearrange("p (b n) -> p b n", b=2)
    SC = view(aA + 3072, 2048).rearrange("p (a h k) -> p a h k", a=2, h=4)
    PT = view(aA + 5120, 2048).rearrange("p (a h k q) -> p a h k q", a=2, h=4, k=2)
    OT = view(aA + 7168, 2048).rearrange("p (h t) -> p h t", h=NH)
    RT = view(aA + 9216, 512, 32)
    free = [None] * 8
    qk_t = [None] * 10
    for n2 in range(5):
        c = c_now + n2
        wait_chunk("pe", c)
        bank = n2 % 2
        wait("pe", free[bank])
        for j in range(2):
            for k in range(KT):
                wait("pe", htok[k]) if n2 == 0 and j == 0 else None
                ins = mm(PS[:, bank, j * 256:(j + 1) * 256], chunk(c)[:, (j * 8 + k) * P:(j * 8 + k + 1) * P],
                         HX[:, k, 0:S], k == 0, k == KT - 1)
        pe = done("pe", ins, frees=c)
        free[bank] = A(QK[:, 2 * n2:2 * n2 + 2, :], PS[:, bank, :].rearrange("p (n t) -> p n t", n=2), ACT.Copy, w=[pe])
        wait("pe", free[bank], free[2 + bank])
        pe = done("pe", mm(PS[0:32, 2 + bank, :], tab_("roper", 32), QK[0:32, 2 * n2:2 * n2 + 2, :], True, True))
        sin = tab_("ropes", 32).unsqueeze(1).broadcast_to([32, 2, S])
        cos = tab_("ropec", 32).unsqueeze(1).broadcast_to([32, 2, S])
        rt = RT.rearrange("p (n t) -> p n t", n=2)
        free[2 + bank] = V(vv.tensor_tensor, rt, PS[0:32, 2 + bank, :].rearrange("p (n t) -> p n t", n=2), sin, ALU.mult, w=[pe])
        V(vv.tensor_tensor, QK[0:32, 2 * n2:2 * n2 + 2, :], QK[0:32, 2 * n2:2 * n2 + 2, :], cos, ALU.mult)
        qk_t[2 * n2] = qk_t[2 * n2 + 1] = V(vv.tensor_tensor, QK[0:32, 2 * n2:2 * n2 + 2, :], QK[0:32, 2 * n2:2 * n2 + 2, :], rt, ALU.add)
    c = c_now + 5
    wait_chunk("pe", c)
    wait("pe", free[0])
    for b in range(2):
        for k in range(KT):
            ins = mm(PS[:, 0, b * 256:(b + 1) * 256], HX[:, k, b * P:(b + 1) * P], chunk(c)[:, k * 256:(k + 1) * 256], k == 0, k == KT - 1)
    pe = done("pe", ins, frees=c)
    v_t = free[0] = A(VT, PS[:, 0, :].rearrange("p (b n) -> p b n", b=2), ACT.Copy, w=[pe])
    c_now += 6
    ada_next = c_now
    c_now += 8
    SM = MISC[:, 128:256]
    ident = tab_("ident")
    sc_free, pt_free = [None, None], [None, None]
    ada_j = 0
    for n, (g, b) in enumerate(((0, 0), (0, 1), (1, 0), (1, 1))):
        a = n % 2
        sm = SM[:, 32 * n:32 * n + 32]
        wait("pe", free[4], free[5], *qk_t)
        for h in range(4):
            ins = mm(PS[:, 4 + h // 2, (h % 2) * 256:(h % 2 + 1) * 256], QK[:, 4 * g + h, b * P:(b + 1) * P], QK[:, 8 + g, :], True, True)
        pe = done("pe", ins)
        mask = tab_("amask")[:, b * 256:(b + 1) * 256].unsqueeze(1).broadcast_to([P, 4, S])
        free[4] = free[5] = V(vv.scalar_tensor_tensor, SC[:, a, :, :], PS[:, 4:6, :].rearrange("p b (h k) -> p (b h) k", h=2), P ** -0.5, mask,
                              ALU.mult, ALU.add, w=[pe, sc_free[a]])
        V(vv.tensor_reduce, sm[:, 0:4], SC[:, a, :, :], AX, ALU.max)
        V(vv.tensor_tensor, sm[:, 0:4], sm[:, 0:4], par_("sinks", 4 * g, 4), ALU.max)
        V(vv.tensor_tensor, sm[:, 4:8], par_("sinks", 4 * g, 4), sm[:, 0:4], ALU.subtract)
        v = V(vv.tensor_scalar, sm[:, 8:12], sm[:, 0:4], -1.0, None, ALU.mult)
        A(sm[:, 12:16], sm[:, 4:8], ACT.Exp, w=[v])
        for h in range(4):
            e = A(SC[:, a, h, :], SC[:, a, h, :], ACT.Exp, bias=sm[:, 8 + h:9 + h], accum_out=sm[:, 16 + h:17 + h])
        for _ in range(2):
            ada_chunk(ada_next + ada_j, 24 + 2 * ada_j)
            ada_j += 1
        V(vv.tensor_tensor, sm[:, 16:20], sm[:, 16:20], sm[:, 12:16], ALU.add, w=[e])
        V(vv.reciprocal, sm[:, 20:24], sm[:, 16:20])
        p_t = V(vv.tensor_tensor, SC[:, a, :, :], SC[:, a, :, :], sm[:, 20:24].unsqueeze(2).broadcast_to([P, 4, S]), ALU.mult)
        wait("pe", p_t, free[6], free[7])
        for h in range(4):
            for kb in range(2):
                ins = nc.tensor.transpose(PS[:, 6 + h // 2, (h % 2) * 256 + kb * P:(h % 2) * 256 + (kb + 1) * P], SC[:, a, h, kb * P:(kb + 1) * P], ident)
        pe = done("pe", ins)
        sc_free[a] = pe
        free[6] = free[7] = A(PT[:, a, :, :, :], PS[:, 6:8, :].rearrange("p b (h k q) -> p (b h) k q", h=2, k=2), ACT.Copy, w=[pe, pt_free[a]])
        wait("pe", free[7], v_t, free[n])
        for h in range(4):
            for kb in range(2):
                ins = mm(PS[:, n, h * P:(h + 1) * P], VT[:, kb, g * P:(g + 1) * P], PT[:, a, h, kb, :], kb == 0, kb == 1)
        pe = done("pe", ins)
        pt_free[a] = pe
        o_t = free[n] = A(OT[:, 4 * g:4 * g + 4, b * P:(b + 1) * P], PS[:, n, :].rearrange("p (h q) -> p h q", h=4), ACT.Copy, w=[pe])

    def project(cs, src, src_tok, gcols, kdim=8, src_w=None):
        toks = []
        for n2, c in enumerate(cs):
            wait_chunk("pe", c)
            bank = 4 + n2
            wait("pe", free[bank], src_tok)
            for j in range(2):
                for k in range(KT):
                    ins = mm(PS[:, bank, j * 256:(j + 1) * 256], chunk(c)[:, (j * 8 + k) * P:(j * 8 + k + 1) * P], src[:, k, 0:S], k == 0, k == KT - 1)
            pe = done("pe", ins, frees=c)
            for j in range(2):
                toks.append(add_branch(2 * n2 + j, PS[:, bank, j * 256:(j + 1) * 256], gcols[:, 2 * n2 + j:2 * n2 + j + 1], pe))
            free[bank] = toks[-1]
        return toks

    ada_bias(24, 16, "ada_b", 24)
    G1 = MISC[:, 96:104]
    V(vv.tensor_scalar, G1, MOD[:, 16:24], 1.0, None, ALU.add)
    xt = project(range(c_now, c_now + 4), OT, o_t, G1)
    c_now += 4
    out, xs = layer_norm(0, xt, MOD[:, 32:40], MOD[:, 24:32], ALPHA, HX)
    for j in range(4):
        ada_chunk(c_now, 40 + 2 * j, junk=view(aA, 1024))
        c_now += 1
    ada_bias(40, 8, "ada_b", 40)

    def clear_sums():
        V(vv.memset, RS[0:1, :], 0.0)
        wait("pe", last("dve"), last("act"))
        for b in range(4):
            ins = mm(PS[:, 4 + b, :], RS[0:1, 0:P], RS[0:1, :], True, False)
        return done("pe", ins)

    def mlp(c0, htok, turns, first, ada_col, conds, last_turns):
        H1 = view(aA + 1024, 1024).rearrange("p (a h t) -> p a h t", a=2, h=2)
        R1 = view(aA + 3072, 1024).rearrange("p (a n) -> p a n", a=2)
        n_ada = 4 * len(conds) + 2 * len(conds)
        per = {"pe": 0, "dve": 2 + 2 * (3 * len(conds) - 1), "act": 2, "pool": 0}
        if first:
            clear_sums()

        def body(i):
            w1c, w2c, adac = (c0, c0 + 2), (c0 + 3, c0 + 5), (c0 + 1, c0 + 4)
            sq_t = [None, None]
            base_act = q.eng["act"][2]
            base_dve = q.eng["dve"][2]
            K = q.loop.per_turn
            for a in range(2):
                wait_chunk("pe", w1c[a])
                relu_before = Tok(q.eng["act"][1], base_act + a + 1 - K["act"], K["act"], q.loop)
                wait("pe", relu_before)
                for j in range(2):
                    for k in range(KT):
                        ins = mm(PS[:, a, j * 256:(j + 1) * 256], chunk(w1c[a])[:, (j * 8 + k) * P:(j * 8 + k + 1) * P], HX[:, k, 0:S], k == 0, k == KT - 1)
                pe = done("pe", ins, frees=w1c[a])
                sq_before = Tok(q.eng["dve"][1], base_dve + (1 if a == 0 else 1 + per_ada + 1) - K["dve"], K["dve"], q.loop)
                r = A(R1[:, a, :], PS[:, a, :], ACT.Relu, w=[pe, sq_before])
                w2_before = Tok(q.freed[w2c[a] % RING], w2c[a] // RING, 1, q.loop)
                sq_t[a] = V(vv.tensor_tensor, H1[:, a, :, :], R1[:, a, :].rearrange("p (h t) -> p h t", h=2),
                            R1[:, a, :].rearrange("p (h t) -> p h t", h=2), ALU.mult, w=[r, w2_before])
                ada_chunk(adac[a], ada_col + 2 * a, conds=conds, junk=view(aA, 1024))
            for a in range(2):
                wait_chunk("pe", w2c[a])
                wait("pe", sq_t[a])
                for j in range(2):
                    for m in range(KT):
                        ins = mm(PS[:, 4 + m // 2, (m % 2) * 256:(m % 2 + 1) * 256],
                                 chunk(w2c[a])[:, (j * 8 + m) * P:(j * 8 + m + 1) * P], H1[:, a, j, :], False, False)
                done("pe", ins, frees=w2c[a])

        per_ada = 3 * len(conds) - 1
        q.run_loop(turns, per, body)
        return c0 + 6 * turns

    all_wait()
    c_now = mlp(c_now, out, 8, True, 48, ((0, 0),), True)
    V(vv.tensor_scalar, G1, MOD[:, 40:48], 1.0, None, ALU.add)
    ada_bias(48, 32, "ada_b", 48)

    def evacuate(gcols):
        pe = last("pe")
        return [add_branch(n, PS[:, 4 + n // 2, (n % 2) * 256:(n % 2 + 1) * 256], gcols[:, n:n + 1], pe) for n in range(KT)]

    xt = evacuate(G1)
    out, xs = layer_norm(1, xt, MOD[:, 56:64], MOD[:, 48:56], ALPHA, HX)

    all_wait()
    rp = lambda n, j, k=1: RPAR[:, RCOL[n][0] + j:RCOL[n][0] + j + k]
    RM = view(aM + 128, 256, BW)
    cs, hba, hbx = RM[:, 0:32], RM[:, 32:64], RM[:, 64:96]
    t0, t1, t2 = RM[:, 96:128], RM[:, 128:160], RM[:, 160:192]
    lam = rp("lam", 0, 32)
    V(vv.tensor_scalar, t0, lam, -1.0, None, ALU.mult)
    V(vv.tensor_tensor, t1, t0, lam, ALU.min)
    A(t1, t1, ACT.Exp, w=[last("dve")])
    V(vv.tensor_scalar, t2, t1, 2.0, None, ALU.add, w=[last("act")])
    V(vv.reciprocal, t2, t2)
    V(vv.tensor_tensor, t1, t1, t2, ALU.mult)
    V(vv.tensor_tensor, t2, t1, t1, ALU.mult)
    V(vv.tensor_scalar, cs, t2, 1.0 / 17, None, ALU.mult)
    for d in (15, 13, 11, 9, 7, 5, 3):
        V(vv.scalar_tensor_tensor, cs, cs, 1.0 / d, t2, ALU.add, ALU.mult)
    V(vv.scalar_tensor_tensor, cs, cs, 1.0, t1, ALU.add, ALU.mult)
    V(vv.tensor_scalar, cs, cs, 4.0, None, ALU.mult)
    V(vv.tensor_scalar, t0, t0, 0.0, 2.0, ALU.max, ALU.mult)
    V(vv.tensor_tensor, cs, cs, t0, ALU.add)
    V(vv.tensor_scalar, hba, rp("ba", 0, 32), 0.5, None, ALU.mult)
    V(vv.tensor_scalar, hbx, rp("bx", 0, 32), 0.5, None, ALU.mult)
    GT = view(aA, 4096, BW).rearrange("p (b t) -> p b t", b=NB)
    Y = view(aT1, 4096, BW).rearrange("p (b t) -> p b t", b=NB)
    XP = view(aH + 2048, 520, BW).rearrange("p (a t) -> p a t", a=2)
    XCV = view(aH + 2600, 1024, BW).rearrange("p (a t) -> p a t", a=4)
    TLb = view(aA + 4096, 2048, BW).rearrange("p (a j d t) -> p a j d t", a=2, j=2, d=2)
    W2b = view(aA + 6144, 2048, BW).rearrange("p (a j d t) -> p a j d t", a=2, j=2, d=2)
    AAb = view(aA + 8192, 2048, BW).rearrange("p (a j d t) -> p a j d t", a=2, j=2, d=2)
    TAb = view(aA + 10240, 1024, BW).rearrange("p (a d t) -> p a d t", a=2, d=2)
    TIb = view(aA + 11264, 1024, BW).rearrange("p (a d t) -> p a d t", a=2, d=2)
    HSC = view(aA + 12288, 1024, BW).rearrange("p (a d t) -> p a d t", a=2, d=2)
    V(vv.memset, XP[:, :, 0:2], 0.0)
    V(vv.memset, XP[:, :, 258:260], 0.0)
    free = [None] * 8
    xcv_t, gate_bank = {}, {}
    w_read = [None, None]

    def z_of(b):
        c = rnn_c[b]
        wait_chunk("pe", c)
        bank = b % 2
        wait("pe", free[bank])
        for j in range(2):
            for k in range(KT):
                wait("pe", out[k]) if b == 0 and j == 0 else None
                ins = mm(PS[0:BW, bank, j * 256:(j + 1) * 256], chunk(c)[:, j * 768 + k * BW:j * 768 + (k + 1) * BW], HX[:, k, 0:S], k == 0, k == KT - 1)
        pe = done("pe", ins)
        A(XP[:, bank, 2:258], PS[0:BW, bank, 0:256], ACT.Copy, w=[pe, xcv_t.get(b - 2)])
        a1 = last("act")
        free[bank] = A(GT[:, b, :], PS[0:BW, bank, 256:512], ACT.Copy)
        xc = XCV[:, b % 4, :]
        V(vv.tensor_scalar, xc, XP[:, bank, 0:256], rp("cw", b), rp("cb", b), ALU.mult, ALU.add, w=[a1, gate_bank.get(b - 4)])
        for j in range(1, 4):
            V(vv.scalar_tensor_tensor, xc, XP[:, bank, j:j + 256], rp("cw", 16 * j + b), xc, ALU.mult, ALU.add)
        xcv_t[b] = last("dve")

    grp_tok = {}

    def gates_of(b):
        c = rnn_c[b]
        g, j = (b // 2) % 2, b % 2
        gb = 2 + 2 * (b % 2)
        wait("pe", xcv_t[b], free[gb], free[gb + 1])
        for d in range(2):
            for m in range(2):
                o = 1536 + (2 * d + m) * BW
                ins = mm(PS[0:BW, gb + d, m * 256:(m + 1) * 256], chunk(c)[0:BW, o:o + BW], XCV[:, b % 4, :], True, True)
        pe = done("pe", ins, frees=c)
        gate_bank[b] = pe
        s = b % 2
        for d in range(2):
            cc = 16 * d + b
            A(TAb[:, s, d, :], PS[0:BW, gb + d, 0:256], ACT.Tanh, scale=0.5, bias=hba[:, cc:cc + 1], w=[pe])
            A(TIb[:, s, d, :], PS[0:BW, gb + d, 256:512], ACT.Tanh, scale=0.5, bias=hbx[:, cc:cc + 1], w=[w_read[s]])
            free[gb + d] = last("act")
            A(TLb[:, g, j, d, :], TAb[:, s, d, :], ACT.Tanh, scale=cs[:, cc:cc + 1], bias=cs[:, cc:cc + 1], w=[grp_tok.get(b // 2 - 2)])
        a = last("act")
        AA, W2 = AAb[:, g, j, :, :], W2b[:, g, j, :, :]
        V(vv.tensor_scalar, AA, TLb[:, g, j, :, :], 1.0, None, ALU.add, w=[a])
        V(vv.reciprocal, AA, AA)
        w_read[s] = V(vv.scalar_tensor_tensor, W2, TIb[:, s, :, :], 1.0, XCV[:, b % 4, :].unsqueeze(1).broadcast_to([BW, 2, S]), ALU.add, ALU.mult)
        V(vv.tensor_tensor, W2, W2, AA, ALU.mult)
        V(vv.tensor_scalar, AA, AA, 2.0, -1.0, ALU.mult, ALU.add)
        gate_bank[b] = last("dve")

    hsc_free = [None, None]

    def scan_pair(gi):
        g = gi % 2
        a = A(TLb[:, g, :, :, :], TLb[:, g, :, :, :], ACT.Sqrt, w=[last("dve")])
        V(vv.tensor_tensor, W2b[:, g, :, :, :], W2b[:, g, :, :, :], TLb[:, g, :, :, :], ALU.mult, w=[a])
        for j in range(2):
            b = 2 * gi + j
            V(vv.tensor_tensor_scan, HSC[:, j, 0, :], AAb[:, g, j, 0, :], W2b[:, g, j, 0, :], 0.0, ALU.mult, ALU.add, w=[hsc_free[j]])
            V(vv.tensor_tensor_scan, HSC[:, j, 1, ::-1], AAb[:, g, j, 1, ::-1], W2b[:, g, j, 1, ::-1], 0.0, ALU.mult, ALU.add)
            hsc_free[j] = G(nc.gpsimd.tensor_tensor, Y[:, b, :], HSC[:, j, 0, :], HSC[:, j, 1, :], ALU.add, w=[last("dve")])
        grp_tok[gi] = last("dve")

    rnn_c = [c_now + 2 * b for b in range(NB)]
    ada_c = [c_now + 2 * b + 1 for b in range(NB)]
    ada_cols = [80 + 2 * j for j in range(8)] + [128 + 2 * j for j in range(8)]
    z_of(0)
    for b in range(NB):
        if b + 1 < NB:
            z_of(b + 1)
        gates_of(b)
        wait("dve", silu_c2) if b == 8 else None
        ada_chunk(ada_c[b], ada_cols[b], conds=(((0 if b < 8 else 1), 0),), junk=PS[:, 6:8, :].rearrange("p b n -> p (b n)"))
        if b % 2 == 1 and b >= 3:
            scan_pair(b // 2 - 1)
    scan_pair(NB // 2 - 1)
    c_now += 2 * NB

    s_late = nc.alloc_semaphore("s_late")
    clear_sums()
    for b4 in range(4):
        bs = slice(4 * b4, 4 * b4 + 4)
        a = A(GT[:, bs, :], GT[:, bs, :], ACT.Gelu_apprx_tanh)
        v = V(vv.tensor_tensor, Y[:, bs, :], Y[:, bs, :], GT[:, bs, :], ALU.mult, w=[a, last("pool")])
        for j2 in range(2):
            c = c_now + 2 * b4 + j2
            wait_chunk("pe", c)
            wait("pe", v)
            for j in range(2):
                for m in range(KT):
                    ins = mm(PS[:, 4 + m // 2, (m % 2) * 256:(m % 2 + 1) * 256],
                             chunk(c)[0:BW, j * 1024 + m * P:j * 1024 + (m + 1) * P], Y[:, 4 * b4 + 2 * j2 + j, :], False, False)
            done("pe", ins, frees=c)
    c_now += 8
    ada_bias(80, 16, "ada_b", 80)
    ada_bias(128, 16, "ada_b2", 32)
    V(vv.tensor_scalar, G1, MOD[:, 64:72], 1.0, None, ALU.add)
    xt = evacuate(G1)
    out, xs = layer_norm(2, xt, MOD[:, 80:88], MOD[:, 72:80], ALPHA, HX)

    all_wait()
    POS = view(aA + 8192, 2048).rearrange("p (k t) -> p k t", k=KT)
    CTX = view(aA + 10240, 2048).rearrange("p (k t) -> p k t", k=KT)
    nc.scalar.dma_start(POS, posT).then_inc(s_late, 16)
    nc.scalar.dma_start(CTX, ctxT).then_inc(s_late, 16)
    LATE = Tok(s_late, 32, 0, None)

    def rms_rows(src, w, xnorm, n=KT, m=D, sq=None):
        sq = T2 if sq is None else sq
        a = A(sq[:, 0:n, :], src, ACT.Square, w=w)
        wait("pe", a)
        for k in range(n):
            ins = mm(VAR, ONES, sq[:, k, :], k == 0, k == n - 1)
        pe = done("pe", ins)
        root(RSTD, VAR, 1.0 / m, par_("eps6"), [pe])
        return V(vv.tensor_tensor, xnorm, src, RSTD.unsqueeze(1).broadcast_to([P, n, S]), ALU.mult)

    rms_rows(CTX, [LATE], CTX)
    all_wait()
    c_now = mlp(c_now, out, 4, True, 96, ((1, 0), (2, 48)), False)
    c_now = mlp(c_now, out, 4, False, 112, ((1, 0),), True)
    V(vv.tensor_scalar, G1, MOD[:, 88:96], 1.0, None, ALU.add)
    ada_bias(96, 32, "ada_b2", 0)
    ada_bias(144, 16, "ada_b2", 0)
    xt = evacuate(G1)
    out, xs = layer_norm(3, xt, None, None, 1.0, None)

    wait("dve", LATE)
    for k in range(KT):
        v = V(vv.tensor_tensor, X[:, k, :], X[:, k, :], POS[:, k, :], ALU.add)
    sc2 = combo[:, 0:8]

    def modulate_norm(xnorm, gname, shift, scale, lo):
        V(vv.tensor_scalar, sc2, MOD[:, scale:scale + 8], 1.0, None, ALU.add)
        V(vv.tensor_tensor, sc2, sc2, par_(gname, 0, 8), ALU.mult)
        return [V(vv.tensor_scalar, H2[:, k, lo:lo + S], xnorm[:, k, :], sc2[:, k:k + 1], MOD[:, shift + k:shift + k + 1], ALU.mult, ALU.add)
                for k in range(KT)]

    modulate_norm(CTX, "n1g", 144, 152, S)
    rms_rows(X[:, :, :], [v], XC[:, :, :])
    htok = modulate_norm(XC, "n1g", 96, 104, 0)
    all_wait()
    Fg = view(aA, 4096).rearrange("p (n t) -> p n t", n=8)
    Vv = view(aA + 4096, 2048).rearrange("p (b n) -> p b n", b=4)
    Q = view(aA + 6144, 1024)
    Gg = view(aA + 7168, 1024)
    ZP = view(aA + 8192, 1548).rearrange("p (n t) -> p n t", n=6)
    FZ = view(aA + 9740, 512).rearrange("p (n t) -> p n t", n=2)
    SG = view(aA + 10252, 1024).rearrange("p (a n) -> p a n", a=2)
    V(vv.memset, ZP[:, :, 0:1], 0.0)
    V(vv.memset, ZP[:, :, 257:258], 0.0)
    LB = MISC[:, 128:152]
    lbr = par_("lb", 0, 8)
    V(vv.tensor_tensor, LB[:, 0:8], lbr, lbr, ALU.subtract)
    A(LB[:, 0:8], LB[:, 0:8], ACT.Exp, w=[last("dve")])
    V(vv.reciprocal, LB[:, 8:16], LB[:, 0:8], w=[last("act")])
    V(vv.tensor_tensor, LB[:, 0:8], LB[:, 0:8], LB[:, 8:16], ALU.mult)
    V(vv.tensor_tensor, LB[:, 0:8], LB[:, 0:8], LB[:, 0:8], ALU.subtract)
    V(vv.tensor_scalar, LB[:, 8:16], LB[:, 0:8], -1.0, 1.0, ALU.mult, ALU.add)
    free = [None] * 8
    f_t = []
    for n in range(4):
        c = c_now + n
        wait_chunk("pe", c)
        for j in range(2):
            bank = 2 * (n % 2) + j
            wait("pe", free[bank])
            for k in range(KT):
                ins = mm(PS[:, bank, :], chunk(c)[:, (j * 8 + k) * P:(j * 8 + k + 1) * P], H2[:, k, :], k == 0, k == KT - 1)
            pe = done("pe", ins, frees=c if j else None)
            t = 2 * n + j
            free[bank] = A(Fg[:, t, :], PS[:, bank, :], ACT.Sigmoid, w=[pe])
            f_t.append(V(vv.tensor_scalar, Fg[:, t, :], Fg[:, t, :], LB[:, 8 + t:9 + t], LB[:, t:t + 1], ALU.mult, ALU.add, w=[free[bank]]))
    for n in range(2):
        c = c_now + 4 + n
        wait_chunk("pe", c)
        for b in range(4):
            for k in range(4):
                kk = 4 * n + k
                lo = b * P
                ins = mm(PS[:, 4 + b, :], H2[:, kk, lo:lo + P], chunk(c)[:, k * 512:(k + 1) * 512], kk == 0, kk == KT - 1)
        pe = done("pe", ins, frees=c)
    for b in range(4):
        free[4 + b] = A(Vv[:, b, :], PS[:, 4 + b, :], ACT.Copy, w=[pe])
    v_t = last("act")

    def in_tiles(c, bank):
        wait_chunk("pe", c)
        wait("pe", free[bank])
        for j in range(2):
            for k in range(KT):
                ins = mm(PS[:, bank, j * 256:(j + 1) * 256], chunk(c)[:, (j * 8 + k) * P:(j * 8 + k + 1) * P], H2[:, k, 0:S], k == 0, k == KT - 1)
        return done("pe", ins, frees=c)

    for n in range(2):
        pe = in_tiles(c_now + 6 + n, n)
        a = A(SG[:, n, :], PS[:, n, :], ACT.Sigmoid, w=[pe])
        free[n] = q_t = V(vv.scalar_tensor_tensor, Q[:, n * 512:(n + 1) * 512], PS[:, n, :], P ** -0.5, SG[:, n, :], ALU.mult, ALU.mult, w=[a])
    for n in range(3):
        pe = in_tiles(c_now + 8 + n, 2 + n % 2)
        z_t = free[2 + n % 2] = A(ZP[:, 2 * n:2 * n + 2, 1:257], PS[:, 2 + n % 2, :].rearrange("p (n t) -> p n t", n=2), ACT.Copy,
                                  w=[pe, last("dve")])
    for n in range(2):
        pe = in_tiles(c_now + 11 + n, n)
        a = A(SG[:, n, :], PS[:, n, :], ACT.Sigmoid, w=[pe, q_t])
        free[n] = V(vv.tensor_tensor, Gg[:, n * 512:(n + 1) * 512], PS[:, n, :], SG[:, n, :], ALU.mult, w=[a])
    pe = in_tiles(c_now + 13, 3)
    fz_t = free[3] = A(FZ[:, :, :], PS[:, 3, :].rearrange("p (n t) -> p n t", n=2), ACT.Copy, w=[pe])
    c_now += 14

    all_wait()
    U = view(aA + 11276, 1536).rearrange("p (n t) -> p n t", n=6)
    VT2 = view(aA + 12812, 512).rearrange("p (b c) -> p b c", b=2)
    YS = view(aA + 13324, 1024).rearrange("p (r n) -> p r n", r=2)
    M1, M2, YV = view(aH, 512), view(aH + 512, 512), view(aH + 1024, 512).rearrange("p (n t) -> p n t", n=2)
    FA = view(aH + 2048, 1024).rearrange("p (b n) -> p b n", b=2)
    FY = view(aH + 3072, 512).rearrange("p (n t) -> p n t", n=2)
    MIX = T1
    for n in range(6):
        V(vv.tensor_scalar, U[:, n, :], ZP[:, n, 0:256], par_("hycw", n), par_("hycb", n), ALU.mult, ALU.add)
        for j in (1, 2):
            V(vv.scalar_tensor_tensor, U[:, n, :], ZP[:, n, j:j + 256], par_("hycw", 6 * j + n), U[:, n, :], ALU.mult, ALU.add)
    y_in, y_t = U[:, 0:2, :], last("dve")
    for o in range(2):
        wait("pe", y_t)
        for b in range(2):
            for n in range(2):
                ins = nc.tensor.transpose(PS[:, 0, b * 256 + n * P:b * 256 + (n + 1) * P], y_in[:, n, b * P:(b + 1) * P], ident)
        pe = done("pe", ins)
        a = A(VT2[:, :, :], PS[:, 0, :].rearrange("p (b c) -> p b c", b=2), ACT.Copy, w=[pe])
        wait("pe", a)
        for r, tb_ in enumerate(("dc", "ds")):
            for f in range(2):
                for b in range(2):
                    ins = mm(PS[:, 1 + r, f * 256:(f + 1) * 256], tab_(tb_)[:, b * 256 + f * P:b * 256 + (f + 1) * P], VT2[:, b, :], b == 0, b == 1)
        pe = done("pe", ins)
        kr, ks = KFv[:, o, 0, :, :].rearrange("p f c -> p (f c)"), KFv[:, o, 1, :, :].rearrange("p f c -> p (f c)")
        V(vv.tensor_tensor, M1, PS[:, 1, :], kr, ALU.mult, w=[pe])
        V(vv.tensor_tensor, M2, PS[:, 2, :], ks, ALU.mult)
        V(vv.tensor_tensor, YS[:, 0, :], M1, M2, ALU.subtract)
        V(vv.tensor_tensor, M1, PS[:, 1, :], ks, ALU.mult)
        V(vv.tensor_tensor, M2, PS[:, 2, :], kr, ALU.mult)
        v = V(vv.tensor_tensor, YS[:, 1, :], M1, M2, ALU.add)
        wait("pe", v)
        for n in range(2):
            for r, tb_ in enumerate(("ic", "is")):
                for f in range(2):
                    ins = mm(PS[:, 3, n * 256:(n + 1) * 256], YS[:, r, f * 256 + n * P:f * 256 + (n + 1) * P], tab_(tb_)[:, f * 256:(f + 1) * 256],
                             r == 0 and f == 0, r == 1 and f == 1)
        pe = done("pe", ins)
        for n in range(2):
            V(vv.scalar_tensor_tensor, YV[:, n, :], y_in[:, n, :], par_("hybias", 2 * o + n), PS[:, 3, n * 256:(n + 1) * 256], ALU.mult, ALU.add, w=[pe])
        y_t = V(vv.tensor_tensor, YV[:, :, :], YV[:, :, :], U[:, 2 + 2 * o:4 + 2 * o, :], ALU.mult)
        y_in = YV
    rms_rows(YV[:, :, :], [y_t], YV[:, :, :], 2, 256)
    for n in range(2):
        V(vv.tensor_scalar, MIX[:, n, :], YV[:, n, :], par_("hyg", n), None, ALU.mult)

    wait("pe", fz_t)
    for b in range(2):
        for n in range(2):
            for r, tb_ in enumerate(("fcc", "fcs")):
                ins = mm(PS[:, 4 + r, b * 256 + n * P:b * 256 + (n + 1) * P], FZ[:, n, b * P:(b + 1) * P], tab_(tb_), True, True)
    pe = done("pe", ins)
    for r in range(2):
        a = A(FA[:, r, :], PS[:, 4 + r, :], ACT.Copy, w=[pe])
    wait("pe", a)
    for n in range(2):
        for r, tb_ in enumerate(("flc", "fls")):
            for b in range(2):
                ins = mm(PS[:, 6, n * 256:(n + 1) * 256], FA[:, r, b * 256 + n * P:b * 256 + (n + 1) * P], tab_(tb_)[:, b * 256:(b + 1) * 256],
                         r == 0 and b == 0, r == 1 and b == 1)
    pe = done("pe", ins)
    a = A(FY[:, :, :], PS[:, 6, :].rearrange("p (n t) -> p n t", n=2), ACT.Copy, w=[pe])
    wait("pe", a)
    for n in range(2):
        ins = mm(PS[:, 7, n * 256:(n + 1) * 256], par_("fnw", n * P, P), FY[:, n, :], True, True)
    pe = done("pe", ins)
    for n in range(2):
        v = V(vv.tensor_scalar, FZ[:, n, :], PS[:, 7, n * 256:(n + 1) * 256], par_("fnb", n), None, ALU.add, w=[pe])
    rms_rows(FZ[:, :, :], [v], FZ[:, :, :], 2, 256)
    for n in range(2):
        V(vv.tensor_scalar, MIX[:, 6 + n, :], FZ[:, n, :], par_("fng", n), None, ALU.mult)

    all_wait()
    ZERO = RS[:, 256:512]
    V(vv.memset, ZERO, 0.0)
    R = view(aT2, 2048).rearrange("p (n t) -> p n t", n=8)
    KC = view(aC, 2048).rearrange("p (n t) -> p n t", n=8)
    KCT = view(aA + 8192, 2048).rearrange("p (n d) -> p n d", n=16)
    ST = view(aA + 12288, 1024).rearrange("p (n v) -> p n v", n=8)
    V(vv.tensor_scalar, KC[:, :, :], Fg[:, :, S:2 * S], -1.0, 1.0, ALU.mult, ALU.add)
    for n in range(8):
        f = Fg[:, n, S:2 * S]
        if n < 4:
            V(vv.tensor_tensor_scan, R[:, n, ::-1], Fg[:, n, 2 * S - 1:S - 1:-1], ZERO, 1.0, ALU.mult, ALU.add)
        else:
            V(vv.tensor_tensor_scan, R[:, n, :], f, ZERO, 1.0, ALU.mult, ALU.add)
    V(vv.tensor_tensor, KC[:, 0:4, 0:S - 1], KC[:, 0:4, 0:S - 1], R[:, 0:4, 1:S], ALU.mult)
    v = V(vv.tensor_tensor, KC[:, 4:8, 1:S], KC[:, 4:8, 1:S], R[:, 4:8, 0:S - 1], ALU.mult)
    wait("pe", v)
    for n in range(16):
        ins = nc.tensor.transpose(PS[:, n // 4, (n % 4) * P:(n % 4 + 1) * P], KC[:, n // 2, (n % 2) * P:(n % 2 + 1) * P], ident)
    pe = done("pe", ins)
    for b in range(4):
        a = A(KCT[:, 4 * b:4 * b + 4, :], PS[:, b, :].rearrange("p (n d) -> p n d", n=4), ACT.Copy, w=[pe])
    wait("pe", a)
    for n in range(8):
        for b in range(2):
            ins = mm(PS[:, 4 + n // 4, (n % 4) * P:(n % 4 + 1) * P], KCT[:, 2 * n + b, :], Vv[:, 2 + b, (n % 4) * P:(n % 4 + 1) * P], b == 0, b == 1)
    pe = done("pe", ins)
    a = A(ST[:, :, :], PS[:, 4:6, :].rearrange("p b (n v) -> p (b n) v", n=4), ACT.Copy, w=[pe])

    KX = view(aT2, 2048)
    KFx, KBx = KX[:, 0:1024], KX[:, 1024:2048]
    PF, SF, SBk, PBk = (view(aH + 1024 * j, 1024) for j in range(4))
    QP, KP = view(aA + 8192, 1024), view(aA + 9216, 1024)
    ATD = view(aA + 10240, 1024).rearrange("p (n t) -> p n t", n=8)
    ATO = view(aA + 11264, 1024).rearrange("p (n t) -> p n t", n=8)
    h4 = lambda ap: ap.rearrange("p (h t) -> p h t", h=4)
    wait("pool", last("dve"), last("act"))
    G(nc.gpsimd.memset, SF, 1.0)
    G(nc.gpsimd.memset, PBk, 1.0)
    A(h4(PF), Fg[:, 0:4, 0:S], ACT.Copy, w=[last("dve")])
    a = A(h4(SBk), Fg[:, 4:8, 0:S], ACT.Copy)
    V(vv.tensor_scalar, h4(KFx), Fg[:, 0:4, 0:S], -1.0, 1.0, ALU.mult, ALU.add, w=[last("pe"), a])
    V(vv.tensor_scalar, h4(KBx), Fg[:, 4:8, 0:S], -1.0, 1.0, ALU.mult, ALU.add, w=[last("pool")])
    halves = lambda ap, n: ap.rearrange("p (g s t) -> p g s t", s=2, t=n)
    for lev in range(9):
        pe_before = last("pe")
        if lev == 0:
            v = V(vv.tensor_tensor, KP, KFx, KBx, ALU.add, w=[pe_before])
            qp, kp_t = Q, v
        else:
            n = 1 << (lev - 1)
            l = lambda ap: halves(ap, n)[:, :, 0, :]
            r = lambda ap: halves(ap, n)[:, :, 1, :]
            G(nc.gpsimd.tensor_tensor, l(KP), l(KFx), l(SF), ALU.mult, w=[pe_before, last("dve")])
            kp_t = G(nc.gpsimd.tensor_tensor, r(KP), r(KBx), r(PBk), ALU.mult)
            V(vv.tensor_tensor, r(QP), r(Q), r(PF), ALU.mult, w=[pe_before])
            v = V(vv.tensor_tensor, l(QP), l(Q), l(SBk), ALU.mult)
            qp = QP
        wait("pe", v, kp_t)
        b0 = 2 * (lev % 2)
        for h in range(4):
            for b in range(2):
                s_b = b if lev < 8 else 1 - b
                ins = mm(PS[:, b0 + h // 2, ((h % 2) * 2 + b) * P:((h % 2) * 2 + b + 1) * P],
                         KP[:, h * S + s_b * P:h * S + (s_b + 1) * P], qp[:, h * S + b * P:h * S + (b + 1) * P], True, True)
        pe = done("pe", ins)
        if lev > 0:
            shape = [P, 1024 // (2 * n), n]
            if lev < 8:
                V(vv.tensor_tensor, l(SF), l(SF), r(PF)[:, :, n - 1:n].broadcast_to(shape), ALU.mult, w=[kp_t])
                V(vv.tensor_tensor, r(PBk), r(PBk), l(SBk)[:, :, 0:1].broadcast_to(shape), ALU.mult)
            V(vv.tensor_tensor, r(PF), r(PF), l(PF)[:, :, n - 1:n].broadcast_to(shape), ALU.mult)
            V(vv.tensor_tensor, l(SBk), l(SBk), r(SBk)[:, :, 0:1].broadcast_to(shape), ALU.mult)
        mask = tab_("lmask")[:, (lev % 8) * P:(lev % 8 + 1) * P].unsqueeze(1).broadcast_to([P, 8, P])
        data = PS[:, b0:b0 + 2, :].rearrange("p b (n t) -> p (b n) t", n=4)
        if lev == 0:
            V(vv.tensor_tensor, ATD[:, :, :], data, mask, ALU.mult, w=[pe])
        elif lev < 8:
            V(vv.copy_predicated, ATD[:, :, :], mask.bitcast(U32), data, w=[pe])
        else:
            V(vv.tensor_copy, ATO[:, :, :], data, w=[pe])
    V(vv.tensor_tensor, QP, Q, PF, ALU.mult, w=[last("pe")])
    v = V(vv.tensor_tensor, KP, Q, SBk, ALU.mult)
    wait("pe", v)
    for h in range(4):
        for b in range(2):
            o = PS[:, 4 + h // 2, ((h % 2) * 2 + b) * P:((h % 2) * 2 + b + 1) * P]
            mm(o, Vv[:, b, h * P:(h + 1) * P], ATD[:, 2 * h + b, :], True, False)
            mm(o, Vv[:, 1 - b, h * P:(h + 1) * P], ATO[:, 2 * h + b, :], False, False)
            mm(o, ST[:, h, :], QP[:, h * S + b * P:h * S + (b + 1) * P], False, False)
            ins = mm(o, ST[:, 4 + h, :], KP[:, h * S + b * P:h * S + (b + 1) * P], False, True)
    pe = done("pe", ins)
    ob = PS[:, 4:6, :].rearrange("p b n -> p (b n)")
    a = A(QP, ob, ACT.Square, w=[pe])
    V(vv.tensor_copy, KP, ob, w=[a])
    wait("pe", a)
    for h2_ in range(2):
        ins = mm(PS[:, 6 + h2_, :], ONES, QP[:, h2_ * 512:(h2_ + 1) * 512], True, True)
    pe = done("pe", ins)
    rb = PF
    root(rb, PS[:, 6:8, :].rearrange("p b n -> p (b n)"), 1.0 / P, par_("eps6"), [pe])
    V(vv.tensor_tensor, KP, KP, rb, ALU.mult)
    for h in range(4):
        v = V(vv.scalar_tensor_tensor, MIX[:, 2 + h, :], KP[:, h * S:(h + 1) * S], par_("hgg", h), Gg[:, h * S:(h + 1) * S], ALU.mult, ALU.mult)
    free = [None] * 8
    xt = project(range(c_now, c_now + 4), MIX, v, MOD[:, 112:120])
    c_now += 4
    rms_rows(X[:, :, :], xt, XC[:, :, :])
    htok = modulate_norm(XC, "n2g", 120, 128, 0)

    all_wait()
    COMB = view(aA, 4096).rearrange("p (e t) -> p e t", e=NE)
    SEL = view(aA + 4096, 2048, NE)
    s_sel = nc.alloc_semaphore("s_sel")
    nc.scalar.dma_start(SEL, sel).then_inc(s_sel, 16)
    for b in range(2):
        for k in range(KT):
            ins = mm(PS[:, b, 0:NE], H2[:, k, b * P:(b + 1) * P], par_("rw", k * NE, NE), k == 0, k == KT - 1)
    pe = done("pe", ins)
    r0 = aA + 6144

    def r3(j, n=16):
        return view(r0 + 64 * j, 2 * n).rearrange("p (b e) -> p b e", b=2)

    PR, SE, ML, EX, E2 = r3(0), r3(1), r3(2), r3(3), r3(4)
    st = view(r0 + 512, 64)
    mx = st[:, 0:2]
    V(vv.tensor_reduce, mx, PS[:, 0:2, 0:NE], AX, ALU.max, w=[pe])
    V(vv.tensor_scalar, mx, mx, -1.0, None, ALU.mult)
    for b in range(2):
        a = A(PR[:, b, :], PS[:, b, 0:NE], ACT.Exp, bias=st[:, b:b + 1], accum_out=st[:, 2 + b:3 + b], w=[last("dve")])
    V(vv.reciprocal, st[:, 4:6], st[:, 2:4], w=[a])
    V(vv.tensor_tensor, PR, PR, st[:, 4:6].unsqueeze(2).broadcast_to([P, 2, NE]), ALU.mult)
    V(vv.tensor_tensor, SE, PR, par_("rb", 0, 16).unsqueeze(1).broadcast_to([P, 2, NE]), ALU.add)
    g4 = view(r0 + 64, 32).rearrange("p (g e) -> p g e", e=4)
    GS, GT2 = view(r0 + 320, 8), view(r0 + 352, 16).rearrange("p (g e) -> p g e", e=2)
    pairs = [(g4[:, :, 0:4:2], g4[:, :, 1:4:2]), (g4[:, :, 0:2], g4[:, :, 2:4]), (g4[:, :, 0:2], g4[:, :, 3:1:-1])]
    for j, (a_, b_) in enumerate(pairs):
        V(vv.tensor_tensor, GT2, a_, b_, ALU.add)
        dst = GS if j == 0 else st[:, 8:16]
        V(vv.tensor_reduce, dst, GT2, AX, ALU.max)
        if j:
            V(vv.tensor_tensor, GS, GS, dst, ALU.max)

    def first_max(val, n, onehot, m, tmp, rows=2):
        V(vv.tensor_reduce, m, val, AX, ALU.max)
        V(vv.tensor_tensor, onehot, val, m.unsqueeze(2).broadcast_to([P, rows, n]), ALU.is_ge)
        io = tab_("iota")[:, 0:n].unsqueeze(1).broadcast_to([P, rows, n])
        V(vv.scalar_tensor_tensor, tmp, onehot, -100.0, io, ALU.mult, ALU.add)
        V(vv.tensor_reduce, m, tmp, AX, ALU.min)
        V(vv.tensor_tensor, onehot, tmp, m.unsqueeze(2).broadcast_to([P, rows, n]), ALU.is_equal)

    G3 = GS.rearrange("p (b g) -> p b g", b=2)
    GO, GTm = st[:, 16:24].rearrange("p (b g) -> p b g", b=2), st[:, 24:32].rearrange("p (b g) -> p b g", b=2)
    first_max(G3, 4, GO, st[:, 32:34], GTm)
    GM = view(r0 + 600, 32).rearrange("p (g e) -> p g e", e=4)
    V(vv.tensor_copy, GM, st[:, 16:24].unsqueeze(2).broadcast_to([P, 8, 4]))
    NG = view(r0 + 640, 32)
    V(vv.tensor_tensor, ML.rearrange("p b e -> p (b e)"), view(r0 + 64, 32), view(r0 + 600, 32), ALU.mult)
    V(vv.tensor_scalar, NG, view(r0 + 600, 32), 1e30, -1e30, ALU.mult, ALU.add)
    V(vv.tensor_tensor, view(r0 + 128, 32), view(r0 + 128, 32), NG, ALU.add)
    TM = view(r0 + 700, 32).rearrange("p (b e) -> p b e", b=2)
    first_max(ML, NE, EX, st[:, 34:36], TM)
    V(vv.scalar_tensor_tensor, ML, EX, -3e30, ML, ALU.mult, ALU.add)
    first_max(ML, NE, E2, st[:, 36:38], TM)
    V(vv.tensor_tensor, EX, EX, E2, ALU.add)
    V(vv.tensor_tensor, EX, EX, PR, ALU.mult)
    V(vv.tensor_reduce, st[:, 38:40], EX, AX, ALU.add)
    V(vv.reciprocal, st[:, 40:42], st[:, 38:40])
    v = V(vv.tensor_tensor, EX, EX, st[:, 40:42].unsqueeze(2).broadcast_to([P, 2, NE]), ALU.mult)
    wait("pe", v, Tok(s_sel, 16, 0, None))
    for b in range(2):
        ins = nc.tensor.transpose(PS[0:NE, 2, b * P:(b + 1) * P], EX[:, b, :], ident)
    pe = done("pe", ins)
    CT = view(r0 + 768, 256, NE)
    a = A(CT, PS[0:NE, 2, 0:256], ACT.Copy, w=[pe])
    wait("pe", a)
    for e in range(NE):
        wait("pe", a)
        ins = mm(PS[:, (e // 2) % 2, (e % 2) * 256:(e % 2 + 1) * 256], SEL[:, e * P:(e + 1) * P], CT, True, True)
        if e % 2:
            pe = done("pe", ins)
            a2 = A(COMB[:, e - 1:e + 1, :], PS[:, (e // 2) % 2, :].rearrange("p (e t) -> p e t", e=2), ACT.Copy, w=[pe])
            a, a_prev = (a if e == 1 else a_prev), a2
    clear_sums()
    HB = view(aA + 8192, 1024).rearrange("p (a n) -> p a n", a=2)
    SGe = view(aA + 9216, 1024).rearrange("p (a n) -> p a n", a=2)
    UC = view(aA + 10240, 1024).rearrange("p (a n) -> p a n", a=2)
    all_wait()
    c0 = c_now

    def expert(i):
        K = q.loop.per_turn
        bd, h_t = q.eng["dve"][2], []
        dsem = q.eng["dve"][1]
        for a_ in range(2):
            before = Tok(dsem, bd + 3 * a_ + 3 - K["dve"], K["dve"], q.loop)
            for u in range(2):
                c = c0 + 2 * a_ + u
                wait_chunk("pe", c)
                if u == 0:
                    wait("pe", before)
                for j in range(2):
                    for k in range(KT):
                        ins = mm(PS[:, 2 * a_ + u, j * 256:(j + 1) * 256], chunk(c)[:, (j * 8 + k) * P:(j * 8 + k + 1) * P], H2[:, k, 0:S], k == 0, k == KT - 1)
                pe = done("pe", ins, frees=c)
                if u == 0:
                    s_t = A(SGe[:, a_, :], PS[:, 2 * a_, :], ACT.Sigmoid, w=[pe, before])
            comb = COMB[:, bass.ds(i, 1), :].broadcast_to([P, 2, S])
            V(vv.tensor_tensor, UC[:, a_, :].rearrange("p (j t) -> p j t", j=2), PS[:, 2 * a_ + 1, :].rearrange("p (j t) -> p j t", j=2), comb, ALU.mult, w=[pe])
            V(vv.tensor_tensor, SGe[:, a_, :], SGe[:, a_, :], PS[:, 2 * a_, :], ALU.mult, w=[s_t])
            down_before = Tok(q.freed[(c0 + 4 + a_) % RING], (c0 + 4 + a_) // RING, 1, q.loop)
            h_t.append(V(vv.tensor_tensor, HB[:, a_, :], SGe[:, a_, :], UC[:, a_, :], ALU.mult, w=[down_before]))
        for a_ in range(2):
            c = c0 + 4 + a_
            wait_chunk("pe", c)
            wait("pe", h_t[a_])
            for j in range(2):
                for m in range(KT):
                    ins = mm(PS[:, 4 + m // 2, (m % 2) * 256:(m % 2 + 1) * 256], chunk(c)[:, (j * 8 + m) * P:(j * 8 + m + 1) * P],
                             HB[:, a_, j * 256:(j + 1) * 256], False, False)
            done("pe", ins, frees=c)

    q.run_loop(NE, {"pe": 0, "dve": 6, "act": 2, "pool": 0}, expert)
    c_now += 6 * NE
    assert c_now == N_CHUNKS, c_now
    xt = evacuate(MOD[:, 136:144])
    rms_rows(X[:, :, :], xt, XC[:, :, :])
    s_out = nc.alloc_semaphore("s_out")
    for k in range(KT):
        v = V(vv.tensor_scalar, X[:, k, :], XC[:, k, :], par_("fing", k), None, ALU.mult)
        if k % 4 == 3:
            nc.sync.wait_ge(v.sem, v.n)
            nc.sync.dma_start(outT[:, k - 3:k + 1, :], X[:, k - 3:k + 1, :]).then_inc(s_out, 16)
    nc.sync.wait_ge(s_out, 32)


def tables():
    f64, f32 = np.float64, np.float32
    t = np.arange(S)
    out = {}
    out["ident"] = np.eye(P)
    inv = f32(500000.0) ** (-np.arange(0, 32, 2, dtype=f32) / f32(32))
    ang = (t.astype(f32)[:, None] * inv[None, :]).astype(f32)
    z = np.zeros((P, S))
    out["ropec"] = z.copy()
    out["ropec"][0:16] = out["ropec"][16:32] = np.cos(ang.astype(f64)).T
    out["ropes"] = z.copy()
    out["ropes"][0:16] = out["ropes"][16:32] = np.sin(ang.astype(f64)).T
    r = np.zeros((P, 32))
    for m in range(16):
        r[m + 16, m] = -1.0
        r[m, m + 16] = 1.0
    out["roper"] = r
    qi = np.arange(S).reshape(2, P).T
    out["amask"] = np.where(np.abs(qi[:, :, None] - t[None, None, :]) <= WIN, 0.0, -1e30).reshape(P, 512)
    tt = np.linspace(0.0, 1.0, S, dtype=f32)
    w = (f32(2.0 * math.pi) * t.astype(f32) / f32(S)).astype(f32)
    bands = np.linspace(1e-4, 15, 16, dtype=f32)
    bw = (bands[None, :] * w[:, None]).astype(f32).astype(f64)
    zf = np.concatenate([tt[:, None], np.cos(bw), -np.sin(bw)], axis=1).T
    out["zf"] = np.zeros((P, S))
    out["zf"][0:33] = zf
    f = np.arange(S)
    th = np.pi * ((2 * f[None, :] + 1) * t[:, None] % 1024) / 512.0
    blk = lambda m: m.reshape(2, P, S).transpose(1, 0, 2).reshape(P, 512)
    out["dc"], out["ds"] = blk(np.cos(th)), blk(np.sin(th))
    out["ic"], out["is"] = blk(np.cos(th).T / 256.0), blk(np.sin(th).T / 256.0)
    fl = 2 * np.pi * (np.outer(t, t) % S) / S
    out["flc"], out["fls"] = blk(np.cos(fl) / 16.0), blk(np.sin(fl) / 16.0)
    c = np.arange(64)
    fc = 2 * np.pi * (np.outer(c, c) % 64) / 64
    e2 = np.eye(2)
    out["fcc"], out["fcs"] = np.kron(e2, np.cos(fc) / 8.0), -np.kron(e2, np.sin(fc) / 8.0)
    dl = np.linspace(math.log(1e-2) / 1.5, math.log(1e-2) / 0.3, 256, dtype=f32)
    dec = np.exp((-tt[:, None] * np.abs(dl)[None, :]).astype(f32).astype(f64))
    out["decf"] = blk(dec)
    decb = dec.copy()
    decb[0] = 0.0
    out["decb"] = blk(decb)
    s_, t_ = np.arange(P)[:, None], np.arange(P)[None, :]
    lm = [np.eye(P)]
    for lev in range(1, 8):
        lm.append((s_ >> lev == t_ >> lev) & (s_ >> (lev - 1) != t_ >> (lev - 1)))
    out["lmask"] = np.stack(lm, 1).reshape(P, 1024)
    out["iota"] = np.tile(np.arange(16.0), (P, 1))
    tab = np.concatenate([out[n] for n in TCOL], axis=1).astype(f32)
    quarter = D // 4
    om = (f32(1.0) / (f32(10000.0) ** (np.arange(quarter, dtype=f32) / f32(quarter)))).astype(f32)
    ar = ((t // 64).astype(f32)[:, None] * om).astype(f32).astype(f64)
    ac = ((t % 64).astype(f32)[:, None] * om).astype(f32).astype(f64)
    pos = np.concatenate([np.sin(ar), np.cos(ar), np.sin(ac), np.cos(ac)], axis=1).astype(f32)
    sel = np.zeros((NE, NE, P), f32)
    for e in range(NE):
        sel[e, e] = 1.0
    return tab, fm(pos), sel.reshape(NE, NE * P)


def fm(x):
    return np.ascontiguousarray(x.T.reshape(-1, P, x.shape[0]).transpose(1, 0, 2))


def cols(v, p=P):
    return v.reshape(-1, p).T


def kernel(**inputs):
    import concourse.bacc as bacc
    from concourse.bass_utils import run_bass_kernel_spmd as run

    I = {k: np.asarray(v) for k, v in inputs.items()}

    def out_tiles(w):
        n = w.shape[1] // P
        return w.reshape(KT, P, n // 2, 2, P).transpose(2, 1, 3, 0, 4).reshape(n // 2, P, CH)

    def in_tiles(w):
        return w.reshape(-1, 2, P, D).transpose(0, 2, 1, 3).reshape(-1, P, CH)

    def ada(w):
        return in_tiles(w.T)

    def pad(a, axis, n):
        shape = list(a.shape)
        shape[axis] = n - a.shape[axis]
        return np.concatenate([a, np.zeros(shape, a.dtype)], axis=axis)

    def turns(*parts):
        return np.stack(parts, 1).reshape(-1, P, CH)

    a = [[ada(I["ada_w"][i, m]) for m in range(2)] for i in range(2)]
    a2 = ada(I["ada_w_2"][0])
    wi = I["attn_w_in"][0]
    v_in = wi[:, 1280:1536].reshape(KT, P, 256).transpose(1, 0, 2).reshape(1, P, CH)
    attn_in = np.concatenate([out_tiles(wi[:, 0:1280]), v_in])

    def mlp(w1, w2, ad):
        w1, w2 = out_tiles(w1), in_tiles(w2)
        return np.stack([w1[0::2], ad[0::2], w1[1::2], w2[0::2], ad[1::2], w2[1::2]], 1).reshape(-1, P, CH)

    rw = I["rnn_w_in"][0].reshape(KT, P, 2, NB, BW).transpose(3, 1, 2, 0, 4).reshape(NB, P, 2 * KT * BW)
    wa, wx = I["rnn_w_a"][0], I["rnn_w_x"][0]
    gw = np.stack([wa[0], wx[0], wa[1], wx[1]], 1).transpose(0, 2, 1, 3).reshape(NB, BW, 4 * BW)
    rnn = pad(np.concatenate([rw, pad(gw, 1, P)], axis=2), 2, CH)
    rnn_ada = np.concatenate([a[1][1][4:12], a2[16:24]])
    rnn = np.stack([rnn, rnn_ada], 1).reshape(-1, P, CH)
    rnn_out = pad(I["rnn_w_out"][0].reshape(8, 2, BW, D).transpose(0, 2, 1, 3).reshape(8, BW, CH), 1, P)
    w2i = I["w_in_2"][0]
    hy, hq, hff, hfb, hi, hg, fn = np.split(w2i, [768, 1280, 1792, 2304, 2816, 3328], axis=1)
    hi = hi.reshape(2, 4, P, 512).transpose(0, 2, 1, 3).reshape(2, P, CH)
    w_in2 = np.concatenate([out_tiles(hff), out_tiles(hfb), hi, out_tiles(hq), out_tiles(hy), out_tiles(hg), out_tiles(fn)])
    moe = []
    for e in range(NE):
        g_, u_ = out_tiles(I["moe_w_gate_2"][0, e]), out_tiles(I["moe_w_up_2"][0, e])
        d_ = in_tiles(I["moe_w_down_2"][0, e])
        moe += [g_[0:1], u_[0:1], g_[1:2], u_[1:2], d_]
    stream = np.concatenate([
        a[0][0], attn_in, a[0][1][0:8], out_tiles(I["attn_w_out"][0]), a[0][1][8:12],
        mlp(I["mlp_w1"][0], I["mlp_w2"][0], np.concatenate([a[1][0], a[1][1][0:4]])),
        rnn, rnn_out,
        mlp(I["mlp_w1"][1], I["mlp_w2"][1], a2[0:16]),
        w_in2, out_tiles(I["w_out_2"][0])] + moe)
    assert stream.shape[0] == N_CHUNKS, stream.shape

    rep = lambda v: np.broadcast_to(v.reshape(1, -1), (P, v.size))
    fnw = np.zeros((2, 2, 64, 2, 64), np.float32)
    fw = I["fn_w_2"][0].reshape(2, 2, 64, 64)
    for j in range(2):
        fnw[:, j, :, j, :] = fw[:, j]
    eps = np.ones((P, 1), np.float32)
    par = {"ada_b": cols(I["ada_b"]), "ada_b2": cols(I["ada_b_2"]), "ln_g": cols(I["ln_g"]), "ln_b": cols(I["ln_b"]),
           "n1g": cols(I["norm1_g_2"]), "n2g": cols(I["norm2_g_2"]), "fing": cols(I["final_norm_g_2"]),
           "hycw": cols(I["hy_conv_w_2"]), "hycb": cols(I["hy_conv_b_2"]), "hybias": cols(I["hy_bias_2"]),
           "hyg": cols(I["hy_norm_g_2"]), "lb": cols(I["hg_lower_bounds_2"]), "hgg": cols(I["hg_norm_g_2"]),
           "fnb": cols(I["fn_b_2"]), "fng": cols(I["fn_norm_g_2"]), "sinks": rep(I["attn_sinks"]), "rb": rep(I["router_b_2"]),
           "rw": I["router_w_2"].reshape(KT, P, NE).transpose(1, 0, 2).reshape(P, KT * NE),
           "fnw": fnw.reshape(2, P, P).transpose(1, 0, 2).reshape(P, 2 * P), "eps5": eps * np.float32(LN_EPS), "eps6": eps * np.float32(RMS_EPS)}
    par = np.concatenate([par[n] for n in PCOL], axis=1)
    rpar = np.concatenate([cols(I[n], BW) for n in ("rnn_conv_w", "rnn_conv_b", "rnn_b_a", "rnn_b_x", "rnn_lam")], axis=1)
    fpar = np.concatenate([pad(I["hy_filt_w1_2"][0], 0, 64), I["hy_filt_w2_2"][0], I["hy_filt_w3_2"][0]]
                          + [I[n][0].reshape(64, 1) for n in ("hy_filt_b1_2", "hy_filt_b2_2", "hy_filt_freq_2")], axis=1)
    tab, pos, sel = tables()
    data = {"stream": stream, "xT": fm(I["x"][0]), "ctxT": fm(I["ctx_2"][0]), "posT": pos,
            "cvec": np.concatenate([I["c"], I["c_2"], I["c_ctx_2"].reshape(1, D)]), "par": par, "rpar": rpar,
            "fpar": fpar, "tab": tab, "sel": sel}
    data = {k: np.ascontiguousarray(v) for k, v in data.items()}
    nc = bacc.Bacc("TRN2", target_bir_lowering=False, num_devices=1)
    aps = [nc.dram_tensor(n, v.shape, F32, kind="ExternalInput").ap() for n, v in data.items()]
    out = nc.dram_tensor("outT", (P, KT, S), F32, kind="ExternalOutput").ap()
    build(nc, *aps, out)
    r = run(nc, [data], core_ids=[0]).results[0]["outT"]
    return np.ascontiguousarray(r.transpose(1, 0, 2).reshape(D, S).T).reshape(1, S, D)
```

```python
import math

import numpy as np

import concourse.bass as bass
from concourse import mybir

F32 = mybir.dt.float32
F32R = mybir.dt.float32r
U32 = mybir.dt.uint32
ALU = mybir.AluOpType
ACT = mybir.ActivationFunctionType
AX = mybir.AxisListType.X

D, S, P = 1024, 256, 128
KT = D // P
NH, NKV, WIN = 8, 2, 128
NB, BW = 16, 96
FF = 4096
HGH = 4
NE, DE = 16, 512
DEPTH = 2
ALPHA = (2.0 * DEPTH) ** 0.25
LN_EPS, RMS_EPS = 1e-5, 1e-6
CH = 2048
HALF = CH // 2
RING = 3
SLOTS = 4
TURN = 6

ADA = 12
N_CHUNKS = 284


def _cols(spec):
    at, out = 0, {}
    for name, n in spec:
        out[name] = (at, at + n)
        at += n
    return out, at


PCOL, PN = _cols([("ada_b", 96), ("ada_b2", 48), ("ln_g", 32), ("ln_b", 32), ("n1g", 8), ("n2g", 8),
                  ("fing", 8), ("hycw", 18), ("hycb", 6), ("hybias", 4), ("hyg", 2), ("lb", 8),
                  ("hgg", 4), ("fnb", 2), ("fng", 2), ("sinks", 8), ("rb", 16), ("rw", 128),
                  ("fnw", 256), ("eps5", 1), ("eps6", 1)])
RCOL, RN = _cols([("cw", 64), ("cb", 16), ("ba", 32), ("bx", 32), ("lam", 32)])
FCOL, FN = _cols([("w1", 64), ("w2", 64), ("w3", 1024), ("b1", 1), ("b2", 1), ("fr", 1)])
TCOL, TN = _cols([("ropec", 256), ("ropes", 256), ("roper", 32), ("amask", 512)])
T2COL, T2N = _cols([("dc", 512), ("ds", 512), ("ic", 512), ("is", 512), ("flc", 512), ("fls", 512),
                    ("fcc", 128), ("fcs", 128), ("lmask", 1024), ("iota", 16), ("zf", 256), ("decf", 512), ("decb", 512)])


class Tok:

    def __init__(self, sem, n, k, loop):
        self.sem, self.n, self.k, self.loop = sem, n, k, loop

    def before(self):
        return Tok(self.sem, self.n - self.k, self.k, self.loop)


class Loop:
    def __init__(self, reg, turns, per_turn):
        self.reg, self.turns, self.per_turn = reg, turns, per_turn


class Count:

    def __init__(self, nc):
        self.nc = nc
        self.loop = None
        self.eng = {}
        for name, e in (("pe", nc.tensor), ("dve", nc.vector), ("act", nc.scalar), ("pool", nc.gpsimd)):
            self.eng[name] = [e, nc.alloc_semaphore("done_" + name), 0, None]
        self.arrived = [nc.alloc_semaphore(f"arrived{j}") for j in range(RING)]
        self.freed = [nc.alloc_semaphore(f"freed{j}") for j in range(RING)]

    def wait(self, name, *toks):
        e = self.eng[name][0]
        for t in toks:
            if t is None:
                continue
            if t.loop is not None and t.loop is self.loop and t.k:
                e.wait_ge(t.sem, self.loop.reg * t.k + t.n)
            elif t.loop is not None and t.loop is not self.loop:
                e.wait_ge(t.sem, t.n + (t.loop.turns - 1) * t.k)
            else:
                e.wait_ge(t.sem, t.n)

    def done(self, name, ins, frees=None):
        rec = self.eng[name]
        if frees is not None:
            ins.then_inc(self.freed[frees % RING], 1)
            rec[3] = Tok(self.freed[frees % RING], frees // RING + 1, TURN // RING if self.loop else 0, self.loop)
        else:
            ins.then_inc(rec[1], 1)
            rec[2] += 1
            rec[3] = Tok(rec[1], rec[2], self.loop.per_turn[name] if self.loop else 0, self.loop)
        return rec[3]

    def last(self, name):
        return self.eng[name][3]

    def wait_chunk(self, name, c):
        n = 16 * (c // RING + 1)
        self.wait(name, Tok(self.arrived[c % RING], n, 16 * (TURN // RING) if self.loop else 0, self.loop))

    def slots_of_turn_before(self, slot_free, first, halves):
        _, sem, n, _ = self.eng["pe"]
        k = self.loop.per_turn["pe"] if self.loop else 0
        for j in range(len(slot_free)):
            slot_free[(first + j) % len(slot_free)] = Tok(sem, n - len(slot_free) + 1 + j, k, self.loop)

    def run_loop(self, turns, per_turn, body):
        base = {k: v[2] for k, v in self.eng.items()}
        engines = [mybir.EngineType.PE, mybir.EngineType.DVE, mybir.EngineType.Activation, mybir.EngineType.Pool]
        with self.nc.Fori(0, turns, engines=engines) as i:
            self.loop = Loop(i, turns, per_turn)
            for k, v in self.eng.items():
                if v[2] and per_turn[k]:
                    v[3] = Tok(v[1], v[2], per_turn[k], self.loop)
            body(i)
            for k, v in self.eng.items():
                assert v[2] - base[k] == per_turn[k], (k, v[2] - base[k], per_turn[k])
                v[2] = base[k] + turns * per_turn[k]
            self.loop = None


def build(nc, stream, xT, ctxT, posT, cvec, par, rpar, fpar, ident_d, tab, tab2, sel, gw, outT):
    q = Count(nc)
    wait, done, last, wait_chunk = q.wait, q.done, q.last, q.wait_chunk
    TOTAL = 53200
    base = (nc.sbuf_base + 31) // 32 * 32
    PS = nc.alloc_psum_tensor("ps", [P, 8, 512], F32)
    at = [0]

    def place(n):
        a = at[0]
        at[0] += n
        return a

    def view(a, n, p=P):
        assert a + n <= TOTAL
        lo = a // 8 * 8
        return nc.alloc_sbuf_tensor_at(f"at{lo}_{n}", [p, a + n - lo], F32, offset=base + 4 * lo)[:, a - lo:]

    def rounded(name, a, n, p=P):
        return nc.alloc_sbuf_tensor_at(name, [p, n], F32R, offset=base + 4 * a)[:]

    ring = view(place(RING * CH), RING * CH)
    WH = rounded("w_high", place(SLOTS * HALF), SLOTS * HALF)
    WL = rounded("w_low", place(SLOTS * HALF), SLOTS * HALF)
    kt = lambda ap, n=KT: ap.rearrange("p (k t) -> p k t", k=n)
    X = kt(view(place(2048), 2048))
    aT1 = place(2048)
    aT2 = place(2048)
    T1, T2 = kt(view(aT1, 2048)), kt(view(aT2, 2048))
    aC = place(2048)
    CB = view(aC, 2048).rearrange("p (a n) -> p a n", a=2)
    MOD = view(place(160), 160)
    PAR = view(place(PN), PN)
    RPAR = view(place(RN), RN, BW)
    ident = view(place(P), P)
    ONES = view(place(P), P)
    aM = place(384)
    MISC = view(aM, 384)
    RS = view(place(512), 512)
    KF = view(place(2048), 2048)
    aX = place(4096)
    aXL = place(4096)
    XH = rounded("x_high", aX, 4096).rearrange("p (s k t) -> p s k t", s=2, k=KT)
    XL = rounded("x_low", aXL, 4096).rearrange("p (s k t) -> p s k t", s=2, k=KT)
    XIN = (XH[:, 0], XL[:, 0])
    aB = at[0]
    aTab2 = aB + 12288
    assert aTab2 + T2N <= TOTAL and aB % 8 == 0 and aX % 8 == 0, (aTab2 + T2N, aB, aX)
    TAB, TAB2 = view(aB, TN), view(aTab2, T2N)

    def par_(name, j=0, n=1):
        return PAR[:, PCOL[name][0] + j:PCOL[name][0] + j + n]

    def tab_(name, p=P):
        if name in TCOL:
            return TAB[0:p, TCOL[name][0]:TCOL[name][1]]
        return TAB2[0:p, T2COL[name][0]:T2COL[name][1]]

    def V(f, *a, w=(), frees=None, **k):
        wait("dve", last("dve"), *w)
        return done("dve", f(*a, **k), frees)

    def A(out, in_, func, w=(), **k):
        wait("act", last("act"), *w)
        return done("act", nc.scalar.activation(out, in_, func, **k))

    def G(f, *a, w=(), **k):
        wait("pool", last("pool"), *w)
        return done("pool", f(*a, **k))

    vv = nc.vector

    def mm(out, lhsT, rhs, start, stop):
        return nc.tensor.matmul(out, lhsT, rhs, start=start, stop=stop, skip_group_check=True)

    def chunk(c):
        return ring[:, (c % RING) * CH:(c % RING + 1) * CH]

    slot_free = [None] * SLOTS
    plan = []
    ready = []
    count = [0]

    def split_next():
        item = plan.pop(0)
        if item[0] == "a":
            ada_chunk(*item[1:])
            return
        _, c, lo, n, frees = item
        s_ = count[0] % SLOTS
        count[0] += 1
        hi, lw = WH[:, s_ * HALF:s_ * HALF + n], WL[:, s_ * HALF:s_ * HALF + n]
        raw = chunk(c)[:, lo:lo + n]
        wait_chunk("act", c)
        a = A(hi, raw, ACT.Copy, w=[slot_free[s_]])
        v = V(vv.tensor_tensor, lw, raw, hi.bitcast(F32), ALU.subtract, w=[a], frees=c if frees else None)
        ready.append((s_, v))

    def weights(c, n=HALF):
        return [("w", c, 0, n, False), ("w", c, n, n, True)]

    def take():
        while len(ready) < SLOTS and any(item[0] == "w" for item in plan):
            split_next()
        s_, v = ready.pop(0)
        wait("pe", v)
        return s_

    def used(s_, ins):
        slot_free[s_] = done("pe", ins)
        return slot_free[s_]

    def part(s_, lo, n=P, p=P):
        a = s_ * HALF + lo
        return WH[0:p, a:a + n], WL[0:p, a:a + n]

    def mm3(out, l, r, start, stop):
        mm(out, l[0], r[0], start, False)
        mm(out, l[0], r[1], False, False)
        return mm(out, l[1], r[0], False, stop)

    def split_act(hi, lo, src, w=()):
        a = A(hi, src, ACT.Copy, w=w)
        return V(vv.tensor_tensor, lo, src, hi.bitcast(F32), ALU.subtract, w=[a])

    both = lambda pair, *ix: (pair[0][ix], pair[1][ix])

    def all_wait():
        toks = {n: last(n) for n in q.eng}
        for n in q.eng:
            wait(n, *[t for m, t in toks.items() if m != n])

    sp = nc.sync
    turns = N_CHUNKS // RING

    def fetch(c, j):
        src = stream[c] if isinstance(c, int) else stream[bass.ds(c, 1)].rearrange("a p n -> (a p) n")
        sp.dma_start(ring[:, j * CH:(j + 1) * CH], src).then_inc(q.arrived[j], 16)

    for j in range(RING):
        fetch(j, j)
    with sp.Fori(1, turns) as i:
        for j in range(RING):
            sp.wait_ge(q.freed[j], i)
            fetch(i * RING + j, j)
    for j in range(N_CHUNKS - turns * RING):
        sp.wait_ge(q.freed[j], turns)
        fetch(turns * RING + j, j)

    s_c, s_par, s_x, s_att, s_rnn = (nc.alloc_semaphore(n) for n in ("s_c", "s_par", "s_x", "s_att", "s_rnn"))
    nc.scalar.dma_start(CB[:, 0, :], cvec[0:1, :].broadcast_to([P, D])).then_inc(s_c, 16)
    nc.scalar.dma_start(PAR, par).then_inc(s_par, 16)
    nc.scalar.dma_start(X, xT).then_inc(s_x, 16)
    A(CB[:, 0, :], CB[:, 0, :], ACT.Silu, w=[Tok(s_c, 16, 0, None)])
    silu_c = last("act")
    nc.scalar.dma_start(TAB, tab).then_inc(s_att, 16)
    nc.scalar.dma_start(ident, ident_d).then_inc(s_att, 16)
    nc.scalar.dma_start(RPAR, rpar).then_inc(s_rnn, 16)
    nc.scalar.dma_start(CB[:, 1, :], cvec[1:2, :].broadcast_to([P, D])).then_inc(s_rnn, 16)
    G(nc.gpsimd.memset, ONES, 1.0)
    wait("pe", last("pool"))
    wait("dve", silu_c, Tok(s_par, 16, 0, None))
    wait("act", Tok(s_par, 16, 0, None))

    JUNK = view(aT2, 1024)

    def ada_chunk(c, col, conds=((0, 0),), junk=None):
        wait_chunk("dve", c)
        junk = JUNK if junk is None else junk
        for j in range(2):
            for n, (v, off) in enumerate(conds):
                src = chunk(c)[:, j * D:(j + 1) * D]
                acc = MOD[:, col + off + j:col + off + j + 1] if q.loop is None else MISC[:, 2 * n + j:2 * n + j + 1]
                V(vv.tensor_tensor_reduce, junk, src, CB[:, v, :], 1.0, 0.0, ALU.mult, ALU.add, acc,
                  frees=c if j == 1 and n == len(conds) - 1 else None)
        if q.loop is not None:
            for n, (v, off) in enumerate(conds):
                V(vv.tensor_copy, MOD[:, bass.ds(q.loop.reg * 4 + (col + off), 2)], MISC[:, 2 * n:2 * n + 2])

    def ada_bias(a, n, name, j):
        V(vv.tensor_tensor, MOD[:, a:a + n], MOD[:, a:a + n], par_(name, j, n), ALU.add)

    c_now = 0
    for j in range(8):
        ada_chunk(c_now, 2 * j)
        c_now += 1
    ada_bias(0, 16, "ada_b", 0)

    XC, SQ = T1, T2
    MEAN, VAR = PS[:, 0, 0:256], PS[:, 1, 0:256]
    RSTD = RS[:, 0:256]
    combo = MISC[:, 16:80]

    def modulated(src, scale, shift, s_=0, w=()):
        his, toks = [], []
        for k in range(0, KT, 2):
            for kk in (k, k + 1):
                v = V(vv.tensor_scalar, T2[:, kk, :], src[:, kk, :], scale[:, kk:kk + 1], shift[:, kk:kk + 1], ALU.mult, ALU.add, w=w)
            his.append(A(XH[:, s_, k:k + 2, :], T2[:, k:k + 2, :], ACT.Copy, w=[v]))
        for n, a in enumerate(his):
            k = 2 * n
            toks += [V(vv.tensor_tensor, XL[:, s_, k:k + 2, :], T2[:, k:k + 2, :], XH[:, s_, k:k + 2, :].bitcast(F32), ALU.subtract, w=[a])] * 2
        return toks

    def add_branch(n, y, g, tok):
        return V(vv.scalar_tensor_tensor, X[:, n, :], y, g, X[:, n, :], ALU.mult, ALU.add, w=[tok])

    def column_sums(bank, src, toks, half=None):
        for k in range(KT):
            wait("pe", toks[k])
            ins = mm(bank, ONES, src[:, k, :], k == 0, k == KT - 1)
        return done("pe", ins)

    def root(dst, src, scale, eps, w):
        A(dst, src, ACT.Sqrt, w=w, scale=scale, bias=eps)
        return V(vv.reciprocal, dst, dst, w=[last("act")])

    def layer_norm(ln, toks, scale_col, shift_col, nxt_alpha, into_xin):
        lg, lb_ = par_("ln_g", 8 * ln, 8), par_("ln_b", 8 * ln, 8)
        pe = column_sums(MEAN, X, toks)
        mean = RS[:, 256:512]
        V(vv.tensor_scalar, mean, MEAN, 1.0 / D, None, ALU.mult, w=[pe])
        sq = []
        for h in range(2):
            v = V(vv.tensor_tensor, XC[:, 4 * h:4 * h + 4, :], X[:, 4 * h:4 * h + 4, :],
                  mean.unsqueeze(1).broadcast_to([P, 4, S]), ALU.subtract)
            sq += [A(SQ[:, 4 * h:4 * h + 4, :], XC[:, 4 * h:4 * h + 4, :], ACT.Square, w=[v])] * 4
        ga, ba = combo[:, 8:16], combo[:, 16:24]
        V(vv.tensor_scalar, ga, lg, nxt_alpha, None, ALU.mult)
        V(vv.tensor_scalar, ba, lb_, nxt_alpha, None, ALU.mult)
        gm, bm = combo[:, 24:32], combo[:, 32:40]
        if into_xin:
            V(vv.tensor_scalar, combo[:, 40:48], scale_col, 1.0, None, ALU.add)
            V(vv.tensor_tensor, gm, lg, combo[:, 40:48], ALU.mult)
            V(vv.tensor_tensor, bm, lb_, combo[:, 40:48], ALU.mult)
            V(vv.tensor_tensor, bm, bm, shift_col, ALU.add)
        pe = column_sums(VAR, SQ, sq)
        v = root(RSTD, VAR, 1.0 / D, par_("eps5"), [pe])
        out, xs = [], []
        for h in range(2):
            V(vv.tensor_tensor, XC[:, 4 * h:4 * h + 4, :], XC[:, 4 * h:4 * h + 4, :],
              RSTD.unsqueeze(1).broadcast_to([P, 4, S]), ALU.mult)
        if into_xin:
            out = modulated(XC, gm, bm)
        for k in range(KT):
            xs.append(V(vv.tensor_scalar, X[:, k, :], XC[:, k, :], ga[:, k:k + 1], ba[:, k:k + 1], ALU.mult, ALU.add))
        return out, xs

    V(vv.tensor_scalar, combo[:, 0:8], MOD[:, 8:16], 1.0, None, ALU.add)
    htok = modulated(X, combo[:, 0:8], MOD[:, 0:8], w=[Tok(s_x, 16, 0, None)])
    V(vv.tensor_scalar, X[:, :, :], X[:, :, :], ALPHA, None, ALU.mult)
    wait("pe", Tok(s_att, 32, 0, None))
    wait("dve", Tok(s_att, 32, 0, None))
    a0 = aB + 1056
    QK = kt(view(a0, 2560), 10)
    VT = view(a0 + 2560, 512).rearrange("p (b n) -> p b n", b=2)
    SC = view(a0 + 3072, 2048).rearrange("p (a h k) -> p a h k", a=2, h=4)
    PT = view(a0 + 5120, 2048).rearrange("p (a h k q) -> p a h k q", a=2, h=4, k=2)
    OT = kt(view(a0 + 7168, 2048))
    OTS = (kt(rounded("o_high", a0 + 9216, 2048)), kt(rounded("o_low", a0 + 11264, 2048)))
    RT = view(a0 + 13312, 512, 32)
    free = [None] * 8
    qk_t = [None] * 10
    for n in range(6):
        plan += weights(c_now + n)
    c_now += 6
    for j in range(4):
        plan.append(("a", c_now + j, 16 + 2 * j))
    c_now += 4

    def out_tile(out, src, htok=None):
        s_ = take()
        for k in range(KT):
            if htok is not None:
                wait("pe", htok[k])
            ins = mm3(out, part(s_, k * P), both(src, slice(None), k), k == 0, k == KT - 1)
        return used(s_, ins)

    for n2 in range(5):
        bank = n2 % 2
        wait("pe", free[bank])
        for j in range(2):
            pe = out_tile(PS[:, bank, j * 256:(j + 1) * 256], XIN, htok if n2 == 0 and j == 0 else None)
        free[bank] = A(QK[:, 2 * n2:2 * n2 + 2, :], PS[:, bank, :].rearrange("p (n t) -> p n t", n=2), ACT.Copy, w=[pe])
        wait("pe", free[bank], free[2 + bank])
        pe = done("pe", mm(PS[0:32, 2 + bank, :], tab_("roper", 32), QK[0:32, 2 * n2:2 * n2 + 2, :], True, True))
        sin = tab_("ropes", 32).unsqueeze(1).broadcast_to([32, 2, S])
        cos = tab_("ropec", 32).unsqueeze(1).broadcast_to([32, 2, S])
        rt = RT.rearrange("p (n t) -> p n t", n=2)
        free[2 + bank] = V(vv.tensor_tensor, rt, PS[0:32, 2 + bank, :].rearrange("p (n t) -> p n t", n=2), sin, ALU.mult, w=[pe])
        V(vv.tensor_tensor, QK[0:32, 2 * n2:2 * n2 + 2, :], QK[0:32, 2 * n2:2 * n2 + 2, :], cos, ALU.mult)
        qk_t[2 * n2] = qk_t[2 * n2 + 1] = V(vv.tensor_tensor, QK[0:32, 2 * n2:2 * n2 + 2, :], QK[0:32, 2 * n2:2 * n2 + 2, :], rt, ALU.add)
    wait("pe", free[0], free[1])
    for half in range(2):
        s_ = take()
        for b in range(2):
            for k in range(4):
                kk = 4 * half + k
                ins = mm3(PS[:, b, 0:256], both(XIN, slice(None), kk, slice(b * P, (b + 1) * P)), part(s_, k * 256, 256), kk == 0, kk == KT - 1)
        pe = used(s_, ins)
    v_t = free[0] = free[1] = A(VT, PS[:, 0:2, 0:256], ACT.Copy, w=[pe])
    SM = MISC[:, 128:256]

    def scores(n, g, b):
        a = n % 2
        sm = SM[:, 32 * n:32 * n + 32]
        wait("pe", free[4], free[5], *qk_t)
        for h in range(4):
            ins = mm(PS[:, 4 + h // 2, (h % 2) * 256:(h % 2 + 1) * 256], QK[:, 4 * g + h, b * P:(b + 1) * P], QK[:, 8 + g, :], True, True)
        pe = done("pe", ins)
        mask = tab_("amask")[:, b * 256:(b + 1) * 256].unsqueeze(1).broadcast_to([P, 4, S])
        free[4] = free[5] = V(vv.scalar_tensor_tensor, SC[:, a, :, :], PS[:, 4:6, :].rearrange("p b (h k) -> p (b h) k", h=2), P ** -0.5, mask,
                              ALU.mult, ALU.add, w=[pe, sc_free[a]])
        V(vv.tensor_reduce, sm[:, 0:4], SC[:, a, :, :], AX, ALU.max)
        V(vv.tensor_tensor, sm[:, 0:4], sm[:, 0:4], par_("sinks", 4 * g, 4), ALU.max)
        V(vv.tensor_tensor, sm[:, 4:8], par_("sinks", 4 * g, 4), sm[:, 0:4], ALU.subtract)
        v = V(vv.tensor_scalar, sm[:, 8:12], sm[:, 0:4], -1.0, None, ALU.mult)
        A(sm[:, 12:16], sm[:, 4:8], ACT.Exp, w=[v])
        for h in range(4):
            e = A(SC[:, a, h, :], SC[:, a, h, :], ACT.Exp, bias=sm[:, 8 + h:9 + h], accum_out=sm[:, 16 + h:17 + h])
        return e

    def attend(n, g, b, e):
        a = n % 2
        sm = SM[:, 32 * n:32 * n + 32]
        V(vv.tensor_tensor, sm[:, 16:20], sm[:, 16:20], sm[:, 12:16], ALU.add, w=[e])
        V(vv.reciprocal, sm[:, 20:24], sm[:, 16:20])
        p_t = V(vv.tensor_tensor, SC[:, a, :, :], SC[:, a, :, :], sm[:, 20:24].unsqueeze(2).broadcast_to([P, 4, S]), ALU.mult)
        wait("pe", p_t, free[6], free[7])
        for h in range(4):
            for kb in range(2):
                ins = nc.tensor.transpose(PS[:, 6 + h // 2, (h % 2) * 256 + kb * P:(h % 2) * 256 + (kb + 1) * P], SC[:, a, h, kb * P:(kb + 1) * P], ident)
        pe = done("pe", ins)
        sc_free[a] = pe
        free[6] = free[7] = A(PT[:, a, :, :, :], PS[:, 6:8, :].rearrange("p b (h k q) -> p (b h) k q", h=2, k=2), ACT.Copy, w=[pe, pt_free[a]])
        wait("pe", free[7], v_t, free[n])
        for h in range(4):
            for kb in range(2):
                ins = mm(PS[:, n, h * P:(h + 1) * P], VT[:, kb, g * P:(g + 1) * P], PT[:, a, h, kb, :], kb == 0, kb == 1)
        pe = done("pe", ins)
        pt_free[a] = pe
        free[n] = A(OT[:, 4 * g:4 * g + 4, b * P:(b + 1) * P], PS[:, n, :].rearrange("p (h q) -> p h q", h=4), ACT.Copy, w=[pe])

    sc_free, pt_free = [None, None], [None, None]
    for j in range(8):
        plan.append(("a", c_now + j, 24 + 2 * j))
    c_now += 8
    batches = ((0, 0), (0, 1), (1, 0), (1, 1))
    e_t = [scores(0, *batches[0]), None, None, None]
    for n in range(4):
        if n < 3:
            e_t[n + 1] = scores(n + 1, *batches[n + 1])
        attend(n, *batches[n], e_t[n])
        if n % 2:
            g = batches[n][0]
            o_t = split_act(OTS[0][:, 4 * g:4 * g + 4, :], OTS[1][:, 4 * g:4 * g + 4, :], OT[:, 4 * g:4 * g + 4, :], w=[free[n]])
        for _ in range(3):
            split_next()

    def project(c0, src, src_tok, gcols):
        toks = []
        wait("pe", src_tok)
        for n2 in range(4):
            bank = 4 + n2
            wait("pe", free[bank])
            for j in range(2):
                pe = out_tile(PS[:, bank, j * 256:(j + 1) * 256], src)
            for j in range(2):
                toks.append(add_branch(2 * n2 + j, PS[:, bank, j * 256:(j + 1) * 256], gcols[:, 2 * n2 + j:2 * n2 + j + 1], pe))
            free[bank] = toks[-1]
        return toks

    for n in range(4):
        plan += weights(c_now + n)
    ada_bias(16, 24, "ada_b", 16)
    G1 = MISC[:, 96:104]
    V(vv.tensor_scalar, G1, MOD[:, 16:24], 1.0, None, ALU.add)
    xt = project(c_now, OTS, o_t, G1)
    c_now += 4
    layer_norm(0, xt, MOD[:, 32:40], MOD[:, 24:32], ALPHA, True)
    for j in range(4):
        ada_chunk(c_now, 40 + 2 * j, junk=view(aT2, 1024))
        c_now += 1
    ada_bias(40, 8, "ada_b", 40)

    def clear_sums():
        V(vv.memset, RS[0:1, :], 0.0)
        wait("pe", last("dve"), last("act"))
        for b in range(4):
            ins = mm(PS[:, 4 + b, :], RS[0:1, 0:P], RS[0:1, :], True, False)
        return done("pe", ins)

    H1 = tuple(rounded("h1_" + n, aB + m * 1024, 1024).rearrange("p (a n) -> p a n", a=2) for m, n in enumerate(("high", "low")))
    R1 = view(aB + 2048, 1024).rearrange("p (a n) -> p a n", a=2)
    R2 = view(aB + 3072, 1024).rearrange("p (a n) -> p a n", a=2)

    def second_product(src_half, s_):
        for m in range(KT):
            ins = mm3(PS[:, 4 + m // 2, (m % 2) * 256:(m % 2 + 1) * 256], part(s_, m * P), src_half, False, False)
        return used(s_, ins)

    def mlp(c0, turns, ada_col, conds):
        halves = 8

        def body(i):
            before = {n: last(n) for n in q.eng}
            q.slots_of_turn_before(slot_free, count[0], halves)
            plan.extend(weights(c0) + weights(c0 + 1) + weights(c0 + 2) + [("a", c0 + 3, ada_col, conds, view(aB + 4096, 1024))]
                        + weights(c0 + 4) + [("a", c0 + 5, ada_col + 2, conds, view(aB + 4096, 1024))])
            h_t = [None, None]
            for a in range(2):
                wait("pe", before["act"])
                for j in range(2):
                    pe = out_tile(PS[:, a, j * 256:(j + 1) * 256], XIN)
                r = A(R1[:, a, :], PS[:, a, :], ACT.Relu, w=[pe, before["dve"]])
                v = V(vv.tensor_tensor, R2[:, a, :], R1[:, a, :], R1[:, a, :], ALU.mult, w=[r, before["act"]])
                h_t[a] = split_act(H1[0][:, a, :], H1[1][:, a, :], R2[:, a, :], w=[v, before["pe"]])
            for a in range(2):
                wait("pe", h_t[a])
                for j in range(2):
                    s_ = take()
                    second_product(both(H1, slice(None), a, slice(j * 256, (j + 1) * 256)), s_)
            while plan:
                split_next()

        q.run_loop(turns, {"pe": halves, "dve": 6 + 6 * len(conds), "act": 12, "pool": 0}, body)
        q.slots_of_turn_before(slot_free, count[0], halves)
        return c0 + 6 * turns

    clear_sums()
    all_wait()
    c_now = mlp(c_now, 8, 48, ((0, 0),))
    V(vv.tensor_scalar, G1, MOD[:, 40:48], 1.0, None, ALU.add)
    ada_bias(48, 32, "ada_b", 48)

    def evacuate(gcols):
        pe = last("pe")
        return [add_branch(n, PS[:, 4 + n // 2, (n % 2) * 256:(n % 2 + 1) * 256], gcols[:, n:n + 1], pe) for n in range(KT)]

    xt = evacuate(G1)
    out, xs = layer_norm(1, xt, MOD[:, 56:64], MOD[:, 48:56], ALPHA, True)

    all_wait()
    rp = lambda n, j, k=1: RPAR[:, RCOL[n][0] + j:RCOL[n][0] + j + k]
    RM = view(aM + 128, 256, BW)
    cs, hba, hbx = RM[:, 0:32], RM[:, 32:64], RM[:, 64:96]
    t0, t1, t2, cs2 = RM[:, 96:128], RM[:, 128:160], RM[:, 160:192], RM[:, 192:224]
    wait("dve", Tok(s_rnn, 32, 0, None))
    silu_c2 = A(CB[:, 1, :], CB[:, 1, :], ACT.Silu, w=[Tok(s_rnn, 32, 0, None)])
    lam = rp("lam", 0, 32)
    V(vv.tensor_scalar, t0, lam, -1.0, None, ALU.mult)
    V(vv.tensor_tensor, t1, t0, lam, ALU.min)
    A(t1, t1, ACT.Exp, w=[last("dve")])
    V(vv.tensor_scalar, t2, t1, 2.0, None, ALU.add, w=[last("act")])
    V(vv.reciprocal, t2, t2)
    V(vv.tensor_tensor, t1, t1, t2, ALU.mult)
    V(vv.tensor_tensor, t2, t1, t1, ALU.mult)
    V(vv.tensor_scalar, cs, t2, 1.0 / 17, None, ALU.mult)
    for d in (15, 13, 11, 9, 7, 5, 3):
        V(vv.scalar_tensor_tensor, cs, cs, 1.0 / d, t2, ALU.add, ALU.mult)
    V(vv.scalar_tensor_tensor, cs, cs, 1.0, t1, ALU.add, ALU.mult)
    V(vv.tensor_scalar, cs, cs, 4.0, None, ALU.mult)
    V(vv.tensor_scalar, t0, t0, 0.0, 2.0, ALU.max, ALU.mult)
    V(vv.tensor_tensor, cs, cs, t0, ALU.add)
    V(vv.tensor_scalar, hba, rp("ba", 0, 32), 0.5, None, ALU.mult)
    V(vv.tensor_scalar, hbx, rp("bx", 0, 32), 0.5, None, ALU.mult)
    V(vv.tensor_scalar, cs2, cs, -2.0, None, ALU.mult)
    pbt = lambda a, n, k: view(a, n, BW).rearrange("p (b t) -> p b t", b=k)
    pajdt = lambda a: view(a, 2048, BW).rearrange("p (a j d t) -> p a j d t", a=2, j=2, d=2)
    padt = lambda a: view(a, 1024, BW).rearrange("p (a d t) -> p a d t", a=2, d=2)
    GT, Y = pbt(aB, 4096, NB), pbt(aT1, 4096, NB)
    TLb, W2b, AAb = pajdt(aB + 4096), pajdt(aB + 6144), pajdt(aB + 8192)
    TAb, TIb, HSC = padt(aX + 2048), padt(aX + 3072), padt(aB + 10240)
    XP = view(aXL + 2048, 520, BW).rearrange("p (a t) -> p a t", a=2)
    XCV = pbt(aXL + 2048 + 520, 1024, 4)
    GW = view(aB + 11264, NB * 4 * BW, BW).rearrange("p (b n) -> p b n", b=NB)
    nc.scalar.dma_start(GW, gw).then_inc(s_rnn, 16)
    V(vv.memset, XP[:, :, 0:2], 0.0)
    V(vv.memset, XP[:, :, 258:260], 0.0)
    wait("pe", Tok(s_rnn, 48, 0, None))
    free = [None] * 8
    xcv_t, xcv_read = {}, {}
    w_read = [None, None]

    def z_of(b):
        bank = b % 2
        wait("pe", free[bank])
        for j in range(2):
            s_ = take()
            for k in range(KT):
                wait("pe", out[k]) if b == 0 and j == 0 else None
                ins = mm3(PS[0:BW, bank, j * 256:(j + 1) * 256], part(s_, k * BW, BW), both(XIN, slice(None), k), k == 0, k == KT - 1)
            pe = used(s_, ins)
        a1 = A(XP[:, bank, 2:258], PS[0:BW, bank, 0:256], ACT.Copy, w=[pe, xcv_t.get(b - 2)])
        free[bank] = A(GT[:, b, :], PS[0:BW, bank, 256:512], ACT.Copy)
        xc = XCV[:, b % 4, :]
        V(vv.tensor_scalar, xc, XP[:, bank, 0:256], rp("cw", b), rp("cb", b), ALU.mult, ALU.add, w=[a1, xcv_read.get(b - 4)])
        for j in range(1, 4):
            V(vv.scalar_tensor_tensor, xc, XP[:, bank, j:j + 256], rp("cw", 16 * j + b), xc, ALU.mult, ALU.add)
        xcv_t[b] = last("dve")

    grp_tok = {}

    def gates_of(b):
        g, j = (b // 2) % 2, b % 2
        gb = 2 + 2 * (b % 2)
        wait("pe", xcv_t[b], free[gb], free[gb + 1])
        for d in range(2):
            for m in range(2):
                o = (2 * d + m) * BW
                ins = mm(PS[0:BW, gb + d, m * 256:(m + 1) * 256], GW[:, b, o:o + BW], XCV[:, b % 4, :], True, True)
        pe = done("pe", ins)
        s = b % 2
        for d in range(2):
            cc = 16 * d + b
            A(TAb[:, s, d, :], PS[0:BW, gb + d, 0:256], ACT.Tanh, scale=0.5, bias=hba[:, cc:cc + 1], w=[pe])
            A(TIb[:, s, d, :], PS[0:BW, gb + d, 256:512], ACT.Tanh, scale=0.5, bias=hbx[:, cc:cc + 1], w=[w_read[s]])
            free[gb + d] = last("act")
            A(TLb[:, g, j, d, :], TAb[:, s, d, :], ACT.Tanh, scale=cs[:, cc:cc + 1], bias=cs[:, cc:cc + 1], w=[grp_tok.get(b // 2 - 2)])
            A(AAb[:, g, j, d, :], TAb[:, s, d, :], ACT.Exp, scale=cs2[:, cc:cc + 1], bias=cs2[:, cc:cc + 1])
        a = last("act")
        AA, W2 = AAb[:, g, j, :, :], W2b[:, g, j, :, :]
        w_read[s] = V(vv.scalar_tensor_tensor, W2, TIb[:, s, :, :], 1.0, XCV[:, b % 4, :].unsqueeze(1).broadcast_to([BW, 2, S]), ALU.add, ALU.mult, w=[a])
        V(vv.scalar_tensor_tensor, W2, AA, 1.0, W2, ALU.add, ALU.mult)
        xcv_read[b] = last("dve")

    hsc_free = [None, None]

    def scan_pair(gi):
        g = gi % 2
        a = A(TLb[:, g, :, :, :], TLb[:, g, :, :, :], ACT.Sqrt, scale=0.25, w=[last("dve")])
        V(vv.tensor_tensor, W2b[:, g, :, :, :], W2b[:, g, :, :, :], TLb[:, g, :, :, :], ALU.mult, w=[a])
        for j in range(2):
            b = 2 * gi + j
            V(vv.tensor_tensor_scan, HSC[:, j, 0, :], AAb[:, g, j, 0, :], W2b[:, g, j, 0, :], 0.0, ALU.mult, ALU.add, w=[hsc_free[j]])
            V(vv.tensor_tensor_scan, HSC[:, j, 1, ::-1], AAb[:, g, j, 1, ::-1], W2b[:, g, j, 1, ::-1], 0.0, ALU.mult, ALU.add)
            hsc_free[j] = G(nc.gpsimd.tensor_tensor, Y[:, b, :], HSC[:, j, 0, :], HSC[:, j, 1, :], ALU.add, w=[last("dve")])
        grp_tok[gi] = last("dve")

    pj = PS[:, 6:8, :].rearrange("p b n -> p (b n)")
    for b in range(NB):
        plan += weights(c_now + 2 * b, KT * BW)
        plan.append(("a", c_now + 2 * b + 1, 80 + 2 * b if b < 8 else 112 + 2 * b, (((0 if b < 8 else 1), 0),), pj))
    c_now += 2 * NB
    wait("dve", silu_c2)
    z_of(0)
    for b in range(NB):
        if b + 1 < NB:
            z_of(b + 1)
        gates_of(b)
        if b % 2 == 1 and b >= 3:
            scan_pair(b // 2 - 1)
    while plan:
        split_next()
    scan_pair(NB // 2 - 1)

    s_late = nc.alloc_semaphore("s_late")
    clear_sums()
    for n in range(8):
        plan += weights(c_now + n)
    c_now += 8
    YS_ = (rounded("y_high", aB + 4096, 4096, BW).rearrange("p (b t) -> p b t", b=NB),
           rounded("y_low", aB + 11264, 4096, BW).rearrange("p (b t) -> p b t", b=NB))
    all_wait()
    for b4 in range(4):
        bs = slice(4 * b4, 4 * b4 + 4)
        a = A(GT[:, bs, :], GT[:, bs, :], ACT.Gelu_apprx_tanh)
        v = V(vv.tensor_tensor, Y[:, bs, :], Y[:, bs, :], GT[:, bs, :], ALU.mult, w=[a])
        y_t = split_act(YS_[0][:, bs, :], YS_[1][:, bs, :], Y[:, bs, :], w=[v])
        for b in range(4 * b4, 4 * b4 + 4):
            s_ = take()
            wait("pe", y_t)
            for m in range(KT):
                ins = mm3(PS[:, 4 + m // 2, (m % 2) * 256:(m % 2 + 1) * 256], part(s_, m * P, P, BW), both(YS_, slice(None), b), False, False)
            used(s_, ins)
    ada_bias(80, 16, "ada_b", 80)
    ada_bias(128, 16, "ada_b2", 32)
    V(vv.tensor_scalar, G1, MOD[:, 64:72], 1.0, None, ALU.add)
    xt = evacuate(G1)
    layer_norm(2, xt, MOD[:, 80:88], MOD[:, 72:80], ALPHA, True)

    all_wait()
    POS, CTX = kt(view(aB + 8192, 2048)), kt(view(aB + 10240, 2048))
    nc.scalar.dma_start(CB[:, 0, :], cvec[2:3, :].broadcast_to([P, D])).then_inc(s_late, 16)
    nc.scalar.dma_start(CTX, ctxT).then_inc(s_late, 16)
    nc.scalar.dma_start(POS, posT).then_inc(s_late, 16)
    nc.scalar.dma_start(TAB2, tab2).then_inc(s_late, 16)
    LATE = Tok(s_late, 64, 0, None)
    A(CB[:, 0, :], CB[:, 0, :], ACT.Silu, w=[LATE])

    def rms_rows(src, w, xnorm, n=KT, m=D, sq=None):
        sq = T2 if sq is None else sq
        a = A(sq[:, 0:n, :], src, ACT.Square, w=w)
        wait("pe", a)
        for k in range(n):
            ins = mm(VAR, ONES, sq[:, k, :], k == 0, k == n - 1)
        pe = done("pe", ins)
        root(RSTD, VAR, 1.0 / m, par_("eps6"), [pe])
        return V(vv.tensor_tensor, xnorm, src, RSTD.unsqueeze(1).broadcast_to([P, n, S]), ALU.mult)

    rms_rows(CTX, [LATE], CTX)
    clear_sums()
    all_wait()
    c_now = mlp(c_now, 4, 96, ((1, 0), (0, 48)))
    c_now = mlp(c_now, 4, 112, ((1, 0),))
    V(vv.tensor_scalar, G1, MOD[:, 88:96], 1.0, None, ALU.add)
    ada_bias(96, 32, "ada_b2", 0)
    ada_bias(144, 16, "ada_b2", 0)
    xt = evacuate(G1)
    layer_norm(3, xt, None, None, 1.0, False)

    wait("dve", LATE)
    for k in range(KT):
        v = V(vv.tensor_tensor, X[:, k, :], X[:, k, :], POS[:, k, :], ALU.add)
    sc2 = combo[:, 0:8]

    def modulate_norm(xnorm, gname, shift, scale, s_=0):
        V(vv.tensor_scalar, sc2, MOD[:, scale:scale + 8], 1.0, None, ALU.add)
        V(vv.tensor_tensor, sc2, sc2, par_(gname, 0, 8), ALU.mult)
        return modulated(xnorm, sc2, MOD[:, shift:shift + 8], s_)

    modulate_norm(CTX, "n1g", 144, 152, 1)
    wait("act", last("dve"))
    rms_rows(X[:, :, :], [v], XC[:, :, :])
    htok = modulate_norm(XC, "n1g", 96, 104, 0)
    all_wait()
    Fg = view(aB, 4096).rearrange("p (n t) -> p n t", n=8)
    Vv = view(aB + 4096, 2048).rearrange("p (b n) -> p b n", b=4)
    ZP = view(aB + 6144, 1548).rearrange("p (n t) -> p n t", n=6)
    Q = view(aC, 1024)
    FZ = view(aC + 1024, 512).rearrange("p (n t) -> p n t", n=2)
    Gg = view(aT2 + 1024, 1024)
    SG = view(aB + 10240, 1024).rearrange("p (a n) -> p a n", a=2)
    V(vv.memset, ZP[:, :, 0:1], 0.0)
    V(vv.memset, ZP[:, :, 257:258], 0.0)
    for n in range(14):
        plan += weights(c_now + n)
    c_now += 14
    LB = MISC[:, 128:152]
    lbr = par_("lb", 0, 8)
    V(vv.tensor_tensor, LB[:, 0:8], lbr, lbr, ALU.subtract)
    A(LB[:, 0:8], LB[:, 0:8], ACT.Exp, w=[last("dve")])
    V(vv.reciprocal, LB[:, 8:16], LB[:, 0:8], w=[last("act")])
    V(vv.tensor_tensor, LB[:, 0:8], LB[:, 0:8], LB[:, 8:16], ALU.mult)
    V(vv.tensor_tensor, LB[:, 0:8], LB[:, 0:8], LB[:, 0:8], ALU.subtract)
    V(vv.tensor_scalar, LB[:, 8:16], LB[:, 0:8], -1.0, 1.0, ALU.mult, ALU.add)
    free = [None] * 8
    for t in range(8):
        bank = t % 4
        wait("pe", free[bank])
        s_ = take()
        for k in range(KT):
            ins = mm3(PS[:, bank, :].rearrange("p (s t) -> p s t", s=2), part(s_, k * P), (XH[:, :, k, :], XL[:, :, k, :]), k == 0, k == KT - 1)
        pe = used(s_, ins)
        free[bank] = A(Fg[:, t, :], PS[:, bank, :], ACT.Sigmoid, w=[pe])
        V(vv.tensor_scalar, Fg[:, t, :], Fg[:, t, :], LB[:, 8 + t:9 + t], LB[:, t:t + 1], ALU.mult, ALU.add, w=[free[bank]])
    for half in range(4):
        s_ = take()
        for b in range(4):
            for k in range(2):
                kk = 2 * half + k
                x_ = tuple(t[:, b // 2, kk, (b % 2) * P:(b % 2 + 1) * P] for t in (XH, XL))
                ins = mm3(PS[:, 4 + b, :], x_, part(s_, k * 512, 512), kk == 0, kk == KT - 1)
        pe = used(s_, ins)
    for b in range(4):
        free[4 + b] = A(Vv[:, b, :], PS[:, 4 + b, :], ACT.Copy, w=[pe])

    def in_tiles(bank):
        wait("pe", free[bank])
        for j in range(2):
            pe = out_tile(PS[:, bank, j * 256:(j + 1) * 256], XIN)
        return pe

    for n in range(2):
        pe = in_tiles(n)
        a = A(SG[:, n, :], PS[:, n, :], ACT.Sigmoid, w=[pe])
        free[n] = q_t = V(vv.scalar_tensor_tensor, Q[:, n * 512:(n + 1) * 512], PS[:, n, :], P ** -0.5, SG[:, n, :], ALU.mult, ALU.mult, w=[a])
    for n in range(3):
        pe = in_tiles(2 + n % 2)
        free[2 + n % 2] = A(ZP[:, 2 * n:2 * n + 2, 1:257], PS[:, 2 + n % 2, :].rearrange("p (n t) -> p n t", n=2), ACT.Copy, w=[pe, last("dve")])
    for n in range(2):
        pe = in_tiles(n)
        a = A(SG[:, n, :], PS[:, n, :], ACT.Sigmoid, w=[pe, q_t])
        free[n] = V(vv.tensor_tensor, Gg[:, n * 512:(n + 1) * 512], PS[:, n, :], SG[:, n, :], ALU.mult, w=[a])
    pe = in_tiles(3)
    fz_t = free[3] = A(FZ[:, :, :], PS[:, 3, :].rearrange("p (n t) -> p n t", n=2), ACT.Copy, w=[pe])

    def sin_of(dst, ps, bcol, frcol, tmp, w):
        TP = 2 * math.pi
        HI = float(np.float32(6.28125))
        V(vv.tensor_scalar, dst, ps, bcol, frcol, ALU.add, ALU.mult, w=w)
        V(vv.tensor_scalar, tmp, dst, 1.0 / TP, 12582912.0, ALU.mult, ALU.add)
        V(vv.tensor_scalar, tmp, tmp, 12582912.0, None, ALU.subtract)
        V(vv.scalar_tensor_tensor, dst, tmp, -HI, dst, ALU.mult, ALU.add)
        V(vv.scalar_tensor_tensor, dst, tmp, -(TP - HI), dst, ALU.mult, ALU.add)
        V(vv.tensor_scalar, dst, dst, math.pi, -math.pi, ALU.min, ALU.max)
        return A(dst, dst, ACT.Sin, w=[last("dve")])

    fp = lambda n: FPAR[:, FCOL[n][0]:FCOL[n][1]]
    all_wait()
    aF = aB + 7696
    FPAR = view(aF, FN, 64)
    s_f = nc.alloc_semaphore("s_f")
    nc.scalar.dma_start(FPAR, fpar).then_inc(s_f, 16)
    wait("pe", Tok(s_f, 16, 0, None))
    wait("dve", Tok(s_f, 16, 0, None))
    h1, tmp1, h2 = view(aF + 1160, 256, 64), view(aF + 1416, 256, 64), view(aF + 1672, 256, 64)
    HS = view(aT1, 1024).rearrange("p (o b c) -> p o b c", o=2, b=2)
    HD = view(aT1 + 1024, 1024).rearrange("p (o b c) -> p o b c", o=2, b=2)
    ht = view(aF + 1928, 512)
    t = done("pe", mm(PS[0:64, 0, 0:256], fp("w1")[0:33, :], tab_("zf", 33), True, True))
    t = sin_of(h1, PS[0:64, 0, 0:256], fp("b1"), fp("fr"), tmp1, [t])
    wait("pe", t)
    t = done("pe", mm(PS[0:64, 1, 0:256], fp("w2"), h1, True, True))
    t = sin_of(h2, PS[0:64, 1, 0:256], fp("b2"), fp("fr"), tmp1, [t])
    wait("pe", t)
    for o in range(2):
        for b in range(2):
            pe = done("pe", mm(PS[:, 2 * o + b, :], h2[:, b * P:(b + 1) * P], fp("w3")[:, o * 512:(o + 1) * 512], True, True))
            V(vv.tensor_tensor, ht[:, 0:256], PS[:, 2 * o + b, 0:256], tab_("decf")[:, b * 256:(b + 1) * 256], ALU.mult, w=[pe])
            V(vv.tensor_tensor, ht[:, 256:512], PS[:, 2 * o + b, 256:512], tab_("decb")[:, b * 256:(b + 1) * 256], ALU.mult)
            V(vv.tensor_tensor, HS[:, o, b, :], ht[:, 0:256], ht[:, 256:512], ALU.add)
            V(vv.tensor_tensor, HD[:, o, b, :], ht[:, 0:256], ht[:, 256:512], ALU.subtract)
    wait("pe", last("dve"))
    KFv = KF.rearrange("p (o r f c) -> p o r f c", o=2, r=2, f=2)
    for o in range(2):
        for r, (tb_, src) in enumerate((("dc", HS), ("ds", HD))):
            for f in range(2):
                for b in range(2):
                    ins = mm(PS[:, 4 + 2 * o + r, f * 256:(f + 1) * 256],
                             tab_(tb_)[:, b * 256 + f * P:b * 256 + (f + 1) * P], src[:, o, b, :], b == 0, b == 1)
            pe = done("pe", ins)
            A(KFv[:, o, r, :, :], PS[:, 4 + 2 * o + r, :].rearrange("p (f c) -> p f c", f=2), ACT.Copy, w=[pe])

    all_wait()
    U = kt(view(aX, 1536), 6)
    VT2 = view(aX + 1536, 512).rearrange("p (b c) -> p b c", b=2)
    YS = view(aX + 2048, 1024).rearrange("p (r n) -> p r n", r=2)
    M1, M2, YV = view(aX + 3072, 512), view(aX + 3584, 512), kt(view(aX + 4096, 512), 2)
    FA = view(aX + 4608, 1024).rearrange("p (b n) -> p b n", b=2)
    FY = kt(view(aX + 5632, 512), 2)
    SQ2 = kt(view(aT2, 512), 2)
    MIX = T1
    for n in range(6):
        V(vv.tensor_scalar, U[:, n, :], ZP[:, n, 0:256], par_("hycw", n), par_("hycb", n), ALU.mult, ALU.add)
        for j in (1, 2):
            V(vv.scalar_tensor_tensor, U[:, n, :], ZP[:, n, j:j + 256], par_("hycw", 6 * j + n), U[:, n, :], ALU.mult, ALU.add)
    y_in, y_t = U[:, 0:2, :], last("dve")
    for o in range(2):
        wait("pe", y_t)
        for b in range(2):
            for n in range(2):
                ins = nc.tensor.transpose(PS[:, 0, b * 256 + n * P:b * 256 + (n + 1) * P], y_in[:, n, b * P:(b + 1) * P], ident)
        pe = done("pe", ins)
        a = A(VT2[:, :, :], PS[:, 0, :].rearrange("p (b c) -> p b c", b=2), ACT.Copy, w=[pe])
        wait("pe", a)
        for r, tb_ in enumerate(("dc", "ds")):
            for f in range(2):
                for b in range(2):
                    ins = mm(PS[:, 1 + r, f * 256:(f + 1) * 256], tab_(tb_)[:, b * 256 + f * P:b * 256 + (f + 1) * P], VT2[:, b, :], b == 0, b == 1)
        pe = done("pe", ins)
        kr, ks = KFv[:, o, 0, :, :].rearrange("p f c -> p (f c)"), KFv[:, o, 1, :, :].rearrange("p f c -> p (f c)")
        V(vv.tensor_tensor, M1, PS[:, 1, :], kr, ALU.mult, w=[pe])
        V(vv.tensor_tensor, M2, PS[:, 2, :], ks, ALU.mult)
        V(vv.tensor_tensor, YS[:, 0, :], M1, M2, ALU.subtract)
        V(vv.tensor_tensor, M1, PS[:, 1, :], ks, ALU.mult)
        V(vv.tensor_tensor, M2, PS[:, 2, :], kr, ALU.mult)
        v = V(vv.tensor_tensor, YS[:, 1, :], M1, M2, ALU.add)
        wait("pe", v)
        for n in range(2):
            for r, tb_ in enumerate(("ic", "is")):
                for f in range(2):
                    ins = mm(PS[:, 3, n * 256:(n + 1) * 256], YS[:, r, f * 256 + n * P:f * 256 + (n + 1) * P], tab_(tb_)[:, f * 256:(f + 1) * 256],
                             r == 0 and f == 0, r == 1 and f == 1)
        pe = done("pe", ins)
        for n in range(2):
            V(vv.scalar_tensor_tensor, YV[:, n, :], y_in[:, n, :], par_("hybias", 2 * o + n), PS[:, 3, n * 256:(n + 1) * 256], ALU.mult, ALU.add, w=[pe])
        y_t = V(vv.tensor_tensor, YV[:, :, :], YV[:, :, :], U[:, 2 + 2 * o:4 + 2 * o, :], ALU.mult)
        y_in = YV
    rms_rows(YV[:, :, :], [y_t], YV[:, :, :], 2, 256, SQ2)
    for n in range(2):
        V(vv.tensor_scalar, MIX[:, n, :], YV[:, n, :], par_("hyg", n), None, ALU.mult)

    wait("pe", fz_t)
    for b in range(2):
        for n in range(2):
            for r, tb_ in enumerate(("fcc", "fcs")):
                ins = mm(PS[:, 4 + r, b * 256 + n * P:b * 256 + (n + 1) * P], FZ[:, n, b * P:(b + 1) * P], tab_(tb_), True, True)
    pe = done("pe", ins)
    for r in range(2):
        a = A(FA[:, r, :], PS[:, 4 + r, :], ACT.Copy, w=[pe])
    wait("pe", a)
    for n in range(2):
        for r, tb_ in enumerate(("flc", "fls")):
            for b in range(2):
                ins = mm(PS[:, 6, n * 256:(n + 1) * 256], FA[:, r, b * 256 + n * P:b * 256 + (n + 1) * P], tab_(tb_)[:, b * 256:(b + 1) * 256],
                         r == 0 and b == 0, r == 1 and b == 1)
    pe = done("pe", ins)
    a = A(FY[:, :, :], PS[:, 6, :].rearrange("p (n t) -> p n t", n=2), ACT.Copy, w=[pe])
    wait("pe", a)
    for n in range(2):
        ins = mm(PS[:, 7, n * 256:(n + 1) * 256], par_("fnw", n * P, P), FY[:, n, :], True, True)
    pe = done("pe", ins)
    for n in range(2):
        v = V(vv.tensor_scalar, FZ[:, n, :], PS[:, 7, n * 256:(n + 1) * 256], par_("fnb", n), None, ALU.add, w=[pe])
    rms_rows(FZ[:, :, :], [v], FZ[:, :, :], 2, 256, SQ2)
    for n in range(2):
        V(vv.tensor_scalar, MIX[:, 6 + n, :], FZ[:, n, :], par_("fng", n), None, ALU.mult)

    all_wait()
    ZERO = RS[:, 256:512]
    V(vv.memset, ZERO, 0.0)
    R = view(aX, 2048).rearrange("p (n t) -> p n t", n=8)
    KC = view(aX + 2048, 2048).rearrange("p (n t) -> p n t", n=8)
    KCT = view(aX + 4096, 2048).rearrange("p (n d) -> p n d", n=16)
    ST = view(aB + 6144, 1024).rearrange("p (n v) -> p n v", n=8)
    V(vv.tensor_scalar, KC[:, :, :], Fg[:, :, S:2 * S], -1.0, 1.0, ALU.mult, ALU.add)
    for n in range(8):
        f = Fg[:, n, S:2 * S]
        if n < 4:
            V(vv.tensor_tensor_scan, R[:, n, ::-1], Fg[:, n, 2 * S - 1:S - 1:-1], ZERO, 1.0, ALU.mult, ALU.add)
        else:
            V(vv.tensor_tensor_scan, R[:, n, :], f, ZERO, 1.0, ALU.mult, ALU.add)
    V(vv.tensor_tensor, KC[:, 0:4, 0:S - 1], KC[:, 0:4, 0:S - 1], R[:, 0:4, 1:S], ALU.mult)
    v = V(vv.tensor_tensor, KC[:, 4:8, 1:S], KC[:, 4:8, 1:S], R[:, 4:8, 0:S - 1], ALU.mult)
    wait("pe", v)
    for n in range(16):
        ins = nc.tensor.transpose(PS[:, n // 4, (n % 4) * P:(n % 4 + 1) * P], KC[:, n // 2, (n % 2) * P:(n % 2 + 1) * P], ident)
    pe = done("pe", ins)
    for b in range(4):
        a = A(KCT[:, 4 * b:4 * b + 4, :], PS[:, b, :].rearrange("p (n d) -> p n d", n=4), ACT.Copy, w=[pe])
    wait("pe", a)
    for n in range(8):
        for b in range(2):
            ins = mm(PS[:, 4 + n // 4, (n % 4) * P:(n % 4 + 1) * P], KCT[:, 2 * n + b, :], Vv[:, 2 + b, (n % 4) * P:(n % 4 + 1) * P], b == 0, b == 1)
    pe = done("pe", ins)
    a = A(ST[:, :, :], PS[:, 4:6, :].rearrange("p b (n v) -> p (b n) v", n=4), ACT.Copy, w=[pe])

    KX = view(aB + 7696, 2048)
    KFx, KBx = KX[:, 0:1024], KX[:, 1024:2048]
    PF, SF, SBk, PBk = (view(aX + 1024 * j, 1024) for j in range(4))
    QP, KP = view(aX + 4096, 1024), view(aX + 5120, 1024)
    ATD = view(aB + 10240, 1024).rearrange("p (n t) -> p n t", n=8)
    ATO = view(aB + 11264, 1024).rearrange("p (n t) -> p n t", n=8)
    h4 = lambda ap: ap.rearrange("p (h t) -> p h t", h=4)
    wait("pool", last("dve"), last("act"), last("pe"))
    G(nc.gpsimd.memset, SF, 1.0)
    G(nc.gpsimd.memset, PBk, 1.0)
    A(h4(PF), Fg[:, 0:4, 0:S], ACT.Copy, w=[last("dve"), last("pe")])
    a = A(h4(SBk), Fg[:, 4:8, 0:S], ACT.Copy)
    V(vv.tensor_scalar, h4(KFx), Fg[:, 0:4, 0:S], -1.0, 1.0, ALU.mult, ALU.add, w=[last("pe"), a])
    V(vv.tensor_scalar, h4(KBx), Fg[:, 4:8, 0:S], -1.0, 1.0, ALU.mult, ALU.add, w=[last("pool")])
    halves = lambda ap, n: ap.rearrange("p (g s t) -> p g s t", s=2, t=n)
    for lev in range(9):
        pe_before = last("pe")
        if lev == 0:
            v = V(vv.tensor_tensor, KP, KFx, KBx, ALU.add, w=[pe_before])
            qp, kp_t = Q, v
        else:
            n = 1 << (lev - 1)
            l = lambda ap: halves(ap, n)[:, :, 0, :]
            r = lambda ap: halves(ap, n)[:, :, 1, :]
            G(nc.gpsimd.tensor_tensor, l(KP), l(KFx), l(SF), ALU.mult, w=[pe_before, last("dve")])
            kp_t = G(nc.gpsimd.tensor_tensor, r(KP), r(KBx), r(PBk), ALU.mult)
            V(vv.tensor_tensor, r(QP), r(Q), r(PF), ALU.mult, w=[pe_before])
            v = V(vv.tensor_tensor, l(QP), l(Q), l(SBk), ALU.mult)
            qp = QP
        wait("pe", v, kp_t)
        b0 = 2 * (lev % 2)
        for h in range(4):
            for b in range(2):
                s_b = b if lev < 8 else 1 - b
                ins = mm(PS[:, b0 + h // 2, ((h % 2) * 2 + b) * P:((h % 2) * 2 + b + 1) * P],
                         KP[:, h * S + s_b * P:h * S + (s_b + 1) * P], qp[:, h * S + b * P:h * S + (b + 1) * P], True, True)
        pe = done("pe", ins)
        if lev > 0:
            shape = [P, 1024 // (2 * n), n]
            if lev < 8:
                V(vv.tensor_tensor, l(SF), l(SF), r(PF)[:, :, n - 1:n].broadcast_to(shape), ALU.mult, w=[kp_t])
                V(vv.tensor_tensor, r(PBk), r(PBk), l(SBk)[:, :, 0:1].broadcast_to(shape), ALU.mult)
            V(vv.tensor_tensor, r(PF), r(PF), l(PF)[:, :, n - 1:n].broadcast_to(shape), ALU.mult)
            V(vv.tensor_tensor, l(SBk), l(SBk), r(SBk)[:, :, 0:1].broadcast_to(shape), ALU.mult)
        mask = tab_("lmask")[:, (lev % 8) * P:(lev % 8 + 1) * P].unsqueeze(1).broadcast_to([P, 8, P])
        data = PS[:, b0:b0 + 2, :].rearrange("p b (n t) -> p (b n) t", n=4)
        if lev == 0:
            V(vv.tensor_tensor, ATD[:, :, :], data, mask, ALU.mult, w=[pe])
        elif lev < 8:
            V(vv.copy_predicated, ATD[:, :, :], mask.bitcast(U32), data, w=[pe])
        else:
            V(vv.tensor_copy, ATO[:, :, :], data, w=[pe])
    V(vv.tensor_tensor, QP, Q, PF, ALU.mult, w=[last("pe")])
    v = V(vv.tensor_tensor, KP, Q, SBk, ALU.mult)
    wait("pe", v)
    for h in range(4):
        for b in range(2):
            o = PS[:, 4 + h // 2, ((h % 2) * 2 + b) * P:((h % 2) * 2 + b + 1) * P]
            mm(o, Vv[:, b, h * P:(h + 1) * P], ATD[:, 2 * h + b, :], True, False)
            mm(o, Vv[:, 1 - b, h * P:(h + 1) * P], ATO[:, 2 * h + b, :], False, False)
            mm(o, ST[:, h, :], QP[:, h * S + b * P:h * S + (b + 1) * P], False, False)
            ins = mm(o, ST[:, 4 + h, :], KP[:, h * S + b * P:h * S + (b + 1) * P], False, True)
    pe = done("pe", ins)
    ob = PS[:, 4:6, :].rearrange("p b n -> p (b n)")
    a = A(QP, ob, ACT.Square, w=[pe])
    V(vv.tensor_copy, KP, ob, w=[a])
    wait("pe", a)
    for h2_ in range(2):
        ins = mm(PS[:, 6 + h2_, :], ONES, QP[:, h2_ * 512:(h2_ + 1) * 512], True, True)
    pe = done("pe", ins)
    rb = PF
    root(rb, PS[:, 6:8, :].rearrange("p b n -> p (b n)"), 1.0 / P, par_("eps6"), [pe])
    V(vv.tensor_tensor, KP, KP, rb, ALU.mult)
    for h in range(4):
        v = V(vv.scalar_tensor_tensor, MIX[:, 2 + h, :], KP[:, h * S:(h + 1) * S], par_("hgg", h), Gg[:, h * S:(h + 1) * S], ALU.mult, ALU.mult)
    free = [None] * 8
    for n in range(4):
        plan += weights(c_now + n)
    c_now += 4
    m_t = split_act(XH[:, 0], XL[:, 0], MIX[:, :, :], w=[v, last("pe")])
    xt = project(c_now, XIN, m_t, MOD[:, 112:120])
    rms_rows(X[:, :, :], xt, XC[:, :, :])
    htok = modulate_norm(XC, "n2g", 120, 128, 0)
    HM = T2

    all_wait()
    COMB = view(aB, 4096).rearrange("p (e t) -> p e t", e=NE)
    SEL = view(aB + 4096, 2048, NE)
    s_sel = nc.alloc_semaphore("s_sel")
    nc.scalar.dma_start(SEL, sel).then_inc(s_sel, 16)
    for b in range(2):
        for k in range(KT):
            ins = mm(PS[:, b, 0:NE], HM[:, k, b * P:(b + 1) * P], par_("rw", k * NE, NE), k == 0, k == KT - 1)
    pe = done("pe", ins)
    ROUT = view(aB + 6144, 1024)

    def r3(j, n=16):
        return ROUT[:, 64 * j:64 * j + 2 * n].rearrange("p (b e) -> p b e", b=2)

    PR, SE, ML, EX, E2 = r3(0), r3(1), r3(2), r3(3), r3(4)
    st = ROUT[:, 512:512 + 64]
    mx = st[:, 0:2]
    V(vv.tensor_reduce, mx, PS[:, 0:2, 0:NE], AX, ALU.max, w=[pe])
    V(vv.tensor_scalar, mx, mx, -1.0, None, ALU.mult)
    for b in range(2):
        a = A(PR[:, b, :], PS[:, b, 0:NE], ACT.Exp, bias=st[:, b:b + 1], accum_out=st[:, 2 + b:3 + b], w=[last("dve")])
    V(vv.reciprocal, st[:, 4:6], st[:, 2:4], w=[a])
    V(vv.tensor_tensor, PR, PR, st[:, 4:6].unsqueeze(2).broadcast_to([P, 2, NE]), ALU.mult)
    V(vv.tensor_tensor, SE, PR, par_("rb", 0, 16).unsqueeze(1).broadcast_to([P, 2, NE]), ALU.add)
    g4 = ROUT[:, 64:64 + 32].rearrange("p (g e) -> p g e", e=4)
    GS, GT2 = ROUT[:, 320:320 + 8], ROUT[:, 352:352 + 16].rearrange("p (g e) -> p g e", e=2)
    pairs = [(g4[:, :, 0:4:2], g4[:, :, 1:4:2]), (g4[:, :, 0:2], g4[:, :, 2:4]), (g4[:, :, 0:2], g4[:, :, 3:1:-1])]
    for j, (a_, b_) in enumerate(pairs):
        V(vv.tensor_tensor, GT2, a_, b_, ALU.add)
        dst = GS if j == 0 else st[:, 8:16]
        V(vv.tensor_reduce, dst, GT2, AX, ALU.max)
        if j:
            V(vv.tensor_tensor, GS, GS, dst, ALU.max)

    def first_max(val, n, onehot, m, tmp, rows=2):
        V(vv.tensor_reduce, m, val, AX, ALU.max)
        V(vv.tensor_tensor, onehot, val, m.unsqueeze(2).broadcast_to([P, rows, n]), ALU.is_ge)
        io = tab_("iota")[:, 0:n].unsqueeze(1).broadcast_to([P, rows, n])
        V(vv.scalar_tensor_tensor, tmp, onehot, -100.0, io, ALU.mult, ALU.add)
        V(vv.tensor_reduce, m, tmp, AX, ALU.min)
        V(vv.tensor_tensor, onehot, tmp, m.unsqueeze(2).broadcast_to([P, rows, n]), ALU.is_equal)

    G3 = GS.rearrange("p (b g) -> p b g", b=2)
    GO, GTm = st[:, 16:24].rearrange("p (b g) -> p b g", b=2), st[:, 24:32].rearrange("p (b g) -> p b g", b=2)
    first_max(G3, 4, GO, st[:, 32:34], GTm)
    GM = ROUT[:, 600:600 + 32].rearrange("p (g e) -> p g e", e=4)
    V(vv.tensor_copy, GM, st[:, 16:24].unsqueeze(2).broadcast_to([P, 8, 4]))
    NG = ROUT[:, 640:640 + 32]
    V(vv.tensor_tensor, ML.rearrange("p b e -> p (b e)"), ROUT[:, 64:64 + 32], ROUT[:, 600:600 + 32], ALU.mult)
    V(vv.tensor_scalar, NG, ROUT[:, 600:600 + 32], 1e30, -1e30, ALU.mult, ALU.add)
    V(vv.tensor_tensor, ROUT[:, 128:128 + 32], ROUT[:, 128:128 + 32], NG, ALU.add)
    TM = ROUT[:, 700:700 + 32].rearrange("p (b e) -> p b e", b=2)
    first_max(ML, NE, EX, st[:, 34:36], TM)
    V(vv.scalar_tensor_tensor, ML, EX, -3e30, ML, ALU.mult, ALU.add)
    first_max(ML, NE, E2, st[:, 36:38], TM)
    V(vv.tensor_tensor, EX, EX, E2, ALU.add)
    V(vv.tensor_tensor, EX, EX, PR, ALU.mult)
    V(vv.tensor_reduce, st[:, 38:40], EX, AX, ALU.add)
    V(vv.reciprocal, st[:, 40:42], st[:, 38:40])
    v = V(vv.tensor_tensor, EX, EX, st[:, 40:42].unsqueeze(2).broadcast_to([P, 2, NE]), ALU.mult)
    wait("pe", v, Tok(s_sel, 16, 0, None))
    for b in range(2):
        ins = nc.tensor.transpose(PS[0:NE, 2, b * P:(b + 1) * P], EX[:, b, :], ident)
    pe = done("pe", ins)
    CT = ROUT[0:NE, 768:1024]
    a = A(CT, PS[0:NE, 2, 0:256], ACT.Copy, w=[pe])
    wait("pe", a)
    for e in range(NE):
        wait("pe", a)
        ins = mm(PS[:, (e // 2) % 2, (e % 2) * 256:(e % 2 + 1) * 256], SEL[:, e * P:(e + 1) * P], CT, True, True)
        if e % 2:
            pe = done("pe", ins)
            a2 = A(COMB[:, e - 1:e + 1, :], PS[:, (e // 2) % 2, :].rearrange("p (e t) -> p e t", e=2), ACT.Copy, w=[pe])
            a, a_prev = (a if e == 1 else a_prev), a2
    clear_sums()
    HB = tuple(rounded("he_" + n, aB + 7696 + m * 1024, 1024).rearrange("p (a n) -> p a n", a=2) for m, n in enumerate(("high", "low")))
    SGe, UC = (view(aB + 9744 + m * 1024, 1024).rearrange("p (a n) -> p a n", a=2) for m in range(2))
    all_wait()
    c0 = c_now

    def expert(i):
        before = {n: last(n) for n in q.eng}
        q.slots_of_turn_before(slot_free, count[0], 12)
        for n in range(6):
            plan.extend(weights(c0 + n))
        h_t = []
        for a_ in range(2):
            wait("pe", before["dve"], before["act"])
            for u in range(2):
                for j in range(2):
                    pe = out_tile(PS[:, 2 * a_ + u, j * 256:(j + 1) * 256], XIN)
                if u == 0:
                    s_t = A(SGe[:, a_, :], PS[:, 2 * a_, :], ACT.Sigmoid, w=[pe, before["dve"]])
                    V(vv.tensor_tensor, SGe[:, a_, :], SGe[:, a_, :], PS[:, 2 * a_, :], ALU.mult, w=[s_t])
            comb = COMB[:, bass.ds(i, 1), :].broadcast_to([P, 2, S])
            V(vv.tensor_tensor, UC[:, a_, :].rearrange("p (j t) -> p j t", j=2), PS[:, 2 * a_ + 1, :].rearrange("p (j t) -> p j t", j=2), comb, ALU.mult, w=[pe])
            v = V(vv.tensor_tensor, UC[:, a_, :], SGe[:, a_, :], UC[:, a_, :], ALU.mult, w=[before["act"]])
            h_t.append(split_act(HB[0][:, a_, :], HB[1][:, a_, :], UC[:, a_, :], w=[v, before["pe"]]))
        for a_ in range(2):
            wait("pe", h_t[a_])
            for j in range(2):
                s_ = take()
                second_product(both(HB, slice(None), a_, slice(j * 256, (j + 1) * 256)), s_)

    q.run_loop(NE, {"pe": 12, "dve": 14, "act": 16, "pool": 0}, expert)
    c_now += 6 * NE
    assert c_now == N_CHUNKS, c_now
    xt = evacuate(MOD[:, 136:144])
    rms_rows(X[:, :, :], xt, XC[:, :, :])
    s_out = nc.alloc_semaphore("s_out")
    for k in range(KT):
        v = V(vv.tensor_scalar, X[:, k, :], XC[:, k, :], par_("fing", k), None, ALU.mult)
        if k % 4 == 3:
            nc.sync.wait_ge(v.sem, v.n)
            nc.sync.dma_start(outT[:, k - 3:k + 1, :], X[:, k - 3:k + 1, :]).then_inc(s_out, 16)
    nc.sync.wait_ge(s_out, 32)


def tables():
    f64, f32 = np.float64, np.float32
    t = np.arange(S)
    out = {}
    inv = f32(500000.0) ** (-np.arange(0, 32, 2, dtype=f32) / f32(32))
    ang = (t.astype(f32)[:, None] * inv[None, :]).astype(f32)
    z = np.zeros((P, S))
    out["ropec"] = z.copy()
    out["ropec"][0:16] = out["ropec"][16:32] = np.cos(ang.astype(f64)).T
    out["ropes"] = z.copy()
    out["ropes"][0:16] = out["ropes"][16:32] = np.sin(ang.astype(f64)).T
    r = np.zeros((P, 32))
    for m in range(16):
        r[m + 16, m] = -1.0
        r[m, m + 16] = 1.0
    out["roper"] = r
    qi = np.arange(S).reshape(2, P).T
    out["amask"] = np.where(np.abs(qi[:, :, None] - t[None, None, :]) <= WIN, 0.0, -1e30).reshape(P, 512)
    tt = np.linspace(0.0, 1.0, S, dtype=f32)
    w = (f32(2.0 * math.pi) * t.astype(f32) / f32(S)).astype(f32)
    bands = np.linspace(1e-4, 15, 16, dtype=f32)
    bw = (bands[None, :] * w[:, None]).astype(f32).astype(f64)
    zf = np.concatenate([tt[:, None], np.cos(bw), -np.sin(bw)], axis=1).T
    out["zf"] = np.zeros((P, S))
    out["zf"][0:33] = zf
    f = np.arange(S)
    th = np.pi * ((2 * f[None, :] + 1) * t[:, None] % 1024) / 512.0
    blk = lambda m: m.reshape(2, P, S).transpose(1, 0, 2).reshape(P, 512)
    out["dc"], out["ds"] = blk(np.cos(th)), blk(np.sin(th))
    out["ic"], out["is"] = blk(np.cos(th).T / 256.0), blk(np.sin(th).T / 256.0)
    fl = 2 * np.pi * (np.outer(t, t) % S) / S
    out["flc"], out["fls"] = blk(np.cos(fl) / 16.0), blk(np.sin(fl) / 16.0)
    c = np.arange(64)
    fc = 2 * np.pi * (np.outer(c, c) % 64) / 64
    e2 = np.eye(2)
    out["fcc"], out["fcs"] = np.kron(e2, np.cos(fc) / 8.0), -np.kron(e2, np.sin(fc) / 8.0)
    dl = np.linspace(math.log(1e-2) / 1.5, math.log(1e-2) / 0.3, 256, dtype=f32)
    dec = np.exp((-tt[:, None] * np.abs(dl)[None, :]).astype(f32).astype(f64))
    out["decf"] = blk(dec)
    decb = dec.copy()
    decb[0] = 0.0
    out["decb"] = blk(decb)
    s_, t_ = np.arange(P)[:, None], np.arange(P)[None, :]
    lm = [np.eye(P)]
    for lev in range(1, 8):
        lm.append((s_ >> lev == t_ >> lev) & (s_ >> (lev - 1) != t_ >> (lev - 1)))
    out["lmask"] = np.stack(lm, 1).reshape(P, 1024)
    out["iota"] = np.tile(np.arange(16.0), (P, 1))
    tab, tab2 = (np.concatenate([out[n] for n in c_], axis=1).astype(f32) for c_ in (TCOL, T2COL))
    quarter = D // 4
    om = (f32(1.0) / (f32(10000.0) ** (np.arange(quarter, dtype=f32) / f32(quarter)))).astype(f32)
    ar = ((t // 64).astype(f32)[:, None] * om).astype(f32).astype(f64)
    ac = ((t % 64).astype(f32)[:, None] * om).astype(f32).astype(f64)
    pos = np.concatenate([np.sin(ar), np.cos(ar), np.sin(ac), np.cos(ac)], axis=1).astype(f32)
    sel = np.zeros((NE, NE, P), f32)
    for e in range(NE):
        sel[e, e] = 1.0
    return tab, tab2, fm(pos), sel.reshape(NE, NE * P)


def fm(x):
    return np.ascontiguousarray(x.T.reshape(-1, P, x.shape[0]).transpose(1, 0, 2))


def cols(v, p=P):
    return v.reshape(-1, p).T


def kernel(**inputs):
    import concourse.bacc as bacc
    from concourse.bass_utils import run_bass_kernel_spmd as run

    I = {k: np.asarray(v) for k, v in inputs.items()}

    def out_tiles(w):
        n = w.shape[1] // P
        return w.reshape(KT, P, n // 2, 2, P).transpose(2, 1, 3, 0, 4).reshape(n // 2, P, CH)

    def in_tiles(w):
        return w.reshape(-1, 2, P, D).transpose(0, 2, 1, 3).reshape(-1, P, CH)

    def ada(w):
        return in_tiles(w.T)

    def pad(a, axis, n):
        shape = list(a.shape)
        shape[axis] = n - a.shape[axis]
        return np.concatenate([a, np.zeros(shape, a.dtype)], axis=axis)

    a = [[ada(I["ada_w"][i, m]) for m in range(2)] for i in range(2)]
    a2 = ada(I["ada_w_2"][0])
    wi = I["attn_w_in"][0]
    v_in = wi[:, 1280:1536].reshape(KT, P, 256).transpose(1, 0, 2).reshape(1, P, CH)
    attn_in = np.concatenate([out_tiles(wi[:, 0:1280]), v_in])

    def mlp(w1, w2, ad):
        w1, w2 = out_tiles(w1), in_tiles(w2)
        return np.stack([w1[0::2], w1[1::2], w2[0::2], ad[0::2], w2[1::2], ad[1::2]], 1).reshape(-1, P, CH)

    rw = I["rnn_w_in"][0].reshape(KT, P, 2, NB, BW).transpose(3, 1, 2, 0, 4).reshape(NB, P, 2 * KT * BW)
    wa, wx = I["rnn_w_a"][0], I["rnn_w_x"][0]
    gw = np.stack([wa[0], wx[0], wa[1], wx[1]], 1).transpose(0, 2, 1, 3).reshape(NB, BW, 4 * BW)
    gw = gw.transpose(1, 0, 2)
    rnn = pad(rw, 2, CH)
    rnn_ada = np.concatenate([a[1][1][4:12], a2[16:24]])
    rnn = np.stack([rnn, rnn_ada], 1).reshape(-1, P, CH)
    rnn_out = pad(I["rnn_w_out"][0].reshape(8, 2, BW, D).transpose(0, 2, 1, 3).reshape(8, BW, CH), 1, P)
    w2i = I["w_in_2"][0]
    hy, hq, hff, hfb, hi, hg, fn = np.split(w2i, [768, 1280, 1792, 2304, 2816, 3328], axis=1)
    hi = hi.reshape(2, 4, P, 512).transpose(0, 2, 1, 3).reshape(2, P, CH)
    w_in2 = np.concatenate([out_tiles(hff), out_tiles(hfb), hi, out_tiles(hq), out_tiles(hy), out_tiles(hg), out_tiles(fn)])
    moe = []
    for e in range(NE):
        g_, u_ = out_tiles(I["moe_w_gate_2"][0, e]), out_tiles(I["moe_w_up_2"][0, e])
        d_ = in_tiles(I["moe_w_down_2"][0, e])
        moe += [g_[0:1], u_[0:1], g_[1:2], u_[1:2], d_]
    stream = np.concatenate([
        a[0][0][0:8], attn_in, a[0][0][8:12], a[0][1][0:8], out_tiles(I["attn_w_out"][0]), a[0][1][8:12],
        mlp(I["mlp_w1"][0], I["mlp_w2"][0], np.concatenate([a[1][0], a[1][1][0:4]])),
        rnn, rnn_out,
        mlp(I["mlp_w1"][1], I["mlp_w2"][1], a2[0:16]),
        w_in2, out_tiles(I["w_out_2"][0])] + moe)
    assert stream.shape[0] == N_CHUNKS, stream.shape

    rep = lambda v: np.broadcast_to(v.reshape(1, -1), (P, v.size))
    fnw = np.zeros((2, 2, 64, 2, 64), np.float32)
    fw = I["fn_w_2"][0].reshape(2, 2, 64, 64)
    for j in range(2):
        fnw[:, j, :, j, :] = fw[:, j]
    eps = np.ones((P, 1), np.float32)
    par = {"ada_b": cols(I["ada_b"]), "ada_b2": cols(I["ada_b_2"]), "ln_g": cols(I["ln_g"]), "ln_b": cols(I["ln_b"]),
           "n1g": cols(I["norm1_g_2"]), "n2g": cols(I["norm2_g_2"]), "fing": cols(I["final_norm_g_2"]),
           "hycw": cols(I["hy_conv_w_2"]), "hycb": cols(I["hy_conv_b_2"]), "hybias": cols(I["hy_bias_2"]),
           "hyg": cols(I["hy_norm_g_2"]), "lb": cols(I["hg_lower_bounds_2"]), "hgg": cols(I["hg_norm_g_2"]),
           "fnb": cols(I["fn_b_2"]), "fng": cols(I["fn_norm_g_2"]), "sinks": rep(I["attn_sinks"]), "rb": rep(I["router_b_2"]),
           "rw": I["router_w_2"].reshape(KT, P, NE).transpose(1, 0, 2).reshape(P, KT * NE),
           "fnw": fnw.reshape(2, P, P).transpose(1, 0, 2).reshape(P, 2 * P), "eps5": eps * np.float32(LN_EPS), "eps6": eps * np.float32(RMS_EPS)}
    par = np.concatenate([par[n] for n in PCOL], axis=1)
    rpar = np.concatenate([cols(I[n], BW) for n in ("rnn_conv_w", "rnn_conv_b", "rnn_b_a", "rnn_b_x", "rnn_lam")], axis=1)
    fpar = np.concatenate([pad(I["hy_filt_w1_2"][0], 0, 64), I["hy_filt_w2_2"][0], I["hy_filt_w3_2"][0]]
                          + [I[n][0].reshape(64, 1) for n in ("hy_filt_b1_2", "hy_filt_b2_2", "hy_filt_freq_2")], axis=1)
    tab, tab2, pos, sel = tables()
    data = {"stream": stream, "xT": fm(I["x"][0]), "ctxT": fm(I["ctx_2"][0]), "posT": pos,
            "cvec": np.concatenate([I["c"], I["c_2"], I["c_ctx_2"].reshape(1, D)]), "par": par, "rpar": rpar,
            "fpar": fpar, "ident": np.eye(P, dtype=np.float32), "tab": tab, "tab2": tab2, "sel": sel, "gw": gw.reshape(BW, NB * 4 * BW)}
    data = {k: np.ascontiguousarray(v) for k, v in data.items()}
    nc = bacc.Bacc("TRN2", target_bir_lowering=False, num_devices=1)
    aps = [nc.dram_tensor(n, v.shape, F32, kind="ExternalInput").ap() for n, v in data.items()]
    out = nc.dram_tensor("outT", (P, KT, S), F32, kind="ExternalOutput").ap()
    build(nc, *aps, out)
    r = run(nc, [data], core_ids=[0]).results[0]["outT"]
    return np.ascontiguousarray(r.transpose(1, 0, 2).reshape(D, S).T).reshape(1, S, D)
```

```python
import itertools
import math

import numpy as np

import concourse.bass as bass
from concourse import mybir

F32 = mybir.dt.float32
F32R = mybir.dt.float32r
U32 = mybir.dt.uint32
ALU = mybir.AluOpType
ACT = mybir.ActivationFunctionType
AX = mybir.AxisListType.X

D, S, P = 1024, 256, 128
KT = D // P
NH, NKV, WIN = 8, 2, 128
NB, BW = 16, 96
FF = 4096
HGH = 4
NE, DE = 16, 512
DEPTH = 2
ALPHA = (2.0 * DEPTH) ** 0.25
LN_EPS, RMS_EPS = 1e-5, 1e-6
CH = 2048
HALF = CH // 2
RING = 6
SLOTS = 4
TURN = 12

N_CHUNKS = 284


def _cols(spec):
    at, out = 0, {}
    for name, n in spec:
        out[name] = (at, at + n)
        at += n
    return out, at


PCOL, PN = _cols([("ada_b", 96), ("ada_b2", 48), ("ln_g", 32), ("ln_b", 32), ("n1g", 8), ("n2g", 8),
                  ("fing", 8), ("hycw", 18), ("hycb", 6), ("hybias", 4), ("hyg", 2), ("lb", 8),
                  ("hgg", 4), ("fnb", 2), ("fng", 2), ("sinks", 8), ("rb", 16), ("rw", 128),
                  ("fnw", 256), ("eps5", 1), ("eps6", 1)])
RCOL, RN = _cols([("cw", 64), ("cb", 16), ("ba", 32), ("bx", 32), ("lam", 32)])
FCOL, FN = _cols([("w1", 64), ("w2", 64), ("w3", 1024), ("b1", 1), ("b2", 1), ("fr", 1)])
TCOL, TN = _cols([("ropec", 256), ("ropes", 256), ("roper", 32), ("amask", 512)])
T2COL, T2N = _cols([("dc", 512), ("ds", 512), ("ic", 512), ("is", 512), ("flc", 512), ("fls", 512),
                    ("fcc", 128), ("fcs", 128), ("lmask", 1024), ("iota", 16), ("zf", 256), ("decf", 512), ("decb", 512)])


class Tok:

    def __init__(self, sem, n, k, loop):
        self.sem, self.n, self.k, self.loop = sem, n, k, loop

    def before(self):
        return Tok(self.sem, self.n - self.k, self.k, self.loop)


class Loop:
    def __init__(self, reg, turns, per_turn):
        self.reg, self.turns, self.per_turn = reg, turns, per_turn


class Count:

    def __init__(self, nc):
        self.nc = nc
        self.loop = None
        self.eng = {}
        for name, e in (("pe", nc.tensor), ("dve", nc.vector), ("act", nc.scalar), ("pool", nc.gpsimd)):
            self.eng[name] = [e, nc.alloc_semaphore("done_" + name), 0, None]
        self.arrived = [nc.alloc_semaphore(f"arrived{j}") for j in range(RING)]
        self.freed = [nc.alloc_semaphore(f"freed{j}") for j in range(RING)]

    def wait(self, name, *toks):
        e = self.eng[name][0]
        for t in toks:
            if t is None:
                continue
            if t.loop is not None and t.loop is self.loop and t.k:
                e.wait_ge(t.sem, self.loop.reg * t.k + t.n)
            elif t.loop is not None and t.loop is not self.loop:
                e.wait_ge(t.sem, t.n + (t.loop.turns - 1) * t.k)
            else:
                e.wait_ge(t.sem, t.n)

    def done(self, name, ins, frees=None):
        rec = self.eng[name]
        if frees is not None:
            ins.then_inc(self.freed[frees % RING], 1)
            rec[3] = Tok(self.freed[frees % RING], frees // RING + 1, TURN // RING if self.loop else 0, self.loop)
        else:
            ins.then_inc(rec[1], 1)
            rec[2] += 1
            rec[3] = Tok(rec[1], rec[2], self.loop.per_turn[name] if self.loop else 0, self.loop)
        return rec[3]

    def last(self, name):
        return self.eng[name][3]

    def wait_piece(self, name, c):
        n = 16 * (c // RING + 1)
        self.wait(name, Tok(self.arrived[c % RING], n, 16 * (TURN // RING) if self.loop else 0, self.loop))

    def run_loop(self, turns, per_turn, body):
        base = {k: v[2] for k, v in self.eng.items()}
        engines = [mybir.EngineType.PE, mybir.EngineType.DVE, mybir.EngineType.Activation, mybir.EngineType.Pool]
        with self.nc.Fori(0, turns, engines=engines) as i:
            self.loop = Loop(i, turns, per_turn)
            for k, v in self.eng.items():
                if v[2] and per_turn[k]:
                    v[3] = Tok(v[1], v[2], per_turn[k], self.loop)
            body(i)
            for k, v in self.eng.items():
                assert v[2] - base[k] == per_turn[k], (k, v[2] - base[k], per_turn[k])
                v[2] = base[k] + turns * per_turn[k]
            self.loop = None


def build(nc, stream, xT, ctxT, posT, cvec, par, rpar, fpar, ident_d, tab, tab2, sel, gw, outT):
    q = Count(nc)
    wait, done, last, wait_piece = q.wait, q.done, q.last, q.wait_piece
    TOTAL = 53208
    base = (nc.sbuf_base + 31) // 32 * 32
    PS = nc.alloc_psum_tensor("ps", [P, 8, 512], F32)
    at = [0]

    def place(n):
        a = at[0]
        at[0] += n
        return a

    def view(a, n, p=P):
        assert a + n <= TOTAL
        lo = a // 8 * 8
        return nc.alloc_sbuf_tensor_at(f"at{lo}_{n}", [p, a + n - lo], F32, offset=base + 4 * lo)[:, a - lo:]

    def rounded(name, a, n, p=P):
        return nc.alloc_sbuf_tensor_at(name, [p, n], F32R, offset=base + 4 * a)[:]

    ring = view(place(RING * HALF), RING * HALF)
    WH = rounded("w_high", place(SLOTS * HALF), SLOTS * HALF)
    WL = rounded("w_low", place(SLOTS * HALF), SLOTS * HALF)
    kt = lambda ap, n=KT: ap.rearrange("p (k t) -> p k t", k=n)
    X = kt(view(place(2048), 2048))
    aT1 = place(2048)
    aT2 = place(2048)
    T1, T2 = kt(view(aT1, 2048)), kt(view(aT2, 2048))
    aC = place(2048)
    CB = view(aC, 2048).rearrange("p (a n) -> p a n", a=2)
    MOD = view(place(160), 160)
    PAR = view(place(PN), PN)
    RPAR = view(place(RN), RN, BW)
    ident = view(place(P), P)
    ONES = view(place(P), P)
    aM = place(384)
    MISC = view(aM, 384)
    RS = view(place(512), 512)
    aKF = place(2048)
    KF = view(aKF, 2048)
    place_row = place(P)
    aX = place(4096)
    aXL = place(4096)
    XH = rounded("x_high", aX, 4096).rearrange("p (s k t) -> p s k t", s=2, k=KT)
    XL = rounded("x_low", aXL, 4096).rearrange("p (s k t) -> p s k t", s=2, k=KT)
    XIN = (XH[:, 0], XL[:, 0])
    aB = at[0]
    aTab2 = aB + 12288
    assert aTab2 + T2N <= TOTAL and aB % 8 == 0 and aX % 8 == 0, (aTab2 + T2N, aB, aX)
    TAB, TAB2 = view(aB, TN), view(aTab2, T2N)

    def par_(name, j=0, n=1):
        return PAR[:, PCOL[name][0] + j:PCOL[name][0] + j + n]

    def tab_(name, p=P):
        if name in TCOL:
            return TAB[0:p, TCOL[name][0]:TCOL[name][1]]
        return TAB2[0:p, T2COL[name][0]:T2COL[name][1]]

    def V(f, *a, w=(), frees=None, **k):
        wait("dve", last("dve"), *w)
        return done("dve", f(*a, **k), frees)

    def A(out, in_, func, w=(), **k):
        wait("act", last("act"), *w)
        return done("act", nc.scalar.activation(out, in_, func, **k))

    def G(f, *a, w=(), frees=None, **k):
        wait("pool", last("pool"), *w)
        return done("pool", f(*a, **k), frees)

    vv = nc.vector

    def mm(out, lhsT, rhs, start, stop):
        return nc.tensor.matmul(out, lhsT, rhs, start=start, stop=stop, skip_group_check=True)

    def piece(c):
        return ring[:, (c % RING) * HALF:(c % RING + 1) * HALF]

    slot_free = [None] * SLOTS
    plan = []
    ready = []
    count = [0]

    def split_next():
        item = plan.pop(0)
        if item[0] == "a":
            ada_chunk(*item[1:])
            return
        c = item[1]
        s_ = count[0] % SLOTS
        count[0] += 1
        hi, lw = WH[:, s_ * HALF:(s_ + 1) * HALF], WL[:, s_ * HALF:(s_ + 1) * HALF]
        wait_piece("act", c)
        a = A(hi, piece(c), ACT.Copy, w=[slot_free[s_]])
        ready.append((s_, V(vv.tensor_tensor, lw, piece(c), hi.bitcast(F32), ALU.subtract, w=[a], frees=c)))

    def weights(c):
        return [("w", 2 * c), ("w", 2 * c + 1)]

    def take():
        while len(ready) < SLOTS and any(item[0] == "w" for item in plan):
            split_next()
        s_, v = ready.pop(0)
        wait("pe", v)
        return s_

    def used(s_, ins):
        slot_free[s_] = done("pe", ins)
        return slot_free[s_]

    def part(s_, lo, n=P, p=P):
        a = s_ * HALF + lo
        return WH[0:p, a:a + n], WL[0:p, a:a + n]

    def carried(c0):
        return [((count[0] - SLOTS + n) % SLOTS, Tok(q.freed[p % RING], p // RING + 1, TURN // RING, q.loop))
                for n, p in enumerate(range(2 * c0 - SLOTS, 2 * c0))]

    def carry_holds(c0):
        for (_, tok), p in zip(ready, range(2 * c0 + 12 - SLOTS, 2 * c0 + 12)):
            assert len(ready) == SLOTS and tok.sem is q.freed[p % RING] and tok.n == p // RING + 1

    def mm3(out, l, r, start, stop):
        mm(out, l[0], r[0], start, False)
        mm(out, l[0], r[1], False, False)
        return mm(out, l[1], r[0], False, stop)

    def split_act(hi, lo, src, w=()):
        a = A(hi, src, ACT.Copy, w=w)
        return V(vv.tensor_tensor, lo, src, hi.bitcast(F32), ALU.subtract, w=[a])

    def earlier(tok, n):
        return Tok(tok.sem, tok.n - n, tok.k, tok.loop)

    both = lambda pair, *ix: (pair[0][ix], pair[1][ix])

    def no_pool_wait():
        toks = {n: last(n) for n in q.eng}
        for n in ("pe", "act", "dve"):
            wait(n, *[toks[m] for m in ("pe", "act", "dve") if m != n])

    def all_wait():
        toks = {n: last(n) for n in q.eng}
        for n in q.eng:
            wait(n, *[t for m, t in toks.items() if m != n])

    sp = nc.sync
    turns = 2 * N_CHUNKS // RING

    def fetch(c, j):
        src = stream[c] if isinstance(c, int) else stream[bass.ds(c, 1)].rearrange("a p n -> (a p) n")
        sp.dma_start(ring[:, j * HALF:(j + 1) * HALF], src).then_inc(q.arrived[j], 16)

    for j in range(RING):
        fetch(j, j)
    with sp.Fori(1, turns) as i:
        for j in range(RING):
            sp.wait_ge(q.freed[j], i)
            fetch(i * RING + j, j)
    for j in range(2 * N_CHUNKS - turns * RING):
        sp.wait_ge(q.freed[j], turns)
        fetch(turns * RING + j, j)

    s_c, s_par, s_x, s_att, s_rnn = (nc.alloc_semaphore(n) for n in ("s_c", "s_par", "s_x", "s_att", "s_rnn"))
    s_c2 = nc.alloc_semaphore("s_c2")
    nc.scalar.dma_start(RPAR, rpar).then_inc(s_rnn, 16)
    nc.scalar.dma_start(CB[:, 0, :], cvec[0:1, :].broadcast_to([P, D])).then_inc(s_c, 16)
    nc.scalar.dma_start(PAR, par).then_inc(s_par, 16)
    nc.scalar.dma_start(X, xT).then_inc(s_x, 16)
    ZROW = view(place_row, P, 1)
    G(nc.gpsimd.memset, ZROW, 0.0)
    G(nc.gpsimd.memset, ONES, 1.0)
    wait("pe", last("pool"))
    rp = lambda n, j, k=1: RPAR[:, RCOL[n][0] + j:RCOL[n][0] + j + k]
    RM = view(aM + 128, 256, BW)
    cs, hba, hbx = RM[:, 0:32], RM[:, 32:64], RM[:, 64:96]
    t0, t1, t2, cs2 = RM[:, 96:128], RM[:, 128:160], RM[:, 160:192], RM[:, 192:224]
    wait("dve", Tok(s_rnn, 16, 0, None))
    lam = rp("lam", 0, 32)
    V(vv.tensor_scalar, t0, lam, -1.0, None, ALU.mult)
    V(vv.tensor_tensor, t1, t0, lam, ALU.min)
    A(t1, t1, ACT.Exp, w=[last("dve")])
    exp_t = last("act")
    silu_c = A(CB[:, 0, :], CB[:, 0, :], ACT.Silu, w=[Tok(s_c, 16, 0, None)])
    V(vv.tensor_scalar, t2, t1, 2.0, None, ALU.add, w=[exp_t])
    V(vv.reciprocal, t2, t2)
    V(vv.tensor_tensor, t1, t1, t2, ALU.mult)
    V(vv.tensor_tensor, t2, t1, t1, ALU.mult)
    V(vv.tensor_scalar, cs, t2, 1.0 / 17, None, ALU.mult)
    for d in (15, 13, 11, 9, 7, 5, 3):
        V(vv.scalar_tensor_tensor, cs, cs, 1.0 / d, t2, ALU.add, ALU.mult)
    V(vv.scalar_tensor_tensor, cs, cs, 1.0, t1, ALU.add, ALU.mult)
    V(vv.tensor_scalar, cs, cs, 4.0, None, ALU.mult)
    V(vv.tensor_scalar, t0, t0, 0.0, 2.0, ALU.max, ALU.mult)
    V(vv.tensor_tensor, cs, cs, t0, ALU.add)
    V(vv.tensor_scalar, hba, rp("ba", 0, 32), 0.5, None, ALU.mult)
    V(vv.tensor_scalar, hbx, rp("bx", 0, 32), 0.5, None, ALU.mult)
    V(vv.tensor_scalar, cs2, cs, -2.0, None, ALU.mult)
    wait("dve", silu_c, Tok(s_par, 16, 0, None))
    wait("act", Tok(s_par, 16, 0, None))

    JUNK = view(aT2, 1024)
    product_read = [None, None]

    def ada_chunk(c, col, conds=((0, 0),), junk=None):
        junk = JUNK if junk is None else junk
        for j in range(2):
            wait_piece("dve", 2 * c + j)
            for n, (v, off) in enumerate(conds):
                acc = MOD[:, col + off + j:col + off + j + 1] if q.loop is None else MISC[:, 2 * n + j:2 * n + j + 1]
                V(vv.tensor_tensor_reduce, junk, piece(2 * c + j), CB[:, v, :], 1.0, 0.0, ALU.mult, ALU.add, acc,
                  frees=2 * c + j if n == len(conds) - 1 else None)
        if q.loop is not None:
            for n, (v, off) in enumerate(conds):
                V(vv.tensor_copy, MOD[:, bass.ds(q.loop.reg * 4 + (col + off), 2)], MISC[:, 2 * n:2 * n + 2])

    def ada_bias(a, n, name, j):
        V(vv.tensor_tensor, MOD[:, a:a + n], MOD[:, a:a + n], par_(name, j, n), ALU.add)

    c_now = 0
    wait("pool", silu_c)
    n_pool = 0
    for j in range(8):
        for h in range(2):
            p_, col = 2 * c_now + h, 2 * j + h
            if p_ % 5 == 1:
                half = view(aT1 + 1024 * (n_pool % 2), 1024)
                wait("pool", product_read[n_pool % 2])
                q.wait_piece("pool", p_)
                t = G(nc.gpsimd.tensor_tensor, half, piece(p_), CB[:, 0, :], ALU.mult, frees=p_)
                product_read[n_pool % 2] = ada_t = A(half, half, ACT.Copy, w=[t], accum_out=MOD[:, col:col + 1])
                n_pool += 1
            else:
                wait_piece("dve", p_)
                V(vv.tensor_tensor_reduce, JUNK, piece(p_), CB[:, 0, :], 1.0, 0.0, ALU.mult, ALU.add, MOD[:, col:col + 1], frees=p_)
        c_now += 1
    wait("dve", ada_t)
    ada_bias(0, 16, "ada_b", 0)

    XC, SQ = T1, T2
    MEAN, VAR = PS[:, 0, 0:256], PS[:, 1, 0:256]
    RSTD = RS[:, 0:256]
    combo = MISC[:, 16:80]

    def modulated(src, scale, shift, s_=0, w=()):
        his, toks = [], []
        for k in range(0, KT, 2):
            for kk in (k, k + 1):
                v = V(vv.tensor_scalar, T2[:, kk, :], src[:, kk, :], scale[:, kk:kk + 1], shift[:, kk:kk + 1], ALU.mult, ALU.add, w=w)
            his.append(A(XH[:, s_, k:k + 2, :], T2[:, k:k + 2, :], ACT.Copy, w=[v]))
        if plan and not ready:
            split_next()
        for n, a in enumerate(his):
            k = 2 * n
            toks += [V(vv.tensor_tensor, XL[:, s_, k:k + 2, :], T2[:, k:k + 2, :], XH[:, s_, k:k + 2, :].bitcast(F32), ALU.subtract, w=[a])] * 2
        return toks

    def add_branch(n, y, g, tok):
        wait("dve", last("pool"))
        return V(vv.scalar_tensor_tensor, X[:, n, :], y, g, X[:, n, :], ALU.mult, ALU.add, w=[tok])

    def column_sums(bank, src, toks, half=None):
        for k in range(KT):
            wait("pe", toks[k])
            ins = mm(bank, ONES, src[:, k, :], k == 0, k == KT - 1)
        return done("pe", ins)

    def root(dst, src, scale, eps, w):
        A(dst, src, ACT.Sqrt, w=w, scale=scale, bias=eps)
        return V(vv.reciprocal, dst, dst, w=[last("act")])

    def layer_norm(ln, toks, scale_col, shift_col, nxt_alpha, into_xin):
        lg, lb_ = par_("ln_g", 8 * ln, 8), par_("ln_b", 8 * ln, 8)
        pe = column_sums(MEAN, X, toks)
        mean = RS[:, 256:512]
        A(MISC[:, 14:15], par_("eps5"), ACT.Sqrt)
        V(vv.tensor_scalar, mean, MEAN, 1.0 / D, None, ALU.mult, w=[pe, last("pool")])
        sq = []
        for k in range(0, KT, 2):
            v = V(vv.tensor_tensor, XC[:, k:k + 2, :], X[:, k:k + 2, :], mean.unsqueeze(1).broadcast_to([P, 2, S]), ALU.subtract)
            sq += [A(SQ[:, k:k + 2, :], XC[:, k:k + 2, :], ACT.Square, w=[v])] * 2
        ga, ba = combo[:, 8:16], combo[:, 16:24]
        V(vv.tensor_scalar, ga, lg, nxt_alpha, None, ALU.mult)
        V(vv.tensor_scalar, ba, lb_, nxt_alpha, None, ALU.mult)
        gm, bm = combo[:, 24:32], combo[:, 32:40]
        if into_xin:
            V(vv.tensor_scalar, combo[:, 40:48], scale_col, 1.0, None, ALU.add)
            V(vv.tensor_tensor, gm, lg, combo[:, 40:48], ALU.mult)
            V(vv.tensor_tensor, bm, lb_, combo[:, 40:48], ALU.mult)
            V(vv.tensor_tensor, bm, bm, shift_col, ALU.add)
        pe = column_sums(VAR, SQ, sq)
        v = root(RSTD, VAR, 1.0 / D, par_("eps5"), [pe])
        out, xs = [], []
        for h in range(2):
            V(vv.tensor_tensor, XC[:, 4 * h:4 * h + 4, :], XC[:, 4 * h:4 * h + 4, :],
              RSTD.unsqueeze(1).broadcast_to([P, 4, S]), ALU.mult)
        if into_xin:
            out = modulated(XC, gm, bm)
        if not into_xin:
            for k in range(KT):
                xs.append(V(vv.tensor_scalar, X[:, k, :], XC[:, k, :], ga[:, k:k + 1], ba[:, k:k + 1], ALU.mult, ALU.add))
            return out, xs
        for k in range(KT):
            xs.append(G(nc.gpsimd.tensor_scalar, X[:, k, :], XC[:, k, :], ga[:, k:k + 1], ba[:, k:k + 1], ALU.mult, ALU.add, w=[last("dve")] if k == 0 else []))
        return out, xs

    def clear_sums(read=None):
        if read is None:
            wait("pe", last("dve"), last("act"))
        wait("pe", read)
        for b in range(4):
            ins = mm(PS[:, 4 + b, :], ZROW, ONES[0:1, :].unsqueeze(1).broadcast_to([1, 4, P]), True, False)
        return done("pe", ins)

    for n in range(6):
        plan += weights(c_now + n)
    c_now += 6
    for j in range(4):
        plan.append(("a", c_now + j, 16 + 2 * j))
    c_now += 4
    V(vv.tensor_scalar, combo[:, 0:8], MOD[:, 8:16], 1.0, None, ALU.add)
    htok = modulated(X, combo[:, 0:8], MOD[:, 0:8], w=[Tok(s_x, 16, 0, None)])
    for k in range(0, KT, 2):
        G(nc.gpsimd.tensor_scalar, X[:, k:k + 2, :], X[:, k:k + 2, :], ALPHA, None, ALU.mult, w=[last("dve"), Tok(s_x, 16, 0, None)])
    nc.scalar.dma_start(TAB, tab).then_inc(s_att, 16)
    nc.scalar.dma_start(ident, ident_d).then_inc(s_att, 16)
    nc.scalar.dma_start(CB[:, 1, :], cvec[1:2, :].broadcast_to([P, D])).then_inc(s_c2, 16)
    wait("pe", Tok(s_att, 32, 0, None))
    wait("dve", Tok(s_att, 32, 0, None))
    a0 = aB + 1056
    QK = kt(view(a0, 2560), 10)
    VT = view(a0 + 2560, 512).rearrange("p (b n) -> p b n", b=2)
    SC = view(a0 + 3072, 2048).rearrange("p (a h k) -> p a h k", a=2, h=4)
    PT = view(a0 + 5120, 2048).rearrange("p (a h k q) -> p a h k q", a=2, h=4, k=2)
    OT = kt(view(a0 + 7168, 2048))
    OTS = (kt(rounded("o_high", a0 + 9216, 2048)), kt(rounded("o_low", a0 + 11264, 2048)))
    RT = view(a0 + 13312, 512, 32)
    free = [None] * 8
    qk_t = [None] * 10

    def out_tile(out, src, htok=None, order=range(KT)):
        s_ = take()
        for k in order:
            if htok is not None:
                wait("pe", htok[k])
            ins = mm3(out, part(s_, k * P), both(src, slice(None), k), k == order[0], k == order[-1])
        return used(s_, ins)

    for n2 in range(5):
        bank = n2 % 2
        wait("pe", free[bank])
        for j in range(2):
            pe = out_tile(PS[:, bank, j * 256:(j + 1) * 256], XIN, htok if n2 == 0 and j == 0 else None)
        free[bank] = A(QK[:, 2 * n2:2 * n2 + 2, :], PS[:, bank, :].rearrange("p (n t) -> p n t", n=2), ACT.Copy, w=[pe])
        wait("pe", free[bank], free[2 + bank])
        pe = done("pe", mm(PS[0:32, 2 + bank, :], tab_("roper", 32), QK[0:32, 2 * n2:2 * n2 + 2, :], True, True))
        sin = tab_("ropes", 32).unsqueeze(1).broadcast_to([32, 2, S])
        cos = tab_("ropec", 32).unsqueeze(1).broadcast_to([32, 2, S])
        rt = RT.rearrange("p (n t) -> p n t", n=2)
        free[2 + bank] = V(vv.tensor_tensor, rt, PS[0:32, 2 + bank, :].rearrange("p (n t) -> p n t", n=2), sin, ALU.mult, w=[pe])
        V(vv.tensor_tensor, QK[0:32, 2 * n2:2 * n2 + 2, :], QK[0:32, 2 * n2:2 * n2 + 2, :], cos, ALU.mult)
        qk_t[2 * n2] = qk_t[2 * n2 + 1] = V(vv.tensor_tensor, QK[0:32, 2 * n2:2 * n2 + 2, :], QK[0:32, 2 * n2:2 * n2 + 2, :], rt, ALU.add)
    wait("pe", free[0], free[1])
    for half in range(2):
        s_ = take()
        for b in range(2):
            for k in range(4):
                kk = 4 * half + k
                ins = mm3(PS[:, b, 0:256], both(XIN, slice(None), kk, slice(b * P, (b + 1) * P)), part(s_, k * 256, 256), kk == 0, kk == KT - 1)
        pe = used(s_, ins)
    silu_c2 = A(CB[:, 1, :], CB[:, 1, :], ACT.Silu, w=[Tok(s_c2, 16, 0, None)])
    v_t = free[0] = free[1] = A(VT, PS[:, 0:2, 0:256], ACT.Copy, w=[pe])
    SM = view(a0 + 13824, 128)

    def scores(n, g, b):
        a = n % 2
        sm = SM[:, 32 * n:32 * n + 32]
        wait("pe", free[4], free[5], *qk_t)
        for h in range(4):
            ins = mm(PS[:, 4 + h // 2, (h % 2) * 256:(h % 2 + 1) * 256], QK[:, 4 * g + h, b * P:(b + 1) * P], QK[:, 8 + g, :], True, True)
        pe = done("pe", ins)
        mask = tab_("amask")[:, b * 256:(b + 1) * 256].unsqueeze(1).broadcast_to([P, 4, S])
        free[4] = free[5] = V(vv.scalar_tensor_tensor, SC[:, a, :, :], PS[:, 4:6, :].rearrange("p b (h k) -> p (b h) k", h=2), P ** -0.5, mask,
                              ALU.mult, ALU.add, w=[pe, sc_free[a]])
        V(vv.tensor_reduce, sm[:, 0:4], SC[:, a, :, :], AX, ALU.max)
        V(vv.tensor_tensor, sm[:, 0:4], sm[:, 0:4], par_("sinks", 4 * g, 4), ALU.max)
        V(vv.tensor_tensor, sm[:, 4:8], par_("sinks", 4 * g, 4), sm[:, 0:4], ALU.subtract)
        v = V(vv.tensor_scalar, sm[:, 8:12], sm[:, 0:4], -1.0, None, ALU.mult)
        A(sm[:, 12:16], sm[:, 4:8], ACT.Exp, w=[v])
        for h in range(4):
            e = A(SC[:, a, h, :], SC[:, a, h, :], ACT.Exp, bias=sm[:, 8 + h:9 + h], accum_out=sm[:, 16 + h:17 + h])
        return e

    def attend(n, g, b, e):
        a = n % 2
        sm = SM[:, 32 * n:32 * n + 32]
        V(vv.tensor_tensor, sm[:, 16:20], sm[:, 16:20], sm[:, 12:16], ALU.add, w=[e])
        V(vv.reciprocal, sm[:, 20:24], sm[:, 16:20])
        p_t = V(vv.tensor_tensor, SC[:, a, :, :], SC[:, a, :, :], sm[:, 20:24].unsqueeze(2).broadcast_to([P, 4, S]), ALU.mult)
        wait("pe", p_t, free[6], free[7])
        for h in range(4):
            for kb in range(2):
                ins = nc.tensor.transpose(PS[:, 6 + h // 2, (h % 2) * 256 + kb * P:(h % 2) * 256 + (kb + 1) * P], SC[:, a, h, kb * P:(kb + 1) * P], ident)
        pe = done("pe", ins)
        sc_free[a] = pe
        free[6] = free[7] = A(PT[:, a, :, :, :], PS[:, 6:8, :].rearrange("p b (h k q) -> p (b h) k q", h=2, k=2), ACT.Copy, w=[pe, pt_free[a]])
        wait("pe", free[7], v_t, free[n])
        for h in range(4):
            for kb in range(2):
                ins = mm(PS[:, n, h * P:(h + 1) * P], VT[:, kb, g * P:(g + 1) * P], PT[:, a, h, kb, :], kb == 0, kb == 1)
        pe = done("pe", ins)
        pt_free[a] = pe
        free[n] = A(OT[:, 4 * g:4 * g + 4, b * P:(b + 1) * P], PS[:, n, :].rearrange("p (h q) -> p h q", h=4), ACT.Copy, w=[pe])

    sc_free, pt_free = [None, None], [None, None]
    for j in range(8):
        plan.append(("a", c_now + j, 24 + 2 * j))
    c_now += 8
    batches = ((0, 0), (0, 1), (1, 0), (1, 1))
    e_t = [scores(0, *batches[0]), None, None, None]
    for n in range(4):
        if n < 3:
            e_t[n + 1] = scores(n + 1, *batches[n + 1])
        attend(n, *batches[n], e_t[n])
        if n % 2:
            g = batches[n][0]
            o_t = split_act(OTS[0][:, 4 * g:4 * g + 4, :], OTS[1][:, 4 * g:4 * g + 4, :], OT[:, 4 * g:4 * g + 4, :], w=[free[n]])
        for _ in range(3):
            split_next()

    def project(c0, src, src_toks, gcols, order=range(KT)):
        toks = []
        for n2 in range(4):
            bank = 4 + n2
            wait("pe", free[bank])
            for j in range(2):
                pe = out_tile(PS[:, bank, j * 256:(j + 1) * 256], src, src_toks, order)
            for j in range(2):
                toks.append(add_branch(2 * n2 + j, PS[:, bank, j * 256:(j + 1) * 256], gcols[:, 2 * n2 + j:2 * n2 + j + 1], pe))
            free[bank] = toks[-1]
        return toks

    for n in range(6):
        plan += weights(c_now + n)
    ada_bias(16, 24, "ada_b", 16)
    G1 = MISC[:, 96:104]
    V(vv.tensor_scalar, G1, MOD[:, 16:24], 1.0, None, ALU.add)
    xt = project(c_now, OTS, [o_t] * KT, G1)
    c_now += 6
    clear_sums()
    layer_norm(0, xt, MOD[:, 32:40], MOD[:, 24:32], ALPHA, True)

    H1 = tuple(rounded("h1_" + n, aB + m * 1024, 1024).rearrange("p (a n) -> p a n", a=2) for m, n in enumerate(("high", "low")))
    R1 = view(aB + 2048, 1024).rearrange("p (a n) -> p a n", a=2)
    R2 = view(aB + 3072, 1024).rearrange("p (a n) -> p a n", a=2)

    def second_product(src_half, s_):
        for m in range(KT):
            ins = mm3(PS[:, 4 + m // 2, (m % 2) * 256:(m % 2 + 1) * 256], part(s_, m * P), src_half, False, False)
        return used(s_, ins)

    def mlp(c0, turns, ada_col, conds):
        per = {"pe": 8, "dve": 6 * len(conds), "act": 12, "pool": 0}
        junk = view(aB + 4096, 1024)

        def body(i):
            before = {n: last(n) for n in q.eng}
            ready[:] = carried(c0)
            plan.extend(weights(c0) + [("a", c0 + 1, ada_col, conds, junk)] + weights(c0 + 2)
                        + [("a", c0 + 3, ada_col + 2, conds, junk)] + weights(c0 + 4) + weights(c0 + 5))
            h_t = [None, None]
            for a in range(2):
                wait("pe", earlier(before["act"], 2))
                for j in range(2):
                    pe = out_tile(PS[:, a, j * 256:(j + 1) * 256], XIN)
                r = A(R1[:, a, :], PS[:, a, :], ACT.Relu, w=[pe, before["dve"]])
                v = V(vv.tensor_tensor, R2[:, a, :], R1[:, a, :], R1[:, a, :], ALU.mult, w=[r, before["act"]])
                h_t[a] = split_act(H1[0][:, a, :], H1[1][:, a, :], R2[:, a, :], w=[v, before["pe"]])
            for a in range(2):
                wait("pe", h_t[a])
                for j in range(2):
                    s_ = take()
                    second_product(both(H1, slice(None), a, slice(j * 256, (j + 1) * 256)), s_)
            while plan:
                split_next()
            carry_holds(c0)

        while plan:
            split_next()
        q.run_loop(turns, per, body)
        return c0 + 6 * turns

    no_pool_wait()
    GW = view(aB + 11264, NB * 4 * BW, BW).rearrange("p (b n) -> p b n", b=NB)
    s_gw = nc.alloc_semaphore("s_gw")
    nc.scalar.dma_start(GW, gw).then_inc(s_gw, 16)
    c_now = mlp(c_now, 8, 40, ((0, 0),))
    ada_bias(40, 32, "ada_b", 40)
    V(vv.tensor_scalar, G1, MOD[:, 40:48], 1.0, None, ALU.add)

    def evacuate(gcols):
        pe = last("pe")
        return [add_branch(n, PS[:, 4 + n // 2, (n % 2) * 256:(n % 2 + 1) * 256], gcols[:, n:n + 1], pe) for n in range(KT)]

    xt = evacuate(G1)
    out, xs = layer_norm(1, xt, MOD[:, 56:64], MOD[:, 48:56], ALPHA, True)

    no_pool_wait()
    pbt = lambda a, n, k: view(a, n, BW).rearrange("p (b t) -> p b t", b=k)
    pajdt = lambda a: view(a, 2048, BW).rearrange("p (a j d t) -> p a j d t", a=2, j=2, d=2)
    padt = lambda a: view(a, 1024, BW).rearrange("p (a d t) -> p a d t", a=2, d=2)
    GT, Y = pbt(aB, 4096, NB), pbt(aT1, 4096, NB)
    TLb, W2b, AAb = pajdt(aB + 4096), pajdt(aB + 6144), pajdt(aB + 8192)
    TAb, TIb, HSC = padt(aX + 2048), padt(aX + 3072), padt(aB + 10240)
    XP = view(aXL + 2048, 520, BW).rearrange("p (a t) -> p a t", a=2)
    XCV = pbt(aXL + 2048 + 520, 1024, 4)
    V(vv.memset, XP[:, :, 0:2], 0.0)
    V(vv.memset, XP[:, :, 258:260], 0.0)
    wait("pe", Tok(s_gw, 16, 0, None))
    free = [None] * 8
    xcv_t, xcv_read = {}, {}
    w_read = [None, None]

    def z_of(b):
        bank = b % 2
        wait("pe", free[bank])
        for j in range(2):
            s_ = take()
            for k in range(KT):
                wait("pe", out[k]) if b == 0 and j == 0 else None
                ins = mm3(PS[0:BW, bank, j * 256:(j + 1) * 256], part(s_, k * BW, BW), both(XIN, slice(None), k), k == 0, k == KT - 1)
            pe = used(s_, ins)
        a1 = A(XP[:, bank, 2:258], PS[0:BW, bank, 0:256], ACT.Copy, w=[pe, xcv_t.get(b - 2)])
        free[bank] = A(GT[:, b, :], PS[0:BW, bank, 256:512], ACT.Copy)
        xc = XCV[:, b % 4, :]
        V(vv.tensor_scalar, xc, XP[:, bank, 0:256], rp("cw", b), rp("cb", b), ALU.mult, ALU.add, w=[a1, xcv_read.get(b - 4)])
        for j in range(1, 4):
            V(vv.scalar_tensor_tensor, xc, XP[:, bank, j:j + 256], rp("cw", 16 * j + b), xc, ALU.mult, ALU.add)
        xcv_t[b] = last("dve")

    grp_tok = {}

    def gates_of(b):
        g, j = (b // 2) % 2, b % 2
        gb = 2 + 2 * (b % 2)
        wait("pe", xcv_t[b], free[gb], free[gb + 1])
        for d in range(2):
            for m in range(2):
                o = (2 * d + m) * BW
                ins = mm(PS[0:BW, gb + d, m * 256:(m + 1) * 256], GW[:, b, o:o + BW], XCV[:, b % 4, :], True, True)
        pe = done("pe", ins)
        s = b % 2
        for d in range(2):
            cc = 16 * d + b
            A(TAb[:, s, d, :], PS[0:BW, gb + d, 0:256], ACT.Tanh, scale=0.5, bias=hba[:, cc:cc + 1], w=[pe])
            A(TIb[:, s, d, :], PS[0:BW, gb + d, 256:512], ACT.Tanh, scale=0.5, bias=hbx[:, cc:cc + 1], w=[w_read[s]])
            free[gb + d] = last("act")
            A(TLb[:, g, j, d, :], TAb[:, s, d, :], ACT.Tanh, scale=cs[:, cc:cc + 1], bias=cs[:, cc:cc + 1], w=[grp_tok.get(b // 2 - 2)])
            A(AAb[:, g, j, d, :], TAb[:, s, d, :], ACT.Exp, scale=cs2[:, cc:cc + 1], bias=cs2[:, cc:cc + 1])
        a = last("act")
        AA, W2 = AAb[:, g, j, :, :], W2b[:, g, j, :, :]
        w_read[s] = V(vv.scalar_tensor_tensor, W2, TIb[:, s, :, :], 1.0, XCV[:, b % 4, :].unsqueeze(1).broadcast_to([BW, 2, S]), ALU.add, ALU.mult, w=[a])
        V(vv.scalar_tensor_tensor, W2, AA, 1.0, W2, ALU.add, ALU.mult)
        xcv_read[b] = last("dve")

    hsc_free = [None, None]
    s_late, s_cc = nc.alloc_semaphore("s_late"), nc.alloc_semaphore("s_cc")

    def scan_pair(gi):
        g = gi % 2
        a = A(TLb[:, g, :, :, :], TLb[:, g, :, :, :], ACT.Sqrt, scale=0.25)
        V(vv.tensor_tensor, W2b[:, g, :, :, :], W2b[:, g, :, :, :], TLb[:, g, :, :, :], ALU.mult, w=[a])
        for j in range(2):
            b = 2 * gi + j
            V(vv.tensor_tensor_scan, HSC[:, j, 0, :], AAb[:, g, j, 0, :], W2b[:, g, j, 0, :], 0.0, ALU.mult, ALU.add, w=[hsc_free[j]])
            V(vv.tensor_tensor_scan, HSC[:, j, 1, ::-1], AAb[:, g, j, 1, ::-1], W2b[:, g, j, 1, ::-1], 0.0, ALU.mult, ALU.add)
            hsc_free[j] = G(nc.gpsimd.tensor_tensor, Y[:, b, :], HSC[:, j, 0, :], HSC[:, j, 1, :], ALU.add, w=[last("dve")])
        grp_tok[gi] = last("dve")

    pj = PS[:, 6:8, :].rearrange("p b n -> p (b n)")
    n_ada = 0
    for b in range(2, NB):
        plan += weights(c_now)
        c_now += 1
        if n_ada < 12:
            plan.append(("a", c_now, 72 + 2 * n_ada, ((0, 0),), pj))
            c_now += 1
            n_ada += 1
    for n in range(10):
        plan += weights(c_now)
        c_now += 1
    wait("dve", silu_c2)
    def gated(half, bs, last_use):
        a = A(GT[:, bs, :], GT[:, bs, :], ACT.Gelu_apprx_tanh)
        v = V(vv.tensor_tensor, Y[:, bs, :], Y[:, bs, :], GT[:, bs, :], ALU.mult, w=[a, last("pool")])
        o = slice(bs.start - 8 * half, bs.stop - 8 * half)
        return split_act(YS_[half][0][:, o, :], YS_[half][1][:, o, :], Y[:, bs, :], w=[v, last_use])

    def out_of(half, bs, y_t):
        for b in range(bs.start, bs.stop):
            s_ = take()
            wait("pe", y_t)
            for m in range(KT):
                ins = mm3(PS[:, 4 + m // 2, (m % 2) * 256:(m % 2 + 1) * 256], part(s_, m * P, P, BW), both(YS_[half], slice(None), b - 8 * half), False, False)
            used(s_, ins)

    z_of(0)
    z_of(1)
    for b in range(NB):
        gates_of(b)
        if b % 2 == 0 and b >= 2:
            scan_pair(b // 2 - 1)
        if b + 2 < NB:
            z_of(b + 2)
    YS_ = [tuple(rounded("y_" + n, a, 2048, BW).rearrange("p (b t) -> p b t", b=8) for n, a in m)
           for m in ((("high0", aX), ("low0", aXL)), (("high1", aKF), ("low1", aB + 11264)))]
    z_read, gates_read = last("pe"), last("act")
    quad = [slice(4 * n, 4 * n + 4) for n in range(4)]
    y_t = [gated(0, quad[n], z_read) for n in range(2)]
    scan_pair(NB // 2 - 1)
    clear_sums(gates_read)
    nc.scalar.dma_start(CB[:, 0, :], cvec[2:3, :].broadcast_to([P, D])).then_inc(s_cc, 16)
    for n in range(2):
        out_of(0, quad[n], y_t[n])
    for n in range(2, 4):
        out_of(1, quad[n], gated(1, quad[n], None))

    ada_bias(72, 24, "ada_b", 72)
    A(CB[:, 0, :], CB[:, 0, :], ACT.Silu, w=[Tok(s_cc, 16, 0, None)])
    V(vv.tensor_scalar, G1, MOD[:, 64:72], 1.0, None, ALU.add)
    xt = evacuate(G1)
    clear_sums()
    layer_norm(2, xt, MOD[:, 80:88], MOD[:, 72:80], ALPHA, True)

    POS, CTX = kt(view(aB + 8192, 2048)), kt(view(aB + 10240, 2048))
    nc.scalar.dma_start(CTX, ctxT).then_inc(s_late, 16)
    nc.scalar.dma_start(POS, posT).then_inc(s_late, 16)
    nc.scalar.dma_start(TAB2, tab2).then_inc(s_late, 16)
    LATE = Tok(s_late, 48, 0, None)

    def rms_rows(src, w, xnorm, n=KT, m=D, sq=None):
        sq = T2 if sq is None else sq
        for k in range(0, n, 2):
            a = A(sq[:, k:k + 2, :], src[:, k:k + 2, :], ACT.Square, w=w if len(w) == 1 else [w[k + 1]])
            wait("pe", a)
            for kk in (k, k + 1):
                ins = mm(VAR, ONES, sq[:, kk, :], kk == 0, kk == n - 1)
        pe = done("pe", ins)
        root(RSTD, VAR, 1.0 / m, par_("eps6"), [pe])
        return V(vv.tensor_tensor, xnorm, src, RSTD.unsqueeze(1).broadcast_to([P, n, S]), ALU.mult)

    no_pool_wait()
    c_now = mlp(c_now, 4, 96, ((1, 0), (0, 48)))
    sc2 = combo[:, 0:8]

    def modulate_norm(xnorm, gname, shift, scale, s_=0):
        V(vv.tensor_scalar, sc2, MOD[:, scale:scale + 8], 1.0, None, ALU.add)
        V(vv.tensor_tensor, sc2, sc2, par_(gname, 0, 8), ALU.mult)
        return modulated(xnorm, sc2, MOD[:, shift:shift + 8], s_)

    wait("dve", LATE)
    wait("pe", LATE)
    wait("act", LATE, last("dve"))
    ada_bias(144, 16, "ada_b2", 0)
    rms_rows(CTX, [last("dve")], CTX)
    modulate_norm(CTX, "n1g", 144, 152, 1)
    c_now = mlp(c_now, 4, 112, ((1, 0),))
    V(vv.tensor_scalar, G1, MOD[:, 88:96], 1.0, None, ALU.add)
    ada_bias(96, 32, "ada_b2", 0)
    xt = evacuate(G1)
    layer_norm(3, xt, None, None, 1.0, False)

    xt = []
    for k in range(0, KT, 2):
        xt += [V(vv.tensor_tensor, X[:, k:k + 2, :], X[:, k:k + 2, :], POS[:, k:k + 2, :], ALU.add)] * 2
    rms_rows(X[:, :, :], xt, XC[:, :, :])
    htok = modulate_norm(XC, "n1g", 96, 104, 0)
    all_wait()
    Fg = view(aB, 4096).rearrange("p (n t) -> p n t", n=8)
    Vv = view(aB + 4096, 2048).rearrange("p (b n) -> p b n", b=4)
    ZP = view(aB + 6144, 1548).rearrange("p (n t) -> p n t", n=6)
    Q = view(aC, 1024)
    FZ = view(aC + 1024, 512).rearrange("p (n t) -> p n t", n=2)
    Gg = view(aT2 + 1024, 1024)
    SG = view(aB + 10240, 1024).rearrange("p (a n) -> p a n", a=2)
    V(vv.memset, ZP[:, :, 0:1], 0.0)
    zp_t = [None] * 3
    zp_edges = V(vv.memset, ZP[:, :, 257:258], 0.0)
    for n in range(2, 14):
        plan += weights(c_now)
        c_now += 1
        if n < 10:
            plan.append(("a", c_now, 128 + 2 * (n - 2), ((1, 0),), view(aT2, 1024)))
            c_now += 1
    for n in range(6):
        plan += weights(c_now)
        c_now += 1
    LB = MISC[:, 128:152]
    lbr = par_("lb", 0, 8)
    V(vv.tensor_tensor, LB[:, 0:8], lbr, lbr, ALU.subtract)
    A(LB[:, 0:8], LB[:, 0:8], ACT.Exp, w=[last("dve")])
    V(vv.reciprocal, LB[:, 8:16], LB[:, 0:8], w=[last("act")])
    V(vv.tensor_tensor, LB[:, 0:8], LB[:, 0:8], LB[:, 8:16], ALU.mult)
    V(vv.tensor_tensor, LB[:, 0:8], LB[:, 0:8], LB[:, 0:8], ALU.subtract)
    V(vv.tensor_scalar, LB[:, 8:16], LB[:, 0:8], -1.0, 1.0, ALU.mult, ALU.add)
    def sin_of(dst, ps, bcol, frcol, tmp, w):
        TP = 2 * math.pi
        HI = float(np.float32(6.28125))
        V(vv.tensor_scalar, dst, ps, bcol, frcol, ALU.add, ALU.mult, w=w)
        V(vv.tensor_scalar, tmp, dst, 1.0 / TP, 12582912.0, ALU.mult, ALU.add)
        V(vv.tensor_scalar, tmp, tmp, 12582912.0, None, ALU.subtract)
        V(vv.scalar_tensor_tensor, dst, tmp, -HI, dst, ALU.mult, ALU.add)
        V(vv.scalar_tensor_tensor, dst, tmp, -(TP - HI), dst, ALU.mult, ALU.add)
        V(vv.tensor_scalar, dst, dst, math.pi, -math.pi, ALU.min, ALU.max)
        return A(dst, dst, ACT.Sin, w=[last("dve")])

    fp = lambda n: FPAR[:, FCOL[n][0]:FCOL[n][1]]
    aF = aB + 7696
    FPAR = view(aF, FN, 64)
    s_f = nc.alloc_semaphore("s_f")
    nc.scalar.dma_start(FPAR, fpar).then_inc(s_f, 16)
    h1, tmp1, h2 = view(aF + 1160, 256, 64), view(aF + 1416, 256, 64), view(aF + 1672, 256, 64)
    HS = view(aT1, 1024).rearrange("p (o b c) -> p o b c", o=2, b=2)
    HD = view(aT1 + 1024, 1024).rearrange("p (o b c) -> p o b c", o=2, b=2)
    ht = view(aF + 1928, 512)
    KFv = KF.rearrange("p (o r f c) -> p o r f c", o=2, r=2, f=2)

    def filters():
        wait("pe", Tok(s_f, 16, 0, None))
        wait("dve", Tok(s_f, 16, 0, None))
        t = done("pe", mm(PS[0:64, 4, 0:256], fp("w1")[0:33, :], tab_("zf", 33), True, True))
        t = sin_of(h1, PS[0:64, 4, 0:256], fp("b1"), fp("fr"), tmp1, [t])
        yield
        wait("pe", t)
        t = done("pe", mm(PS[0:64, 5, 0:256], fp("w2"), h1, True, True))
        t = sin_of(h2, PS[0:64, 5, 0:256], fp("b2"), fp("fr"), tmp1, [t])
        yield
        wait("pe", t)
        for o in range(2):
            for b in range(2):
                pe = done("pe", mm(PS[:, 4 + 2 * o + b, :], h2[:, b * P:(b + 1) * P], fp("w3")[:, o * 512:(o + 1) * 512], True, True))
                V(vv.tensor_tensor, ht[:, 0:256], PS[:, 4 + 2 * o + b, 0:256], tab_("decf")[:, b * 256:(b + 1) * 256], ALU.mult, w=[pe])
                V(vv.tensor_tensor, ht[:, 256:512], PS[:, 4 + 2 * o + b, 256:512], tab_("decb")[:, b * 256:(b + 1) * 256], ALU.mult)
                V(vv.tensor_tensor, HS[:, o, b, :], ht[:, 0:256], ht[:, 256:512], ALU.add)
                V(vv.tensor_tensor, HD[:, o, b, :], ht[:, 0:256], ht[:, 256:512], ALU.subtract)
                yield
        wait("pe", last("dve"))
        for o in range(2):
            for r, (tb_, src) in enumerate((("dc", HS), ("ds", HD))):
                for f in range(2):
                    for b in range(2):
                        ins = mm(PS[:, 4 + 2 * o + r, f * 256:(f + 1) * 256],
                                 tab_(tb_)[:, b * 256 + f * P:b * 256 + (f + 1) * P], src[:, o, b, :], b == 0, b == 1)
                pe = done("pe", ins)
                A(KFv[:, o, r, :, :], PS[:, 4 + 2 * o + r, :].rearrange("p (f c) -> p f c", f=2), ACT.Copy, w=[pe])
            yield

    free = [None] * 8
    steps = filters()
    for t in range(8):
        bank = t % 4
        wait("pe", free[bank])
        s_ = take()
        for k in range(KT):
            ins = mm3(PS[:, bank, :].rearrange("p (s t) -> p s t", s=2), part(s_, k * P), (XH[:, :, k, :], XL[:, :, k, :]), k == 0, k == KT - 1)
        pe = used(s_, ins)
        free[bank] = A(Fg[:, t, :], PS[:, bank, :], ACT.Sigmoid, w=[pe])
        V(vv.tensor_scalar, Fg[:, t, :], Fg[:, t, :], LB[:, 8 + t:9 + t], LB[:, t:t + 1], ALU.mult, ALU.add, w=[free[bank]])
        if t > 0:
            next(steps, None)
            if t > 4:
                next(steps, None)
    for _ in steps:
        pass
    wait("pe", last("act"))
    for half in range(4):
        s_ = take()
        for b in range(4):
            for k in range(2):
                kk = 2 * half + k
                x_ = tuple(t[:, b // 2, kk, (b % 2) * P:(b % 2 + 1) * P] for t in (XH, XL))
                ins = mm3(PS[:, 4 + b, :], x_, part(s_, k * 512, 512), kk == 0, kk == KT - 1)
        pe = used(s_, ins)
    for b in range(4):
        free[4 + b] = A(Vv[:, b, :], PS[:, 4 + b, :], ACT.Copy, w=[pe])

    def in_tiles(bank):
        wait("pe", free[bank])
        for j in range(2):
            pe = out_tile(PS[:, bank, j * 256:(j + 1) * 256], XIN)
        return pe

    ZERO = RS[:, 256:512]
    V(vv.memset, ZERO, 0.0)
    R = view(aX + 2048, 2048).rearrange("p (n t) -> p n t", n=8)
    KC = view(aX + 6144, 2048).rearrange("p (n t) -> p n t", n=8)
    KCT = view(aB + 7696, 2048).rearrange("p (n d) -> p n d", n=16)
    ST = view(aX + 6144, 1024).rearrange("p (n v) -> p n v", n=8)

    v_read = last("pe")

    def context():
        V(vv.tensor_scalar, KC[:, :, :], Fg[:, :, S:2 * S], -1.0, 1.0, ALU.mult, ALU.add, w=[v_read])
        yield
        for n in range(8):
            f = Fg[:, n, S:2 * S]
            if n < 4:
                V(vv.tensor_tensor_scan, R[:, n, ::-1], Fg[:, n, 2 * S - 1:S - 1:-1], ZERO, 1.0, ALU.mult, ALU.add)
            else:
                V(vv.tensor_tensor_scan, R[:, n, :], f, ZERO, 1.0, ALU.mult, ALU.add)
            if n == 3:
                yield
        V(vv.tensor_tensor, KC[:, 0:4, 0:S - 1], KC[:, 0:4, 0:S - 1], R[:, 0:4, 1:S], ALU.mult)
        v = V(vv.tensor_tensor, KC[:, 4:8, 1:S], KC[:, 4:8, 1:S], R[:, 4:8, 0:S - 1], ALU.mult)
        yield
        wait("pe", v)
        for n in range(16):
            ins = nc.tensor.transpose(PS[:, 4 + n // 4, (n % 4) * P:(n % 4 + 1) * P], KC[:, n // 2, (n % 2) * P:(n % 2 + 1) * P], ident)
        pe = done("pe", ins)
        for b in range(4):
            a = A(KCT[:, 4 * b:4 * b + 4, :], PS[:, 4 + b, :].rearrange("p (n d) -> p n d", n=4), ACT.Copy, w=[pe])
        yield
        wait("pe", a)
        for n in range(8):
            for b in range(2):
                ins = mm(PS[:, 4 + n // 4, (n % 4) * P:(n % 4 + 1) * P], KCT[:, 2 * n + b, :], Vv[:, 2 + b, (n % 4) * P:(n % 4 + 1) * P], b == 0, b == 1)
        pe = done("pe", ins)
        a = A(ST[:, :, :], PS[:, 4:6, :].rearrange("p b (n v) -> p (b n) v", n=4), ACT.Copy, w=[pe])


    U = kt(view(aX + 2048, 1536), 6)

    def short_conv():
        for n in range(6):
            V(vv.tensor_scalar, U[:, n, :], ZP[:, n, 0:256], par_("hycw", n), par_("hycb", n), ALU.mult, ALU.add, w=[zp_t[n // 2]])
            for j in (1, 2):
                V(vv.scalar_tensor_tensor, U[:, n, :], ZP[:, n, j:j + 256], par_("hycw", 6 * j + n), U[:, n, :], ALU.mult, ALU.add)
            if n % 2:
                yield

    steps = itertools.chain(context(), short_conv())
    for n in range(2):
        pe = in_tiles(n)
        a = A(SG[:, n, :], PS[:, n, :], ACT.Sigmoid, w=[pe])
        free[n] = q_t = V(vv.scalar_tensor_tensor, Q[:, n * 512:(n + 1) * 512], PS[:, n, :], P ** -0.5, SG[:, n, :], ALU.mult, ALU.mult, w=[a])
    for n in range(3):
        next(steps, None)
        pe = in_tiles(2 + n % 2)
        free[2 + n % 2] = zp_t[n] = A(ZP[:, 2 * n:2 * n + 2, 1:257], PS[:, 2 + n % 2, :].rearrange("p (n t) -> p n t", n=2), ACT.Copy, w=[pe, zp_edges])
    for n in range(2):
        next(steps, None)
        next(steps, None)
        pe = in_tiles(n)
        a = A(SG[:, n, :], PS[:, n, :], ACT.Sigmoid, w=[pe, q_t])
        free[n] = V(vv.tensor_tensor, Gg[:, n * 512:(n + 1) * 512], PS[:, n, :], SG[:, n, :], ALU.mult, w=[a])
    pe = in_tiles(3)
    for _ in steps:
        pass
    fz_t = free[3] = A(FZ[:, :, :], PS[:, 3, :].rearrange("p (n t) -> p n t", n=2), ACT.Copy, w=[pe])

    all_wait()
    VT2 = view(aX + 3584, 512).rearrange("p (b c) -> p b c", b=2)
    YS = view(aB + 2048, 1024).rearrange("p (r n) -> p r n", r=2)
    M1, M2, YV = view(aB + 3072, 512), view(aB + 3584, 512), kt(view(aC + 1536, 512), 2)
    FA = view(aX + 7168, 1024).rearrange("p (b n) -> p b n", b=2)
    FY = kt(view(aT2 + 512, 512), 2)
    SQ2 = kt(view(aT2, 512), 2)
    MIX = T1
    KX = view(aB + 7696, 2048)
    KFx, KBx = KX[:, 0:1024], KX[:, 1024:2048]
    PF, SF, SBk, PBk = (view(a, 1024) for a in (aX, aX + 1024, aB, aB + 1024))
    QP, KP = view(aX + 4096, 1024), view(aX + 5120, 1024)
    QKP = ((QP, KP), (view(aT1 + 512, 1024), view(aTab2 + T2COL["decf"][0], 1024)))
    ATD = view(aB + 10240, 1024).rearrange("p (n t) -> p n t", n=8)
    ATO = view(aB + 11264, 1024).rearrange("p (n t) -> p n t", n=8)
    h4 = lambda ap: ap.rearrange("p (h t) -> p h t", h=4)
    G(nc.gpsimd.memset, SF, 1.0)
    pf_t = A(h4(PF), Fg[:, 0:4, 0:S], ACT.Copy)
    V(vv.tensor_scalar, h4(KFx), Fg[:, 0:4, 0:S], -1.0, 1.0, ALU.mult, ALU.add)
    kfx_t = last("dve")
    V(vv.tensor_scalar, h4(KBx), Fg[:, 4:8, 0:S], -1.0, 1.0, ALU.mult, ALU.add)
    a = A(h4(SBk), Fg[:, 4:8, 0:S], ACT.Copy, w=[kfx_t])
    G(nc.gpsimd.memset, PBk, 1.0, w=[pf_t, kfx_t])
    wait("dve", a, last("pool"))
    started = last("dve")
    halves = lambda ap, n: ap.rearrange("p (g s t) -> p g s t", s=2, t=n)

    def hyena_and_fourier():
        y_in, y_t = U[:, 0:2, :], last("dve")
        for o in range(2):
            yield
            wait("pe", y_t)
            for b in range(2):
                for n in range(2):
                    ins = nc.tensor.transpose(PS[:, 0, b * 256 + n * P:b * 256 + (n + 1) * P], y_in[:, n, b * P:(b + 1) * P], ident)
            pe = done("pe", ins)
            yield
            a = A(VT2[:, :, :], PS[:, 0, :].rearrange("p (b c) -> p b c", b=2), ACT.Copy, w=[pe])
            yield
            wait("pe", a)
            for r, tb_ in enumerate(("dc", "ds")):
                for f in range(2):
                    for b in range(2):
                        ins = mm(PS[:, 1 + r, f * 256:(f + 1) * 256], tab_(tb_)[:, b * 256 + f * P:b * 256 + (f + 1) * P], VT2[:, b, :], b == 0, b == 1)
            pe = done("pe", ins)
            yield
            kr, ks = KFv[:, o, 0, :, :].rearrange("p f c -> p (f c)"), KFv[:, o, 1, :, :].rearrange("p f c -> p (f c)")
            V(vv.tensor_tensor, M1, PS[:, 1, :], kr, ALU.mult, w=[pe])
            V(vv.tensor_tensor, M2, PS[:, 2, :], ks, ALU.mult)
            V(vv.tensor_tensor, YS[:, 0, :], M1, M2, ALU.subtract)
            V(vv.tensor_tensor, M1, PS[:, 1, :], ks, ALU.mult)
            V(vv.tensor_tensor, M2, PS[:, 2, :], kr, ALU.mult)
            v = V(vv.tensor_tensor, YS[:, 1, :], M1, M2, ALU.add)
            yield
            wait("pe", v)
            for n in range(2):
                for r, tb_ in enumerate(("ic", "is")):
                    for f in range(2):
                        ins = mm(PS[:, 3, n * 256:(n + 1) * 256], YS[:, r, f * 256 + n * P:f * 256 + (n + 1) * P], tab_(tb_)[:, f * 256:(f + 1) * 256],
                                 r == 0 and f == 0, r == 1 and f == 1)
            pe = done("pe", ins)
            yield
            for n in range(2):
                V(vv.scalar_tensor_tensor, YV[:, n, :], y_in[:, n, :], par_("hybias", 2 * o + n), PS[:, 3, n * 256:(n + 1) * 256], ALU.mult, ALU.add, w=[pe])
            y_t = V(vv.tensor_tensor, YV[:, :, :], YV[:, :, :], U[:, 2 + 2 * o:4 + 2 * o, :], ALU.mult)
            y_in = YV
        yield
        rms_rows(YV[:, :, :], [y_t], YV[:, :, :], 2, 256, SQ2)
        for n in range(2):
            V(vv.tensor_scalar, MIX[:, n, :], YV[:, n, :], par_("hyg", n), None, ALU.mult)

        yield
        wait("pe", fz_t, last("dve"))
        for b in range(2):
            for n in range(2):
                for r, tb_ in enumerate(("fcc", "fcs")):
                    ins = mm(PS[:, r, b * 256 + n * P:b * 256 + (n + 1) * P], FZ[:, n, b * P:(b + 1) * P], tab_(tb_), True, True)
        pe = done("pe", ins)
        yield
        for r in range(2):
            a = A(FA[:, r, :], PS[:, r, :], ACT.Copy, w=[pe])
        yield
        wait("pe", a)
        for n in range(2):
            for r, tb_ in enumerate(("flc", "fls")):
                for b in range(2):
                    ins = mm(PS[:, 2, n * 256:(n + 1) * 256], FA[:, r, b * 256 + n * P:b * 256 + (n + 1) * P], tab_(tb_)[:, b * 256:(b + 1) * 256],
                             r == 0 and b == 0, r == 1 and b == 1)
        pe = done("pe", ins)
        yield
        a = A(FY[:, :, :], PS[:, 2, :].rearrange("p (n t) -> p n t", n=2), ACT.Copy, w=[pe])
        yield
        wait("pe", a)
        for n in range(2):
            ins = mm(PS[:, 3, n * 256:(n + 1) * 256], par_("fnw", n * P, P), FY[:, n, :], True, True)
        pe = done("pe", ins)
        yield
        for n in range(2):
            v = V(vv.tensor_scalar, FZ[:, n, :], PS[:, 3, n * 256:(n + 1) * 256], par_("fnb", n), None, ALU.add, w=[pe])
        yield
        rms_rows(FZ[:, :, :], [v], FZ[:, :, :], 2, 256, SQ2)
        for n in range(2):
            V(vv.tensor_scalar, MIX[:, 6 + n, :], FZ[:, n, :], par_("fng", n), None, ALU.mult)


    def pick(lev, b0, pe):
        mask = tab_("lmask")[:, (lev % 8) * P:(lev % 8 + 1) * P].unsqueeze(1).broadcast_to([P, 8, P])
        data = PS[:, b0:b0 + 2, :].rearrange("p b (n t) -> p (b n) t", n=4)
        if lev == 0:
            V(vv.tensor_tensor, ATD[:, :, :], data, mask, ALU.mult, w=[pe])
        elif lev < 8:
            V(vv.copy_predicated, ATD[:, :, :], mask.bitcast(U32), data, w=[pe])
        else:
            V(vv.tensor_copy, ATO[:, :, :], data, w=[pe])

    MXS = (kt(rounded("mix_high", aB, 2048)), kt(rounded("mix_low", aB + 2048, 2048)))
    m_t = [None] * KT
    read_t = []

    def to_output(k, v):
        t = split_act(MXS[0][:, k, :], MXS[1][:, k, :], MIX[:, k, :], w=[v])
        for n in range(k.start, k.stop):
            m_t[n] = t

    def levels():
        used_by, updated, pending = [None, None], started, None
        for lev in range(9):
            QPl, KPl = QKP[(lev + 1) % 2]
            free_ = used_by[(lev + 1) % 2]
            n = 1 << max(lev - 1, 0)
            l = lambda ap: halves(ap, n)[:, :, 0, :]
            r = lambda ap: halves(ap, n)[:, :, 1, :]
            if lev == 0:
                v = kp_t = V(vv.tensor_tensor, KPl, KFx, KBx, ALU.add)
                qp = Q
            else:
                G(nc.gpsimd.tensor_tensor, l(KPl), l(KFx), l(SF), ALU.mult, w=[free_, updated])
                kp_t = G(nc.gpsimd.tensor_tensor, r(KPl), r(KBx), r(PBk), ALU.mult)
                V(vv.tensor_tensor, r(QPl), r(Q), r(PF), ALU.mult, w=[free_])
                v = V(vv.tensor_tensor, l(QPl), l(Q), l(SBk), ALU.mult)
                qp = QPl
                yield
            wait("pe", v, kp_t)
            b0 = 4 + 2 * (lev % 2)
            for h in range(4):
                for b in range(2):
                    s_b = b if lev < 8 else 1 - b
                    ins = mm(PS[:, b0 + h // 2, ((h % 2) * 2 + b) * P:((h % 2) * 2 + b + 1) * P],
                             KPl[:, h * S + s_b * P:h * S + (s_b + 1) * P], qp[:, h * S + b * P:h * S + (b + 1) * P], True, True)
            pe = used_by[(lev + 1) % 2] = done("pe", ins)
            if lev > 0:
                shape = [P, 1024 // (2 * n), n]
                if lev < 8:
                    V(vv.tensor_tensor, l(SF), l(SF), r(PF)[:, :, n - 1:n].broadcast_to(shape), ALU.mult, w=[kp_t])
                    updated = V(vv.tensor_tensor, r(PBk), r(PBk), l(SBk)[:, :, 0:1].broadcast_to(shape), ALU.mult)
                V(vv.tensor_tensor, r(PF), r(PF), l(PF)[:, :, n - 1:n].broadcast_to(shape), ALU.mult)
                V(vv.tensor_tensor, l(SBk), l(SBk), r(SBk)[:, :, 0:1].broadcast_to(shape), ALU.mult)
            yield
            if pending:
                pick(*pending)
                yield
            pending = (lev, b0, pe)
        level_pe = used_by[0]
        pick(*pending)
        V(vv.tensor_tensor, QP, Q, PF, ALU.mult, w=[level_pe])
        v = V(vv.tensor_tensor, KP, Q, SBk, ALU.mult)
        yield
        wait("pe", v)
        for h in range(4):
            for b in range(2):
                o = PS[:, 4 + h // 2, ((h % 2) * 2 + b) * P:((h % 2) * 2 + b + 1) * P]
                mm(o, Vv[:, b, h * P:(h + 1) * P], ATD[:, 2 * h + b, :], True, False)
                mm(o, Vv[:, 1 - b, h * P:(h + 1) * P], ATO[:, 2 * h + b, :], False, False)
                mm(o, ST[:, h, :], QP[:, h * S + b * P:h * S + (b + 1) * P], False, False)
                ins = mm(o, ST[:, 4 + h, :], KP[:, h * S + b * P:h * S + (b + 1) * P], False, True)
        pe = done("pe", ins)
        ob = PS[:, 4:6, :].rearrange("p b n -> p (b n)")
        a = A(QP, ob, ACT.Square, w=[pe])
        read_t[:] = [V(vv.tensor_copy, KP, ob, w=[a])] * 2
        yield
        wait("pe", a)
        for h2_ in range(2):
            ins = mm(PS[:, 6 + h2_, :], ONES, QP[:, h2_ * 512:(h2_ + 1) * 512], True, True)
        pe = done("pe", ins)
        rb = PF
        yield
        A(rb, PS[:, 6:8, :].rearrange("p b n -> p (b n)"), ACT.Sqrt, w=[pe], scale=1.0 / P, bias=par_("eps6"))
        read_t.extend([last("act")] * 2)
        for h in range(4):
            hs = slice(h * S, (h + 1) * S)
            V(vv.reciprocal, rb[:, hs], rb[:, hs], w=[last("act")] if h == 0 else [])
            V(vv.tensor_tensor, KP[:, hs], KP[:, hs], rb[:, hs], ALU.mult)
            v = V(vv.scalar_tensor_tensor, MIX[:, 2 + h, :], KP[:, hs], par_("hgg", h), Gg[:, hs], ALU.mult, ALU.mult)
            to_output(slice(2 + h, 3 + h), v)

    ahead = levels()
    next(ahead)
    for _ in hyena_and_fourier():
        next(ahead, None)
    for _ in ahead:
        pass
    to_output(slice(0, 2), last("dve"))
    to_output(slice(6, 8), last("dve"))
    free = [None] * 4 + read_t
    ada_bias(128, 16, "ada_b2", 32)
    xt = project(c_now, MXS, m_t, MOD[:, 112:120], (2, 3, 4, 5, 0, 1, 6, 7))
    rms_rows(X[:, :, :], xt, XC[:, :, :])
    htok = modulate_norm(XC, "n2g", 120, 128, 0)
    HM = T2

    all_wait()
    COMB = view(aB, 4096).rearrange("p (e t) -> p e t", e=NE)
    SEL = view(aB + 4096, 2048, NE)
    s_sel = nc.alloc_semaphore("s_sel")
    nc.scalar.dma_start(SEL, sel).then_inc(s_sel, 16)

    def router():
        for b in range(2):
            for k in range(KT):
                ins = mm(PS[:, 4 + b, 0:NE], HM[:, k, b * P:(b + 1) * P], par_("rw", k * NE, NE), k == 0, k == KT - 1)
        pe = done("pe", ins)
        yield
        ROUT = view(aB + 6144, 1024)

        def r3(j, n=16):
            return ROUT[:, 64 * j:64 * j + 2 * n].rearrange("p (b e) -> p b e", b=2)

        PR, SE, ML, EX, E2 = r3(0), r3(1), r3(2), r3(3), r3(4)
        st = ROUT[:, 512:512 + 64]
        mx = st[:, 0:2]
        V(vv.tensor_reduce, mx, PS[:, 4:6, 0:NE], AX, ALU.max, w=[pe])
        V(vv.tensor_scalar, mx, mx, -1.0, None, ALU.mult)
        for b in range(2):
            a = A(PR[:, b, :], PS[:, 4 + b, 0:NE], ACT.Exp, bias=st[:, b:b + 1], accum_out=st[:, 2 + b:3 + b], w=[last("dve")])
        V(vv.reciprocal, st[:, 4:6], st[:, 2:4], w=[a])
        V(vv.tensor_tensor, PR, PR, st[:, 4:6].unsqueeze(2).broadcast_to([P, 2, NE]), ALU.mult)
        V(vv.tensor_tensor, SE, PR, par_("rb", 0, 16).unsqueeze(1).broadcast_to([P, 2, NE]), ALU.add)
        yield
        g4 = ROUT[:, 64:64 + 32].rearrange("p (g e) -> p g e", e=4)
        GS, GT2 = ROUT[:, 320:320 + 8], ROUT[:, 352:352 + 16].rearrange("p (g e) -> p g e", e=2)
        pairs = [(g4[:, :, 0:4:2], g4[:, :, 1:4:2]), (g4[:, :, 0:2], g4[:, :, 2:4]), (g4[:, :, 0:2], g4[:, :, 3:1:-1])]
        for j, (a_, b_) in enumerate(pairs):
            V(vv.tensor_tensor, GT2, a_, b_, ALU.add)
            dst = GS if j == 0 else st[:, 8:16]
            V(vv.tensor_reduce, dst, GT2, AX, ALU.max)
            if j:
                V(vv.tensor_tensor, GS, GS, dst, ALU.max)

        def first_max(val, n, onehot, m, tmp, rows=2):
            V(vv.tensor_reduce, m, val, AX, ALU.max)
            V(vv.tensor_tensor, onehot, val, m.unsqueeze(2).broadcast_to([P, rows, n]), ALU.is_ge)
            io = tab_("iota")[:, 0:n].unsqueeze(1).broadcast_to([P, rows, n])
            V(vv.scalar_tensor_tensor, tmp, onehot, -100.0, io, ALU.mult, ALU.add)
            V(vv.tensor_reduce, m, tmp, AX, ALU.min)
            V(vv.tensor_tensor, onehot, tmp, m.unsqueeze(2).broadcast_to([P, rows, n]), ALU.is_equal)

        G3 = GS.rearrange("p (b g) -> p b g", b=2)
        GO, GTm = st[:, 16:24].rearrange("p (b g) -> p b g", b=2), st[:, 24:32].rearrange("p (b g) -> p b g", b=2)
        yield
        first_max(G3, 4, GO, st[:, 32:34], GTm)
        GM = ROUT[:, 600:600 + 32].rearrange("p (g e) -> p g e", e=4)
        V(vv.tensor_copy, GM, st[:, 16:24].unsqueeze(2).broadcast_to([P, 8, 4]))
        NG = ROUT[:, 640:640 + 32]
        V(vv.tensor_tensor, ML.rearrange("p b e -> p (b e)"), ROUT[:, 64:64 + 32], ROUT[:, 600:600 + 32], ALU.mult)
        V(vv.tensor_scalar, NG, ROUT[:, 600:600 + 32], 1e30, -1e30, ALU.mult, ALU.add)
        V(vv.tensor_tensor, ROUT[:, 128:128 + 32], ROUT[:, 128:128 + 32], NG, ALU.add)
        TM = ROUT[:, 700:700 + 32].rearrange("p (b e) -> p b e", b=2)
        yield
        first_max(ML, NE, EX, st[:, 34:36], TM)
        V(vv.scalar_tensor_tensor, ML, EX, -3e30, ML, ALU.mult, ALU.add)
        yield
        first_max(ML, NE, E2, st[:, 36:38], TM)
        yield
        V(vv.tensor_tensor, EX, EX, E2, ALU.add)
        V(vv.tensor_tensor, EX, EX, PR, ALU.mult)
        V(vv.tensor_reduce, st[:, 38:40], EX, AX, ALU.add)
        V(vv.reciprocal, st[:, 40:42], st[:, 38:40])
        v = V(vv.tensor_tensor, EX, EX, st[:, 40:42].unsqueeze(2).broadcast_to([P, 2, NE]), ALU.mult)
        yield
        wait("pe", v, Tok(s_sel, 16, 0, None))
        for b in range(2):
            ins = nc.tensor.transpose(PS[0:NE, 6, b * P:(b + 1) * P], EX[:, b, :], ident)
        pe = done("pe", ins)
        CT = ROUT[0:NE, 768:1024]
        a = A(CT, PS[0:NE, 6, 0:256], ACT.Copy, w=[pe])
        wait("pe", a)
        yield
        for e in range(NE):
            wait("pe", a)
            ins = mm(PS[:, 4 + (e // 2) % 2, (e % 2) * 256:(e % 2 + 1) * 256], SEL[:, e * P:(e + 1) * P], CT, True, True)
            if e % 2:
                pe = done("pe", ins)
                a2 = A(COMB[:, e - 1:e + 1, :], PS[:, 4 + (e // 2) % 2, :].rearrange("p (e t) -> p e t", e=2), ACT.Copy, w=[pe])
                a, a_prev = (a if e == 1 else a_prev), a2

    HB = tuple(rounded("he_" + n, aB + 7696 + m * 1024, 1024).rearrange("p (a n) -> p a n", a=2) for m, n in enumerate(("high", "low")))
    SGe, UC = (view(aB + 9744 + m * 1024, 1024).rearrange("p (a n) -> p a n", a=2) for m in range(2))
    all_wait()
    def expert(i, c0, more=True):
        before = {n: last(n) for n in q.eng}
        if q.loop:
            ready[:] = carried(c0)
        for n in range(6 if more else 4):
            plan.extend(weights(c0 + n))
        h_t = []
        for a_ in range(2):
            wait("pe", before["dve"])
            for u in range(2):
                for j in range(2):
                    pe = out_tile(PS[:, 2 * a_ + u, j * 256:(j + 1) * 256], XIN)
                if u == 0:
                    s_t = A(SGe[:, a_, :], PS[:, 2 * a_, :], ACT.Sigmoid, w=[pe, before["dve"]])
                    V(vv.tensor_tensor, SGe[:, a_, :], SGe[:, a_, :], PS[:, 2 * a_, :], ALU.mult, w=[s_t])
            comb = COMB[:, bass.ds(i + 1, 1) if q.loop else slice(i, i + 1), :].broadcast_to([P, 2, S])
            V(vv.tensor_tensor, UC[:, a_, :].rearrange("p (j t) -> p j t", j=2), PS[:, 2 * a_ + 1, :].rearrange("p (j t) -> p j t", j=2), comb, ALU.mult, w=[pe])
            v = V(vv.tensor_tensor, UC[:, a_, :], SGe[:, a_, :], UC[:, a_, :], ALU.mult, w=[before["act"]])
            h_t.append(split_act(HB[0][:, a_, :], HB[1][:, a_, :], UC[:, a_, :], w=[v, before["pe"]]))
        for a_ in range(2):
            wait("pe", h_t[a_])
            for j in range(2):
                s_ = take()
                second_product(both(HB, slice(None), a_, slice(j * 256, (j + 1) * 256)), s_)
        while plan:
            split_next()
        if q.loop:
            carry_holds(c0)

    for n in range(6):
        plan += weights(c_now + n)
    steps = router()
    next(steps)
    for a_ in range(2):
        for u in range(2):
            for j in range(2):
                pe = out_tile(PS[:, 2 * a_ + u, j * 256:(j + 1) * 256], XIN)
                next(steps, None)
            if u == 0:
                s_t = A(SGe[:, a_, :], PS[:, 2 * a_, :], ACT.Sigmoid, w=[pe])
                V(vv.tensor_tensor, SGe[:, a_, :], SGe[:, a_, :], PS[:, 2 * a_, :], ALU.mult, w=[s_t])
        V(vv.tensor_tensor, UC[:, a_, :], SGe[:, a_, :], PS[:, 2 * a_ + 1, :], ALU.mult, w=[pe])
    for _ in steps:
        pass
    comb_t = last("act")
    clear_sums()
    for a_ in range(2):
        both_j = UC[:, a_, :].rearrange("p (j t) -> p j t", j=2)
        v = V(vv.tensor_tensor, both_j, both_j, COMB[:, 0:1, :].broadcast_to([P, 2, S]), ALU.mult, w=[comb_t])
        wait("pe", split_act(HB[0][:, a_, :], HB[1][:, a_, :], UC[:, a_, :], w=[v]))
        for j in range(2):
            s_ = take()
            second_product(both(HB, slice(None), a_, slice(j * 256, (j + 1) * 256)), s_)
    c_now += 6
    while plan:
        split_next()
    q.run_loop(NE - 2, {"pe": 12, "dve": 8, "act": 16, "pool": 0}, lambda i: expert(i, c_now))
    c_now += 6 * (NE - 2)
    expert(NE - 1, c_now, more=False)
    c_now += 4
    assert c_now == N_CHUNKS, c_now
    xt = evacuate(MOD[:, 136:144])
    rms_rows(X[:, :, :], xt, XC[:, :, :])
    s_out = nc.alloc_semaphore("s_out")
    for k in range(KT):
        v = V(vv.tensor_scalar, X[:, k, :], XC[:, k, :], par_("fing", k), None, ALU.mult)
        if k % 4 == 3:
            nc.sync.wait_ge(v.sem, v.n)
            nc.sync.dma_start(outT[:, k - 3:k + 1, :], X[:, k - 3:k + 1, :]).then_inc(s_out, 16)
    nc.sync.wait_ge(s_out, 32)


def tables():
    f64, f32 = np.float64, np.float32
    t = np.arange(S)
    out = {}
    inv = f32(500000.0) ** (-np.arange(0, 32, 2, dtype=f32) / f32(32))
    ang = (t.astype(f32)[:, None] * inv[None, :]).astype(f32)
    z = np.zeros((P, S))
    out["ropec"] = z.copy()
    out["ropec"][0:16] = out["ropec"][16:32] = np.cos(ang.astype(f64)).T
    out["ropes"] = z.copy()
    out["ropes"][0:16] = out["ropes"][16:32] = np.sin(ang.astype(f64)).T
    r = np.zeros((P, 32))
    for m in range(16):
        r[m + 16, m] = -1.0
        r[m, m + 16] = 1.0
    out["roper"] = r
    qi = np.arange(S).reshape(2, P).T
    out["amask"] = np.where(np.abs(qi[:, :, None] - t[None, None, :]) <= WIN, 0.0, -1e30).reshape(P, 512)
    tt = np.linspace(0.0, 1.0, S, dtype=f32)
    w = (f32(2.0 * math.pi) * t.astype(f32) / f32(S)).astype(f32)
    bands = np.linspace(1e-4, 15, 16, dtype=f32)
    bw = (bands[None, :] * w[:, None]).astype(f32).astype(f64)
    zf = np.concatenate([tt[:, None], np.cos(bw), -np.sin(bw)], axis=1).T
    out["zf"] = np.zeros((P, S))
    out["zf"][0:33] = zf
    f = np.arange(S)
    th = np.pi * ((2 * f[None, :] + 1) * t[:, None] % 1024) / 512.0
    blk = lambda m: m.reshape(2, P, S).transpose(1, 0, 2).reshape(P, 512)
    out["dc"], out["ds"] = blk(np.cos(th)), blk(np.sin(th))
    out["ic"], out["is"] = blk(np.cos(th).T / 256.0), blk(np.sin(th).T / 256.0)
    fl = 2 * np.pi * (np.outer(t, t) % S) / S
    out["flc"], out["fls"] = blk(np.cos(fl) / 16.0), blk(np.sin(fl) / 16.0)
    c = np.arange(64)
    fc = 2 * np.pi * (np.outer(c, c) % 64) / 64
    e2 = np.eye(2)
    out["fcc"], out["fcs"] = np.kron(e2, np.cos(fc) / 8.0), -np.kron(e2, np.sin(fc) / 8.0)
    dl = np.linspace(math.log(1e-2) / 1.5, math.log(1e-2) / 0.3, 256, dtype=f32)
    dec = np.exp((-tt[:, None] * np.abs(dl)[None, :]).astype(f32).astype(f64))
    out["decf"] = blk(dec)
    decb = dec.copy()
    decb[0] = 0.0
    out["decb"] = blk(decb)
    s_, t_ = np.arange(P)[:, None], np.arange(P)[None, :]
    lm = [np.eye(P)]
    for lev in range(1, 8):
        lm.append((s_ >> lev == t_ >> lev) & (s_ >> (lev - 1) != t_ >> (lev - 1)))
    out["lmask"] = np.stack(lm, 1).reshape(P, 1024)
    out["iota"] = np.tile(np.arange(16.0), (P, 1))
    tab, tab2 = (np.concatenate([out[n] for n in c_], axis=1).astype(f32) for c_ in (TCOL, T2COL))
    quarter = D // 4
    om = (f32(1.0) / (f32(10000.0) ** (np.arange(quarter, dtype=f32) / f32(quarter)))).astype(f32)
    ar = ((t // 64).astype(f32)[:, None] * om).astype(f32).astype(f64)
    ac = ((t % 64).astype(f32)[:, None] * om).astype(f32).astype(f64)
    pos = np.concatenate([np.sin(ar), np.cos(ar), np.sin(ac), np.cos(ac)], axis=1).astype(f32)
    sel = np.zeros((NE, NE, P), f32)
    for e in range(NE):
        sel[e, e] = 1.0
    return tab, tab2, fm(pos), sel.reshape(NE, NE * P)


def fm(x):
    return np.ascontiguousarray(x.T.reshape(-1, P, x.shape[0]).transpose(1, 0, 2))


def cols(v, p=P):
    return v.reshape(-1, p).T


def kernel(**inputs):
    import concourse.bacc as bacc
    from concourse.bass_utils import run_bass_kernel_spmd as run

    I = {k: np.asarray(v) for k, v in inputs.items()}

    def out_tiles(w):
        n = w.shape[1] // P
        return w.reshape(KT, P, n // 2, 2, P).transpose(2, 1, 3, 0, 4).reshape(n // 2, P, CH)

    def in_tiles(w):
        return w.reshape(-1, 2, P, D).transpose(0, 2, 1, 3).reshape(-1, P, CH)

    def ada(w):
        return in_tiles(w.T)

    def pad(a, axis, n):
        shape = list(a.shape)
        shape[axis] = n - a.shape[axis]
        return np.concatenate([a, np.zeros(shape, a.dtype)], axis=axis)

    a = [[ada(I["ada_w"][i, m]) for m in range(2)] for i in range(2)]
    a2 = ada(I["ada_w_2"][0])
    wi = I["attn_w_in"][0]
    v_in = wi[:, 1280:1536].reshape(KT, P, 256).transpose(1, 0, 2).reshape(1, P, CH)
    attn_in = np.concatenate([out_tiles(wi[:, 0:1280]), v_in])

    def mlp(w1, w2, ad, after):
        w1, w2 = np.concatenate([out_tiles(w1), after[0:2]]), in_tiles(w2)
        turns = np.stack([w2[0::2], ad[0::2], w2[1::2], ad[1::2], w1[2::2], w1[3::2]], 1).reshape(-1, P, CH)
        return np.concatenate([w1[0:2], turns])

    def between(main, ad):
        n = len(ad)
        return np.concatenate([np.stack([main[0:n], ad], 1).reshape(-1, P, CH), main[n:]])

    rw = I["rnn_w_in"][0].reshape(KT, P, 2, NB, BW).transpose(3, 1, 2, 0, 4).reshape(NB, P, 2, KT * BW)
    wa, wx = I["rnn_w_a"][0], I["rnn_w_x"][0]
    gw = np.stack([wa[0], wx[0], wa[1], wx[1]], 1).transpose(0, 2, 1, 3).reshape(NB, BW, 4 * BW)
    gw = gw.transpose(1, 0, 2)
    rnn = pad(rw, 3, HALF).reshape(NB, P, CH)
    rnn_out = pad(I["rnn_w_out"][0].reshape(8, 2, BW, D).transpose(0, 2, 1, 3).reshape(8, BW, CH), 1, P)
    w2i = I["w_in_2"][0]
    hy, hq, hff, hfb, hi, hg, fn = np.split(w2i, [768, 1280, 1792, 2304, 2816, 3328], axis=1)
    hi = hi.reshape(2, 4, P, 512).transpose(0, 2, 1, 3).reshape(2, P, CH)
    w_in2 = np.concatenate([out_tiles(hff), out_tiles(hfb), hi, out_tiles(hq), out_tiles(hy), out_tiles(hg), out_tiles(fn)])
    moe = []
    for e in range(NE):
        g_, u_ = out_tiles(I["moe_w_gate_2"][0, e]), out_tiles(I["moe_w_up_2"][0, e])
        d_ = in_tiles(I["moe_w_down_2"][0, e])
        moe += [g_[0:1], u_[0:1], g_[1:2], u_[1:2], d_]
    stream = np.concatenate([
        a[0][0][0:8], attn_in, a[0][0][8:12], a[0][1][0:8], out_tiles(I["attn_w_out"][0]),
        mlp(I["mlp_w1"][0], I["mlp_w2"][0], np.concatenate([a[0][1][8:12], a[1][0]]), rnn),
        between(rnn[2:], a[1][1]), rnn_out,
        mlp(I["mlp_w1"][1], I["mlp_w2"][1], a2[0:16], w_in2),
        between(w_in2[2:], a2[16:24]), out_tiles(I["w_out_2"][0])] + moe)
    assert stream.shape[0] == N_CHUNKS, stream.shape

    rep = lambda v: np.broadcast_to(v.reshape(1, -1), (P, v.size))
    fnw = np.zeros((2, 2, 64, 2, 64), np.float32)
    fw = I["fn_w_2"][0].reshape(2, 2, 64, 64)
    for j in range(2):
        fnw[:, j, :, j, :] = fw[:, j]
    eps = np.ones((P, 1), np.float32)
    par = {"ada_b": cols(I["ada_b"]), "ada_b2": cols(I["ada_b_2"]), "ln_g": cols(I["ln_g"]), "ln_b": cols(I["ln_b"]),
           "n1g": cols(I["norm1_g_2"]), "n2g": cols(I["norm2_g_2"]), "fing": cols(I["final_norm_g_2"]),
           "hycw": cols(I["hy_conv_w_2"]), "hycb": cols(I["hy_conv_b_2"]), "hybias": cols(I["hy_bias_2"]),
           "hyg": cols(I["hy_norm_g_2"]), "lb": cols(I["hg_lower_bounds_2"]), "hgg": cols(I["hg_norm_g_2"]),
           "fnb": cols(I["fn_b_2"]), "fng": cols(I["fn_norm_g_2"]), "sinks": rep(I["attn_sinks"]), "rb": rep(I["router_b_2"]),
           "rw": I["router_w_2"].reshape(KT, P, NE).transpose(1, 0, 2).reshape(P, KT * NE),
           "fnw": fnw.reshape(2, P, P).transpose(1, 0, 2).reshape(P, 2 * P), "eps5": eps * np.float32(LN_EPS), "eps6": eps * np.float32(RMS_EPS)}
    par = np.concatenate([par[n] for n in PCOL], axis=1)
    rpar = np.concatenate([cols(I[n], BW) for n in ("rnn_conv_w", "rnn_conv_b", "rnn_b_a", "rnn_b_x", "rnn_lam")], axis=1)
    fpar = np.concatenate([pad(I["hy_filt_w1_2"][0], 0, 64), I["hy_filt_w2_2"][0], I["hy_filt_w3_2"][0]]
                          + [I[n][0].reshape(64, 1) for n in ("hy_filt_b1_2", "hy_filt_b2_2", "hy_filt_freq_2")], axis=1)
    tab, tab2, pos, sel = tables()
    stream = stream.reshape(N_CHUNKS, P, 2, HALF).transpose(0, 2, 1, 3).reshape(2 * N_CHUNKS, P, HALF)
    data = {"stream": stream, "xT": fm(I["x"][0]), "ctxT": fm(I["ctx_2"][0]), "posT": pos,
            "cvec": np.concatenate([I["c"], I["c_2"], I["c_ctx_2"].reshape(1, D)]), "par": par, "rpar": rpar,
            "fpar": fpar, "ident": np.eye(P, dtype=np.float32), "tab": tab, "tab2": tab2, "sel": sel, "gw": gw.reshape(BW, NB * 4 * BW)}
    data = {k: np.ascontiguousarray(v) for k, v in data.items()}
    nc = bacc.Bacc("TRN2", target_bir_lowering=False, num_devices=1)
    aps = [nc.dram_tensor(n, v.shape, F32, kind="ExternalInput").ap() for n, v in data.items()]
    out = nc.dram_tensor("outT", (P, KT, S), F32, kind="ExternalOutput").ap()
    build(nc, *aps, out)
    r = run(nc, [data], core_ids=[0]).results[0]["outT"]
    return np.ascontiguousarray(r.transpose(1, 0, 2).reshape(D, S).T).reshape(1, S, D)
```
